# Optimizing a Trainium2 kernel written in Bass

```python
import jax, jax.numpy as jnp
from jax import lax
import numpy as np

D_MODEL = 1024
BATCH = 1
SEQ = 256
DEPTH = 1

HEAD_DIM = 64
MOBA_HEADS = 4
MOBA_BLOCK = 256
MOBA_TOPK = 3
MOBA_Q_CHUNK = 32
FOX_HEADS = 4
ATTN_Q_BLOCK = 128
CONV_CH = 256
CONV_K = 31
MLA_HEADS = 4
MLA_Q_LORA = 256
MLA_KV_LORA = 128
MLA_NOPE = 64
MLA_ROPE = 32
MLA_V = 64
ROPE_THETA = 10000.0
BRANCH_W = 256
N_BRANCH = 4
N_GROUPS = 4
EXPERTS_PER_GROUP = 8
N_EXPERTS = N_GROUPS * EXPERTS_PER_GROUP
TOPK_IN_GROUP = 2
EXPERT_FF = 256
MOE_ROW_BLOCK = 128
NORM_EPS = 1e-6
NEG_INF = -1e30

MOBA_W = MOBA_HEADS * HEAD_DIM
FOX_W = FOX_HEADS * HEAD_DIM
IN_COLS = 3 * MOBA_W + 3 * FOX_W + FOX_HEADS + 2 * CONV_CH + MLA_Q_LORA + MLA_KV_LORA + MLA_ROPE

kernel_name = "hybrid_moba_fox_conv_mla_hmoe"

def rmsnorm(x, g):
    xf = x.astype(jnp.float32)
    y = xf * lax.rsqrt(jnp.mean(xf * xf, axis=-1, keepdims=True) + NORM_EPS)
    return (y * g.astype(jnp.float32)).astype(x.dtype)

def layernorm(x, g, b):
    xf = x.astype(jnp.float32)
    mu = jnp.mean(xf, axis=-1, keepdims=True)
    var = jnp.mean(jnp.square(xf - mu), axis=-1, keepdims=True)
    y = (xf - mu) * lax.rsqrt(var + NORM_EPS)
    return (y * g.astype(jnp.float32) + b.astype(jnp.float32)).astype(x.dtype)

def split_heads(t, n):
    b, s, _ = t.shape
    return t.reshape(b, s, n, -1).transpose(0, 2, 1, 3)

def merge_heads(t):
    b, h, s, d = t.shape
    return t.transpose(0, 2, 1, 3).reshape(b, s, h * d)

def rope(x, cos, sin):
    x1, x2 = jnp.split(x, 2, axis=-1)
    y = jnp.concatenate([x1 * cos - x2 * sin, x2 * cos + x1 * sin], axis=-1)
    return y.astype(x.dtype)

def moba_attention(q, k, v, slopes):
    b, h, s, dh = q.shape
    nb = -(-s // MOBA_BLOCK)
    sp = nb * MOBA_BLOCK
    n_sel = min(MOBA_TOPK, nb - 1)
    pad = ((0, 0), (0, 0), (0, sp - s), (0, 0))
    q, k, v = jnp.pad(q, pad), jnp.pad(k, pad), jnp.pad(v, pad)
    kb = k.reshape(b, h, nb, MOBA_BLOCK, dh)
    vb = v.reshape(b, h, nb, MOBA_BLOCK, dh)
    kmean = jnp.mean(kb.astype(jnp.float32), axis=3)
    scale = dh ** -0.5
    nc = sp // MOBA_Q_CHUNK
    qc = jnp.moveaxis(q.reshape(b, h, nc, MOBA_Q_CHUNK, dh), 2, 0)
    bi = jnp.arange(b)[:, None, None, None]
    hi = jnp.arange(h)[None, :, None, None]
    m = slopes[None, :, None, None]
    blk_ids = jnp.arange(nb)
    in_blk = jnp.arange(MOBA_BLOCK)

    def chunk(args):
        qi, ci = args
        t = ci * MOBA_Q_CHUNK + jnp.arange(MOBA_Q_CHUNK)
        cur = (ci * MOBA_Q_CHUNK) // MOBA_BLOCK
        k_own = lax.dynamic_slice_in_dim(k, cur * MOBA_BLOCK, MOBA_BLOCK, axis=2)
        v_own = lax.dynamic_slice_in_dim(v, cur * MOBA_BLOCK, MOBA_BLOCK, axis=2)
        dist_own = t[:, None] - (cur * MOBA_BLOCK + in_blk)[None, :]
        s_own = jnp.einsum("bhcd,bhjd->bhcj", qi, k_own).astype(jnp.float32) * scale
        s_own = jnp.where(dist_own >= 0, s_own - m * dist_own, NEG_INF)
        if n_sel == 0:
            p = jax.nn.softmax(s_own, axis=-1).astype(v.dtype)
            return jnp.einsum("bhcj,bhjd->bhcd", p, v_own)
        gate = jnp.einsum("bhcd,bhnd->bhcn", qi.astype(jnp.float32), kmean)
        gate = jnp.where(blk_ids < cur, gate, NEG_INF)
        _, sel = lax.top_k(gate, n_sel)
        valid = sel < cur
        kg = kb[bi, hi, sel]
        vg = vb[bi, hi, sel]
        dist_sel = t[:, None, None] - (sel[..., None] * MOBA_BLOCK + in_blk)
        s_sel = jnp.einsum("bhcd,bhckjd->bhckj", qi, kg).astype(jnp.float32) * scale - m[..., None] * dist_sel
        s_sel = jnp.where(valid[..., None], s_sel, NEG_INF)
        c = qi.shape[2]
        logits = jnp.concatenate([s_sel.reshape(b, h, c, n_sel * MOBA_BLOCK), s_own], axis=-1)
        p = jax.nn.softmax(logits, axis=-1).astype(v.dtype)
        p_sel = p[..., : n_sel * MOBA_BLOCK].reshape(b, h, c, n_sel, MOBA_BLOCK)
        p_own = p[..., n_sel * MOBA_BLOCK:]
        return jnp.einsum("bhckj,bhckjd->bhcd", p_sel, vg) + jnp.einsum("bhcj,bhjd->bhcd", p_own, v_own)

    out = lax.map(chunk, (qc, jnp.arange(nc)))
    out = jnp.moveaxis(out, 0, 2).reshape(b, h, sp, dh)
    return out[:, :, :s]

def causal_sweep(q, k, v, scale, cum_log_f=None):
    s = q.shape[2]
    outs = []
    for i in range(s // ATTN_Q_BLOCK):
        lo, hi = i * ATTN_Q_BLOCK, (i + 1) * ATTN_Q_BLOCK
        sc = jnp.einsum("bhqd,bhkd->bhqk", q[:, :, lo:hi], k[:, :, :hi]).astype(jnp.float32) * scale
        if cum_log_f is not None:
            sc = sc + cum_log_f[:, :, lo:hi, None] - cum_log_f[:, :, None, :hi]
        mask = jnp.arange(hi)[None, :] <= (lo + jnp.arange(ATTN_Q_BLOCK))[:, None]
        p = jax.nn.softmax(jnp.where(mask, sc, NEG_INF), axis=-1).astype(v.dtype)
        outs.append(jnp.einsum("bhqk,bhkd->bhqd", p, v[:, :, :hi]))
    return jnp.concatenate(outs, axis=2)

def token_mixer(xn, w_in, b_forget, conv_w, conv_b, conv_ln_g, conv_ln_b, mla_gq, mla_wuq, mla_gkv, mla_wukv,
                w_gate, b_gate, w_branch, w_out, slopes, cos, sin):
    b, s, _ = xn.shape
    splits = np.cumsum([3 * MOBA_W, 3 * FOX_W, FOX_HEADS, 2 * CONV_CH, MLA_Q_LORA, MLA_KV_LORA]).tolist()
    proj = xn @ w_in
    moba_qkv, fox_qkv, fox_f, conv_in, c_q, c_kv, k_rope = jnp.split(proj, splits, axis=-1)

    qa, ka, va = (split_heads(t, MOBA_HEADS) for t in jnp.split(moba_qkv, 3, axis=-1))
    y_a = merge_heads(moba_attention(qa, ka, va, slopes))

    qb, kb, vb = (split_heads(t, FOX_HEADS) for t in jnp.split(fox_qkv, 3, axis=-1))
    log_f = jax.nn.log_sigmoid((fox_f + b_forget).astype(jnp.float32))
    cum = jnp.cumsum(log_f, axis=1).transpose(0, 2, 1)
    y_b = merge_heads(causal_sweep(qb, kb, vb, HEAD_DIM ** -0.5, cum))

    u = conv_in[..., :CONV_CH] * jax.nn.sigmoid(conv_in[..., CONV_CH:])
    u = lax.conv_general_dilated(u, conv_w[:, None, :], window_strides=(1,), padding=[(CONV_K - 1, 0)],
                                 dimension_numbers=("NWC", "WIO", "NWC"), feature_group_count=CONV_CH) + conv_b
    y_c = jax.nn.silu(layernorm(u, conv_ln_g, conv_ln_b))

    cq = rmsnorm(c_q, mla_gq)
    qd = (cq @ mla_wuq).reshape(b, s, MLA_HEADS, MLA_NOPE + MLA_ROPE)
    q_nope, q_pe = qd[..., :MLA_NOPE], rope(qd[..., MLA_NOPE:], cos[:, None, :], sin[:, None, :])
    ckv = rmsnorm(c_kv, mla_gkv)
    kvd = (ckv @ mla_wukv).reshape(b, s, MLA_HEADS, MLA_NOPE + MLA_V)
    k_nope, vd = kvd[..., :MLA_NOPE], kvd[..., MLA_NOPE:]
    k_pe = jnp.broadcast_to(rope(k_rope, cos, sin)[:, :, None, :], (b, s, MLA_HEADS, MLA_ROPE))
    qh = jnp.concatenate([q_nope, q_pe], axis=-1).transpose(0, 2, 1, 3)
    kh = jnp.concatenate([k_nope, k_pe], axis=-1).transpose(0, 2, 1, 3)
    vh = vd.transpose(0, 2, 1, 3)
    y_d = merge_heads(causal_sweep(qh, kh, vh, (MLA_NOPE + MLA_ROPE) ** -0.5))

    merged = jnp.zeros_like(xn)
    for i, y in enumerate((y_a, y_b, y_c, y_d)):
        gate = jax.nn.sigmoid(xn @ w_gate[i] + b_gate[i])
        merged = merged + gate * (y @ w_branch[i])
    return merged @ w_out

def grouped_expert_ffn(xt, eid, wt, w1, w3, w2):
    t, d = xt.shape
    a = eid.shape[0]
    tok = jnp.arange(a) // TOPK_IN_GROUP
    order = jnp.argsort(eid)
    se, st, sw = eid[order], tok[order], wt[order]
    counts = jnp.bincount(eid, length=N_EXPERTS)
    starts = jnp.cumsum(counts) - counts
    pcounts = ((counts + MOE_ROW_BLOCK - 1) // MOE_ROW_BLOCK) * MOE_ROW_BLOCK
    pends = jnp.cumsum(pcounts)
    pstarts = pends - pcounts
    dest = pstarts[se] + jnp.arange(a) - starts[se]
    p_rows = a + N_EXPERTS * MOE_ROW_BLOCK
    n_blk = p_rows // MOE_ROW_BLOCK
    rows = jnp.zeros((p_rows, d), xt.dtype).at[dest].set(xt[st])
    blk_e = jnp.minimum(jnp.searchsorted(pends, jnp.arange(n_blk) * MOE_ROW_BLOCK, side="right"), N_EXPERTS - 1)

    def ffn(args):
        xb, e = args
        return (jax.nn.silu(xb @ w1[e]) * (xb @ w3[e])) @ w2[e]

    out = lax.map(ffn, (rows.reshape(n_blk, MOE_ROW_BLOCK, d), blk_e)).reshape(p_rows, d)
    y = out[dest] * sw[:, None].astype(out.dtype)
    return jax.ops.segment_sum(y, st, num_segments=t)

def hierarchical_moe(h, w_rg, b_rg, w_re, b_re, w1, w3, w2):
    b, s, d = h.shape
    xt = h.reshape(b * s, d)
    g_logits = (xt @ w_rg + b_rg).astype(jnp.float32)
    p_group = jax.nn.softmax(g_logits, axis=-1)
    _, g_sel = lax.top_k(g_logits, 1)
    e_logits = (xt @ w_re + b_re).astype(jnp.float32).reshape(-1, N_GROUPS, EXPERTS_PER_GROUP)
    e_in = jnp.take_along_axis(e_logits, g_sel[:, :, None], axis=1)[:, 0]
    top_l, top_i = lax.top_k(e_in, TOPK_IN_GROUP)
    wts = jax.nn.softmax(top_l, axis=-1) * jnp.take_along_axis(p_group, g_sel, axis=1)
    eid = g_sel * EXPERTS_PER_GROUP + top_i
    y = grouped_expert_ffn(xt, eid.reshape(-1), wts.reshape(-1), w1, w3, w2)
    return y.reshape(b, s, d)

def setup_inputs(seed: int = 0) -> dict:
    key = jax.random.key(seed)
    ks = jax.random.split(key, 26)
    f32 = jnp.float32
    nrm = lambda k, shape, sc: jax.random.normal(k, shape, f32) * sc
    L = DEPTH
    return {
        "x": nrm(ks[0], (BATCH, SEQ, D_MODEL), 1.0),
        "norm1_g": 1.0 + nrm(ks[1], (L, D_MODEL), 0.02),
        "w_in": nrm(ks[2], (L, D_MODEL, IN_COLS), D_MODEL ** -0.5),
        "b_forget": 4.0 + nrm(ks[3], (L, FOX_HEADS), 0.5),
        "conv_w": nrm(ks[4], (L, CONV_K, CONV_CH), CONV_K ** -0.5),
        "conv_b": nrm(ks[5], (L, CONV_CH), 0.02),
        "conv_ln_g": 1.0 + nrm(ks[6], (L, CONV_CH), 0.02),
        "conv_ln_b": nrm(ks[7], (L, CONV_CH), 0.02),
        "mla_gq": 1.0 + nrm(ks[8], (L, MLA_Q_LORA), 0.02),
        "mla_wuq": nrm(ks[9], (L, MLA_Q_LORA, MLA_HEADS * (MLA_NOPE + MLA_ROPE)), MLA_Q_LORA ** -0.5),
        "mla_gkv": 1.0 + nrm(ks[10], (L, MLA_KV_LORA), 0.02),
        "mla_wukv": nrm(ks[11], (L, MLA_KV_LORA, MLA_HEADS * (MLA_NOPE + MLA_V)), MLA_KV_LORA ** -0.5),
        "w_gate": nrm(ks[12], (L, N_BRANCH, D_MODEL, D_MODEL), D_MODEL ** -0.5),
        "b_gate": nrm(ks[13], (L, N_BRANCH, D_MODEL), 0.02),
        "w_branch": nrm(ks[14], (L, N_BRANCH, BRANCH_W, D_MODEL), BRANCH_W ** -0.5),
        "w_out": nrm(ks[15], (L, D_MODEL, D_MODEL), D_MODEL ** -0.5),
        "norm2_g": 1.0 + nrm(ks[16], (L, D_MODEL), 0.02),
        "w_router_group": nrm(ks[17], (L, D_MODEL, N_GROUPS), D_MODEL ** -0.5),
        "b_router_group": nrm(ks[18], (L, N_GROUPS), 0.01),
        "w_router_expert": nrm(ks[19], (L, D_MODEL, N_EXPERTS), D_MODEL ** -0.5),
        "b_router_expert": nrm(ks[20], (L, N_EXPERTS), 0.01),
        "w_exp_gate": nrm(ks[21], (L, N_EXPERTS, D_MODEL, EXPERT_FF), D_MODEL ** -0.5),
        "w_exp_up": nrm(ks[22], (L, N_EXPERTS, D_MODEL, EXPERT_FF), D_MODEL ** -0.5),
        "w_exp_down": nrm(ks[23], (L, N_EXPERTS, EXPERT_FF, D_MODEL), EXPERT_FF ** -0.5),
        "final_g": 1.0 + nrm(ks[24], (D_MODEL,), 0.02),
    }

def reference(x, norm1_g, w_in, b_forget, conv_w, conv_b, conv_ln_g, conv_ln_b, mla_gq, mla_wuq, mla_gkv,
              mla_wukv, w_gate, b_gate, w_branch, w_out, norm2_g, w_router_group, b_router_group,
              w_router_expert, b_router_expert, w_exp_gate, w_exp_up, w_exp_down, final_g):
    s = x.shape[1]
    slopes = jnp.exp2(-8.0 * (jnp.arange(MOBA_HEADS, dtype=jnp.float32) + 1.0) / MOBA_HEADS)
    inv_freq = ROPE_THETA ** (-jnp.arange(0, MLA_ROPE, 2, dtype=jnp.float32) / MLA_ROPE)
    ang = jnp.arange(s, dtype=jnp.float32)[:, None] * inv_freq[None, :]
    cos, sin = jnp.cos(ang), jnp.sin(ang)
    h = x
    for l in range(DEPTH):
        xn = rmsnorm(h, norm1_g[l])
        h = h + token_mixer(xn, w_in[l], b_forget[l], conv_w[l], conv_b[l], conv_ln_g[l], conv_ln_b[l],
                            mla_gq[l], mla_wuq[l], mla_gkv[l], mla_wukv[l], w_gate[l], b_gate[l],
                            w_branch[l], w_out[l], slopes, cos, sin)
        hn = rmsnorm(h, norm2_g[l])
        h = h + hierarchical_moe(hn, w_router_group[l], b_router_group[l], w_router_expert[l],
                                 b_router_expert[l], w_exp_gate[l], w_exp_up[l], w_exp_down[l])
    return rmsnorm(h, final_g)


_drawn_inputs = setup_inputs


def setup_inputs(seed=0):
    import zlib

    import numpy as np

    out = dict(_drawn_inputs(seed))
    spreads = {}
    factors = {'conv_ln_b': 15.98,
     'mla_gq': 3.167,
     'mla_gkv': 4.641,
     'b_gate': 3.142,
     'b_router_group': 14.304,
     'b_router_expert': 27.202,
     'final_g': 23.252,
     'b_forget': 24.696,
     'conv_b': 5.073,
     'conv_ln_g': 8.0,
     'norm2_g': 4.47}
    for name, (base, spread) in spreads.items():
        noise = np.random.default_rng([zlib.crc32(name.encode()), seed]).standard_normal(out[name].shape)
        drawn = base * np.exp(spread * noise) if base else spread * noise
        out[name] = __import__('jax').numpy.asarray(drawn.astype(out[name].dtype))
    for name, factor in factors.items():
        out[name] = (out[name] * factor).astype(out[name].dtype)
    return out
```

```python
from contextlib import ExitStack

import numpy as np

import concourse.bass as bass
from concourse import mybir

F32 = mybir.dt.float32
F32R = mybir.dt.float32r
I32 = mybir.dt.int32
ALU = mybir.AluOpType
ACT = mybir.ActivationFunctionType
AXX = mybir.AxisListType.X

P = 128
D = 1024
T = 256
TT = T // P
KD = D // P
HD = 64
HEADS = 4
NE = 32
EG = 8
NG = 4
FF = 256
CONV_K = 31
EPS = 1e-6
NEG = -1e30
CAP = 64
QUAD = 4
NQ = NE // QUAD
ROUNDS = T // CAP - 1
MAXOVER = 2 * T // (CAP + 1)
SLOT = 2 * D
RAWW = 10 * 256
NRAW = 3
SPLITW = 8 * 260

W_IN_UNITS = [("conv_a", 1540, 1796), ("conv_g", 1796, 2052), ("cq", 2052, 2308), ("ckv", 2308, 2468),
              ("fox_v", 1280, 1540), ("fox_q", 768, 1024), ("fox_k", 1024, 1280),
              ("moba_q", 0, 256), ("moba_k", 256, 512), ("moba_v", 512, 768)]
BRANCHES = [2, 3, 1, 0]
NIN = len(W_IN_UNITS)
NGATE = 4 * len(BRANCHES)
NOUT = 4
UNITS = NIN + NGATE + NOUT
PREFETCH_AT = NIN + 2

ROWS = {}
_r = 0
for _n, _c in (("conv_w", 2 * CONV_K), ("conv_b", 2), ("ln_g", 2), ("ln_b", 2), ("gq", 2), ("gkv", 1), ("b_gate", 32)):
    ROWS[_n] = _r
    _r += _c
NROWS = _r

TAB = {}
_r = 0
for _n, _c in (("ident", P), ("dist", 384), ("mask", 384), ("tri", 256), ("cos", T), ("sin", T), ("kcs", T),
               ("rep", P), ("iota", CAP), ("code", 2 * ROUNDS * NQ)):
    TAB[_n] = (_r, _r + _c)
    _r += _c
NTAB = _r


def shape_tables():
    t = np.zeros((P, NTAB), np.float32)

    def put(name, a):
        t[:, TAB[name][0]:TAB[name][1]] = a

    p = np.arange(P)[:, None]
    put("ident", np.eye(P))
    q = np.concatenate([np.broadcast_to(p, (P, P)), np.broadcast_to(p + P, (P, T))], 1)
    s = np.concatenate([np.arange(P), np.arange(T)])[None, :]
    put("dist", np.where(q >= s, -(q - s), NEG))
    put("mask", np.where(q >= s, 0.0, NEG))
    put("tri", np.arange(T)[None, :] >= p)
    inv = (np.float32(10000.0) ** (-np.arange(0, 32, 2, dtype=np.float32) / np.float32(32))).astype(np.float32)
    ang = (np.arange(T, dtype=np.float32)[:, None] * inv[None, :]).astype(np.float32)
    cos, sin = np.cos(ang).T, np.sin(ang).T
    cos32, sin32 = np.concatenate([cos, cos]), np.concatenate([-sin, sin])
    put("cos", np.tile(cos32, (4, 1)))
    put("sin", np.tile(sin32, (4, 1)))
    put("kcs", np.concatenate([cos32, sin32, cos32, sin32]))
    put("rep", (p % 32) == (np.arange(P) % 32)[None, :])
    put("iota", np.arange(CAP))
    r, qd = np.divmod(np.arange(ROUNDS * NQ), NQ)
    put("code", np.concatenate([(r + 1) * NE + qd * QUAD, qd]))
    return t


def after(engine, semaphore, value):
    if not isinstance(value, int) or value > 0:
        engine.wait_ge(semaphore, value)


def trunk_kernel(nc, A, out):
    ctx = ExitStack()
    with ctx:
        def sb(name, shape, dt=F32):
            return ctx.enter_context(nc.sbuf_tensor(name, shape, dt))

        names = """x_in params_in tables_in norm_in wmla_in bias_in router_in final_in
            sumsq xvar xroot xscaled params_ps params_sb half_params xt_ps x_hi x_split
            w_hi w_lo unit_done proj_evac
            conv_t conv_u conv_acc conv_out ln_sum ln_cent ln_sq ln_var ln_ve ln_root ln_rec ln_z ln_t yc_ready
            cq_sb cq_sq cq_sum cq_ve cq_root cq_rec cq_ready
            ckv_sb ckv_sq ckv_sum ckv_ve ckv_root ckv_rec ckv_ready krope_sb kpe_ps kpe_ready
            wrot_ready zeros_ready mla_ps mla_evac rope_mul
            fox_f fox_exp fox_ln fox_ready fox_ps cum_ready
            score_ps logit_ready row_max neg_max prob_exp row_sum prob_ready pt_ps pt_sb pv_ps attn_ready
            gate_ps gate_t merged tmp_mul merge_hi merge_split
            h_ready h_sq h_var h_root h_scaled hs_hi hs_split hst_ps hst_sb logits_ps router_exp
            rank_ps sel_ready gather_ps xe_ready over_ready over_ps
            wselt_ps selt_sb hid_ps hid_t hid_ready hidt_ps hidt_sb y_ps y_hi y_split o_ps o_added
            final_sq final_var final_root out_ready stored router_chain sel_chain step_chain x_chain over_chain
            over_w over_sel""".split()
        s = type("Semaphores", (), {n: ctx.enter_context(nc.semaphore(n)) for n in names})
        raw_in = [ctx.enter_context(nc.semaphore(f"raw_in{i}")) for i in range(NRAW)]
        exp_in = [ctx.enter_context(nc.semaphore(f"exp_in{i}")) for i in range(12)]

        EX = sb("expert_slots", [P, 12 * SLOT])
        mixer_area = 6 * SLOT

        def ex(slot):
            return EX[:, slot * SLOT:(slot + 1) * SLOT]

        def area(at, n):
            return EX[:, mixer_area + at:mixer_area + at + n]

        RAW = [area(i * RAWW, RAWW) for i in range(NRAW)]
        kb_at = NRAW * RAWW
        KB = {b: area(kb_at + i * 1024, 1024).rearrange("p (h t) -> p h t", h=HEADS) for i, b in enumerate((3, 1, 0))}
        KPE = area(kb_at + 3072, 1024).rearrange("p (h t) -> p h t", h=HEADS)
        VMLA = area(kb_at + 4096, 512).rearrange("p (t c) -> p t c", t=TT)
        HS = EX[:, 10 * SLOT:11 * SLOT].rearrange("p (t d) -> p t d", t=TT)

        XH = sb("act_hi", [P, KD * T], F32R)
        XL = sb("act_lo", [P, KD * T], F32R)
        WH = sb("w_high", [P, 2, SPLITW], F32R)
        WL = sb("w_low", [P, 2, SPLITW], F32R)
        H = sb("residual", [P, TT, D])
        M = sb("merged_t", [P, KD * T])
        SEL = sb("select", [P, TT, QUAD, CAP], F32R)
        SELT = sb("select_t", [P, 2, T], F32R)
        TABS = sb("shape_tables", [P, NTAB])
        VEC = sb("vectors", [P, 272])
        SCR_N = 8900 - 384
        SCR = sb("scratch", [P, SCR_N])

        def tab(name):
            return TABS[:, TAB[name][0]:TAB[name][1]]

        ident = tab("ident")
        ones_mat = TABS[:, TAB["tri"][0] + P:TAB["tri"][0] + 2 * P]
        tri = tab("tri")

        def carver(area_ap, size):
            used = [0]

            def carve(n, start=None):
                if start is not None:
                    used[0] = start
                a = area_ap[:, used[0]:used[0] + n]
                used[0] += n
                assert used[0] <= size, used[0]
                return a
            return carve

        mx = carver(SCR[:, :], SCR_N)
        Q = {b: mx(512).rearrange("p (j t) -> p j t", j=2) for b in (3, 1, 0)}
        QPE = mx(T)
        VF = mx(2 * 260).rearrange("p (t c) -> p t c", t=TT)
        UPADV = mx(2 * 286)
        UPAD = UPADV.rearrange("p (j t) -> p j t", j=2)
        CACC = mx(512).rearrange("p (j t) -> p j t", j=2)
        YT = {b: mx(512).rearrange("p (j t) -> p j t", j=2) for b in (1, 3)}
        YT[2] = CACC
        YT[0] = UPADV[:, 0:512].rearrange("p (j t) -> p j t", j=2)
        CQV = mx(512)
        CQ = CQV.rearrange("p (j t) -> p j t", j=2)
        VM = CQV.rearrange("p (t c) -> p t c", t=TT)
        PTS = mx(384)
        TMPA = mx(512)
        TMPB = mx(512)
        CBW = mx(1024)
        WUKV = CBW[:, 0:512]
        WROT = CBW[:, 512:768].rearrange("p (j h c) -> p j h c", j=2, h=HEADS)
        CKV = CBW[:, 768:1024]
        CB = CBW[0:HEADS, :].rearrange("p (h t) -> p h t", h=HEADS)
        ROWP = PTS[:, 0:P]
        PRB = mx(768)
        PR = PRB.rearrange("p (h c) -> p h c", h=2)
        WUQ = PRB.rearrange("p (j n) -> p j n", j=2)
        VMAP = {3: VMLA, 1: VF, 0: VM}

        mo = carver(SCR[:, :], SCR_N)
        WSEL = mo(512).rearrange("p (t e c) -> p t e c", t=TT, e=QUAD)
        HT_ = mo(512).rearrange("p (a f) -> p a f", a=2)
        TH = mo(512).rearrange("p (a f) -> p a f", a=2)
        HTT = mo(512).rearrange("p (a j c) -> p a j c", a=2, j=2)
        FG = mo(D)
        WR = mo(KD * 36).rearrange("p (k n) -> p k n", k=KD)
        LG = mo(72).rearrange("p (t n) -> p t n", t=TT)
        RB = mo(800)
        RANK = mo(TT * (ROUNDS + 1) * NE).rearrange("p (t r) -> p t r", t=TT)
        WT = mo(TT * NE).rearrange("p (t e) -> p t e", t=TT)
        OV = mo(700)
        YOUT = mo(2 * D).rearrange("p (t d) -> p t d", t=TT)

        vv = carver(VEC[:, :], 272)
        PAR = vv(NROWS)
        HPAR = vv(4)
        G1 = vv(KD)
        G2 = vv(KD)
        BF = vv(HEADS)
        BR = vv(36)
        SS = vv(2)
        RS = vv(2)
        FW = vv(4 * 8)
        FLOG = vv(8).rearrange("p (t h) -> p t h", t=TT)
        CTOK = vv(8).rearrange("p (t h) -> p t h", t=TT)
        MAXV = vv(4)
        NMAX = vv(4)
        SUMV = vv(4)
        RECV = vv(4)
        WS = vv(2)
        ZB = vv(1)
        HGB = vv(32)
        LIST = sb("overflow_list", [1, 24], I32)

        def par(name, i=0):
            c = ROWS[name] + i
            return PAR[:, c:c + 1]

        bank = [ctx.enter_context(nc.psum_tensor(f"bank{i}", [P, 512], F32)) for i in range(8)]
        PA, PB, BRB, S0, S1, PT, PV, MISC = bank

        x_v = A["x"][0].rearrange("(t p) d -> p t d", p=P)
        out_v = out[0].rearrange("(t p) d -> p t d", p=P)
        w_in_v = A["w_in"][0].rearrange("(p k) n -> p k n", k=KD)
        w_out_v = A["w_out"][0].rearrange("(m p) n -> p m n", p=P)
        e_gate = A["w_exp_gate"][0].rearrange("e (p k) f -> e p (k f)", k=KD)
        e_up = A["w_exp_up"][0].rearrange("e (p k) f -> e p (k f)", k=KD)
        e_down = A["w_exp_down"][0].rearrange("e (p j) d -> e p (j d)", j=2)

        def unit_dmas(n):
            raw = RAW[n % NRAW]
            if n < NIN:
                _, a, b = W_IN_UNITS[n]
                return [(raw[:, 0:8 * (b - a)].rearrange("p (k n) -> p k n", k=8), w_in_v[:, :, a:b])]
            if n < NIN + NGATE:
                g = n - NIN
                i, u = BRANCHES[g // 4], g % 4
                cols = slice(u * 256, u * 256 + 256)
                return [(raw[:, 0:2048].rearrange("p (k n) -> p k n", k=8),
                         A["w_gate"][0, i].rearrange("(p k) n -> p k n", k=8)[:, :, cols]),
                        (raw[:, 2048:2560].rearrange("p (j n) -> p j n", j=2),
                         A["w_branch"][0, i].rearrange("(j p) n -> p j n", p=P)[:, :, cols])]
            u = n - NIN - NGATE
            return [(raw[:, 0:2048].rearrange("p (m n) -> p m n", m=2), w_out_v[:, 2 * u:2 * u + 2, :])]

        def raw_count(n):
            return sum(16 * (2 if NIN <= m < NIN + NGATE else 1) for m in range(n % NRAW, n + 1, NRAW))

        def unit_width(n):
            return 8 * (W_IN_UNITS[n][2] - W_IN_UNITS[n][1]) if n < NIN else 2048

        slot_plan = [(pair, kind, e) for pair in range(2) for kind in range(3) for e in range(2)]

        def expert_slot(pair, kind, e):
            return ex(slot_plan.index((pair, kind, e)))

        PAIRS = [(3, 0), (3, 1), (1, 0), (1, 1), (0, 0), (0, 1)]

        block = ctx.enter_context(nc.Block())

        @block.sync
        def _(sp):
            for t in range(TT):
                sp.dma_start(H[:, t, :], x_v[:, t, :]).then_inc(s.x_in, 16)

            def load_unit(n):
                if n >= NRAW:
                    m = n - NRAW
                    sp.wait_ge(s.w_lo, m + 1)
                    if NIN <= m < NIN + NGATE:
                        sp.wait_ge(s.unit_done, m + 1)
                for dst, src in unit_dmas(n):
                    sp.dma_start(dst, src).then_inc(raw_in[n % NRAW], 16)

            def load_expert(slot, q):
                pair, kind, e = slot_plan[slot]
                src = (e_gate, e_up, e_down)[kind]
                sp.dma_start(ex(slot), src[q * QUAD + 2 * pair + e]).then_inc(exp_in[slot], 16)

            for n in range(UNITS):
                load_unit(n)
                if n == PREFETCH_AT:
                    for slot in range(6):
                        load_expert(slot, 0)
            sp.wait_ge(s.w_lo, UNITS)
            for slot in range(6, 10):
                load_expert(slot, 0)
            sp.wait_ge(s.hs_split, TT)
            sp.wait_ge(s.hst_ps, 4)
            for slot in range(10, 12):
                load_expert(slot, 0)

            def free_slot(slot, n):
                pair, kind, _ = slot_plan[slot]
                if kind < 2:
                    after(sp, s.hid_ps, n * 2 - 1 + pair)
                else:
                    after(sp, s.y_ps, n * 4 - 2 + 2 * pair)

            with sp.Fori(1, NQ) as i:
                for slot in range(12):
                    if slot_plan[slot][2] == 0:
                        free_slot(slot, i)
                    load_expert(slot, i)
            sp.wait_ge(s.over_ready, 1)
            count = sp.value_load(LIST[0:1, 0:1], min_val=0, max_val=MAXOVER)
            with sp.If(count > 0):
                with sp.Fori(0, count) as j:
                    q = sp.value_load(LIST[0:1, bass.ds(j + 9, 1)], min_val=0, max_val=NQ - 1)
                    for slot in range(12):
                        if slot_plan[slot][2] == 0:
                            free_slot(slot, j + NQ)
                        load_expert(slot, q)
            sp.end_ifs()
            for t in range(TT):
                sp.wait_ge(s.out_ready, t + 1)
                sp.dma_start(out_v[:, t, :], YOUT[:, t, :]).then_inc(s.stored, 16)
            sp.wait_ge(s.stored, 16 * TT)

        @block.gpsimd
        def _(pool):
            for b in (3, 1, 0):
                nc.gpsimd.memset(KB[b], 0.0).then_inc(s.zeros_ready, 1)
            nc.gpsimd.memset(KPE, 0.0).then_inc(s.zeros_ready, 1)
            nc.gpsimd.memset(UPAD[:, :, 0:30], 0.0).then_inc(s.zeros_ready, 1)
            nc.gpsimd.memset(ZB, 0.0).then_inc(s.zeros_ready, 1)
            pool.wait_ge(s.wmla_in, 96)
            wq = WUQ[:, :, 256:384].rearrange("p j (h c) -> p j h c", h=HEADS)
            for j in range(2):
                nc.gpsimd.tensor_copy(WROT[:, j, :, 0:16], wq[:, j, :, 16:32]).then_inc(s.wrot_ready, 1)
                nc.gpsimd.tensor_copy(WROT[:, j, :, 16:32], wq[:, j, :, 0:16]).then_inc(s.wrot_ready, 1)

        @block.scalar
        def _(act):
            def rows(name):
                return ROWP[ROWS[name]:ROWS[name] + {"conv_w": 62, "b_gate": 32, "gkv": 1}.get(name, 2), :]

            act.dma_start(TABS[:, :], A["tables"]).then_inc(s.tables_in, 16)
            act.dma_start(rows("conv_w"), A["conv_w"][0].rearrange("k (j p) -> (k j) p", p=P)).then_inc(s.params_in, 16)
            for name, key in (("conv_b", "conv_b"), ("ln_g", "conv_ln_g"), ("ln_b", "conv_ln_b"), ("gq", "mla_gq"),
                              ("gkv", "mla_gkv")):
                act.dma_start(rows(name), A[key][0].rearrange("(j p) -> j p", p=P)).then_inc(s.params_in, 16)
            act.dma_start(rows("b_gate"), A["b_gate"][0].rearrange("i (m p) -> (i m) p", p=P)).then_inc(s.params_in, 16)
            act.dma_start(G1, A["norm1_g"][0].rearrange("(p k) -> p k", k=KD)).then_inc(s.norm_in, 16)
            act.dma_start(G2, A["norm2_g"][0].rearrange("(p k) -> p k", k=KD)).then_inc(s.norm_in, 16)
            for j in range(2):
                wuq = A["mla_wuq"][0, j * P:(j + 1) * P, :].rearrange("p (h c) -> p h c", h=HEADS)
                act.dma_start(WUQ[:, j, 0:256].rearrange("p (h c) -> p h c", h=HEADS), wuq[:, :, 0:64]).then_inc(s.wmla_in, 16)
                act.dma_start(WUQ[:, j, 256:384].rearrange("p (h c) -> p h c", h=HEADS), wuq[:, :, 64:96]).then_inc(s.wmla_in, 16)
            wukv = A["mla_wukv"][0].rearrange("p (h a c) -> p h a c", h=HEADS, a=2)
            for a in range(2):
                act.dma_start(WUKV[:, a * 256:(a + 1) * 256].rearrange("p (h c) -> p h c", h=HEADS), wukv[:, :, a, :])\
                    .then_inc(s.wmla_in, 16)
            act.dma_start(BF, A["b_forget"][0].partition_broadcast(P)).then_inc(s.bias_in, 16)
            act.dma_start(BR[:, 0:4], A["b_router_group"][0].partition_broadcast(P)).then_inc(s.bias_in, 16)
            act.dma_start(BR[:, 4:36], A["b_router_expert"][0].partition_broadcast(P)).then_inc(s.bias_in, 16)

            for t in range(TT):
                act.wait_ge(s.x_in, 32)
                nc.scalar.activation(M[:, t * D:(t + 1) * D], H[:, t, :], ACT.Square, accum_out=SS[:, t:t + 1]).then_inc(s.sumsq, 1)
            act.wait_ge(s.xvar, 1)
            nc.scalar.activation(RS, SS, ACT.Sqrt).then_inc(s.xroot, 1)
            act.wait_ge(s.norm_in, 32)
            for b in range(4):
                act.wait_ge(s.xt_ps, b + 1)
                for k in (2 * b, 2 * b + 1):
                    nc.scalar.activation(XH[:, k * T:(k + 1) * T], bank[b][:, (k % 2) * T:(k % 2 + 1) * T], ACT.Copy,
                                         scale=G1[:, k:k + 1]).then_inc(s.x_hi, 1)

            def split_hi(n):
                act.wait_ge(raw_in[n % NRAW], raw_count(n))
                if n >= 2:
                    act.wait_ge(s.unit_done, n - 1)
                    act.wait_ge(s.w_lo, n - 1)
                if n < NIN and W_IN_UNITS[n][0] == "ckv":
                    raw = RAW[n % NRAW][:, 0:8 * 160].rearrange("p (k n) -> p k n", k=8)
                    dst = WH[:, n % 2, 0:8 * 192].rearrange("p (k n) -> p k n", k=8)
                    nc.scalar.activation(dst[:, :, 0:160], raw, ACT.Copy)
                    nc.scalar.activation(dst[:, :, 160:176], raw[:, :, 144:160], ACT.Copy)
                    nc.scalar.activation(dst[:, :, 176:192], raw[:, :, 128:144], ACT.Copy).then_inc(s.w_hi, 1)
                    return
                w = unit_width(n)
                nc.scalar.activation(WH[:, n % 2, 0:w], RAW[n % NRAW][:, 0:w], ACT.Copy).then_inc(s.w_hi, 1)

            split_hi(0)
            split_hi(1)
            act.wait_ge(s.unit_done, 2)
            nc.scalar.activation(TMPA, PB[:, :], ACT.Tanh, scale=0.5).then_inc(s.conv_t, 1)
            split_hi(2)
            split_hi(3)
            act.wait_ge(s.unit_done, 3)
            act.wait_ge(s.conv_u, 1)
            nc.scalar.activation(CQ.rearrange("p j t -> p (j t)"), PA[:, :], ACT.Copy).then_inc(s.cq_sb, 1)
            nc.scalar.activation(TMPA, PA[:, :], ACT.Square).then_inc(s.cq_sq, 1)
            split_hi(4)
            act.wait_ge(s.unit_done, 4)
            nc.scalar.activation(CKV, PB[:, 0:T], ACT.Copy).then_inc(s.ckv_sb, 1)
            nc.scalar.activation(TMPB[:, 0:T], PB[:, 0:T], ACT.Square).then_inc(s.ckv_sq, 1)
            act.wait_ge(s.cq_ve, 1)
            nc.scalar.activation(TMPA[:, 0:T], TMPA[:, 0:T], ACT.Sqrt).then_inc(s.cq_root, 1)
            act.wait_ge(s.ckv_ve, 1)
            nc.scalar.activation(TMPB[:, 0:T], TMPB[:, 0:T], ACT.Sqrt).then_inc(s.ckv_root, 1)
            split_hi(5)
            act.wait_ge(s.fox_f, 1)
            nc.scalar.activation(FW[:, 16:24], FW[:, 8:16], ACT.Exp, scale=-1.0).then_inc(s.fox_exp, 1)
            act.wait_ge(s.fox_exp, 1)
            nc.scalar.activation(FW[:, 24:32], FW[:, 16:24], ACT.Ln, bias=1.0).then_inc(s.fox_ln, 1)
            for n in range(6, 10):
                split_hi(n)
                u = n - 1
                act.wait_ge(s.unit_done, u + 1)
                pb = (PA, PB)[u % 2]
                kind = W_IN_UNITS[u][0]
                b = 1 if kind.startswith("fox") else 0
                if kind.endswith("q"):
                    nc.scalar.activation(Q[b].rearrange("p j t -> p (j t)"), pb[:, :], ACT.Copy).then_inc(s.proj_evac, 1)
                else:
                    act.wait_ge(s.zeros_ready, 6)
                    for h in range(HEADS):
                        r = slice(64 * (h % 2), 64 * (h % 2) + 64)
                        ins = nc.scalar.activation(KB[b][r, h, :], pb[r, (h // 2) * T:(h // 2 + 1) * T], ACT.Copy)
                    ins.then_inc(s.proj_evac, 1)
            act.wait_ge(s.ln_cent, 1)
            nc.scalar.activation(TMPA, CACC.rearrange("p j t -> p (j t)"), ACT.Square).then_inc(s.ln_sq, 1)
            split_hi(10)
            act.wait_ge(s.unit_done, 10)
            nc.scalar.activation(VM.rearrange("p t c -> p (t c)"), PB[:, :], ACT.Copy).then_inc(s.proj_evac, 1)
            act.wait_ge(s.ln_ve, 1)
            nc.scalar.activation(TMPA[:, 0:T], TMPA[:, 0:T], ACT.Sqrt).then_inc(s.ln_root, 1)
            act.wait_ge(s.ln_z, 1)
            nc.scalar.activation(TMPA, CACC.rearrange("p j t -> p (j t)"), ACT.Tanh).then_inc(s.ln_t, 1)

            def exp_pair(p):
                b = PAIRS[p][0]
                scale = (96.0 if b == 3 else 64.0) ** -0.5
                act.wait_ge(s.neg_max, p + 1)
                for h in range(2):
                    for qt in range(2):
                        c = slice(0, P) if qt == 0 else slice(P, 384)
                        i = 2 * h + qt
                        nc.scalar.activation(PR[:, h, c], PR[:, h, c], ACT.Exp, bias=NMAX[:, i:i + 1], scale=scale,
                                             accum_out=SUMV[:, i:i + 1]).then_inc(s.prob_exp, 1)

            for g in range(NGATE):
                if g % 2 == 0 and g // 2 < len(PAIRS):
                    exp_pair(g // 2)
                if NIN + g + 1 < UNITS:
                    split_hi(NIN + g + 1)
                act.wait_ge(s.gate_ps, g + 1)
                if g >= 1:
                    act.wait_ge(s.tmp_mul, g)
                i, u = BRANCHES[g // 4], g % 4
                for m in range(2):
                    c = i * 8 + u * 2 + m
                    nc.scalar.activation(TMPB[:, m * T:(m + 1) * T], (PA, PB)[g % 2][:, m * T:(m + 1) * T], ACT.Tanh,
                                         bias=HGB[:, c:c + 1], scale=0.5).then_inc(s.gate_t, 1)
            act.wait_ge(s.unit_done, NIN + NGATE)
            act.wait_ge(s.merged, NGATE - 4)
            for m in range(KD):
                nc.scalar.activation(XH[:, m * T:(m + 1) * T], M[:, m * T:(m + 1) * T], ACT.Copy, scale=0.5)\
                    .then_inc(s.merge_hi, 1)
            for n in range(NIN + NGATE + 1, UNITS):
                split_hi(n)
            act.wait_ge(s.h_ready, 2 * TT)
            wr = WR
            act.dma_start(wr[:, :, 0:NG], A["w_router_group"][0].rearrange("(p k) n -> p k n", k=KD)).then_inc(s.router_in, 16)
            act.dma_start(wr[:, :, NG:36], A["w_router_expert"][0].rearrange("(p k) n -> p k n", k=KD)).then_inc(s.router_in, 16)
            act.dma_start(FG, A["final_g"].partition_broadcast(P)).then_inc(s.final_in, 16)
            for t in range(TT):
                nc.scalar.activation(M[:, t * D:(t + 1) * D], H[:, t, :], ACT.Square, accum_out=SS[:, t:t + 1])\
                    .then_inc(s.h_sq, 1)
            act.wait_ge(s.h_var, 1)
            nc.scalar.activation(RS, SS, ACT.Sqrt).then_inc(s.h_root, 1)
            for t in range(TT):
                act.wait_ge(s.h_scaled, t + 1)
                nc.scalar.activation(XH[:, t * D:(t + 1) * D], HS[:, t, :], ACT.Copy).then_inc(s.hs_hi, 1)
            act.wait_ge(s.router_exp, 1)
            nc.scalar.activation(RB[:, 8:16], RB[:, 0:8], ACT.Exp).then_inc(s.router_exp, 1)
            act.wait_ge(s.router_exp, 3)
            nc.scalar.activation(RB[:, 18:20], RB[:, 16:18], ACT.Exp).then_inc(s.router_exp, 1)

            def step(n):
                for pair in range(2):
                    after(act, s.hid_ps, n * 2 + pair + 1)
                    after(act, s.hid_ready, n * 2 + pair)
                    nc.scalar.activation(TH[:, pair, :], bank[0 + pair][:, 0:FF], ACT.Tanh, scale=0.5)\
                        .then_inc(s.hid_t, 1)
                for pair in range(2):
                    for half in range(2):
                        after(act, s.y_ps, n * 4 + 2 * pair + half + 1)
                        after(act, s.o_ps, n * 4)
                        after(act, s.selt_sb, n * 2 + pair + 1)
                        nc.scalar.activation(WH[:, pair, half * 512:half * 512 + 512], bank[2 + half][:, :], ACT.Copy,
                                             scale=WS[:, pair:pair + 1]).then_inc(s.y_hi, 1)

            step(0)
            with act.Fori(1, NQ) as i:
                step(i)
            act.wait_ge(s.over_ready, 1)
            count = act.value_load(LIST[0:1, 0:1], min_val=0, max_val=MAXOVER)
            with act.If(count > 0):
                with act.Fori(0, count) as j:
                    step(j + NQ)
            act.end_ifs()
            act.wait_ge(s.final_sq, 1)
            for t in range(TT):
                nc.scalar.activation(YOUT[:, t, :], H[:, t, :], ACT.Square, accum_out=SS[:, t:t + 1])\
                    .then_inc(s.final_sq, 1)
            act.wait_ge(s.final_var, 1)
            nc.scalar.activation(RS, SS, ACT.Sqrt).then_inc(s.final_root, 1)

        @block.vector
        def _(dve):
            V = nc.vector
            chain = [0]

            def link(ins):
                chain[0] += 1
                ins.then_inc(s.x_chain, 1)
                dve.wait_ge(s.x_chain, chain[0])

            f32 = lambda ap: ap.bitcast(F32)

            dve.wait_ge(s.sumsq, TT)
            V.tensor_scalar(SS, SS, 1.0 / D, EPS, ALU.mult, ALU.add).then_inc(s.xvar, 1)
            dve.wait_ge(s.xroot, 1)
            link(V.reciprocal(RS, RS))
            for t in range(TT):
                V.tensor_scalar(M[:, t * D:(t + 1) * D], H[:, t, :], RS[:, t:t + 1], None, ALU.mult).then_inc(s.xscaled, 1)
            dve.wait_ge(s.params_ps, 1)
            V.tensor_copy(PAR, MISC[:, 0:NROWS]).then_inc(s.params_sb, 1)
            dve.wait_ge(s.params_sb, 1)
            V.tensor_scalar(HPAR, PAR[:, ROWS["ln_g"]:ROWS["ln_g"] + 4], 0.5, None, ALU.mult).then_inc(s.half_params, 1)
            V.tensor_scalar(HGB, PAR[:, ROWS["b_gate"]:ROWS["b_gate"] + 32], 0.5, None, ALU.mult).then_inc(s.half_params, 1)
            for k in range(KD):
                dve.wait_ge(s.x_hi, 2 * (k // 2) + 2)
                V.scalar_tensor_tensor(XL[:, k * T:(k + 1) * T], bank[k // 2][:, (k % 2) * T:(k % 2 + 1) * T],
                                       G1[:, k:k + 1], f32(XH[:, k * T:(k + 1) * T]), ALU.mult, ALU.subtract)\
                    .then_inc(s.x_split, 1)

            def split_lo(n):
                dve.wait_ge(s.w_hi, n + 1)
                if n < NIN and W_IN_UNITS[n][0] == "ckv":
                    raw = RAW[n % NRAW][:, 0:8 * 160].rearrange("p (k n) -> p k n", k=8)
                    hi = f32(WH[:, n % 2, 0:8 * 192]).rearrange("p (k n) -> p k n", k=8)
                    lo = WL[:, n % 2, 0:8 * 192].rearrange("p (k n) -> p k n", k=8)
                    for a, b, c in ((0, 0, 160), (160, 144, 16), (176, 128, 16)):
                        ins = V.tensor_tensor(lo[:, :, a:a + c], raw[:, :, b:b + c], hi[:, :, a:a + c], ALU.subtract)
                    ins.then_inc(s.w_lo, 1)
                    return
                w = unit_width(n)
                V.tensor_tensor(WL[:, n % 2, 0:w], RAW[n % NRAW][:, 0:w], f32(WH[:, n % 2, 0:w]), ALU.subtract)\
                    .then_inc(s.w_lo, 1)

            steps = [0]

            def conv_steps(count):
                for _ in range(count):
                    k, j = divmod(steps[0], 2)
                    if k >= CONV_K:
                        return
                    if steps[0] >= 2:
                        dve.wait_ge(s.conv_acc, steps[0] - 1)
                    w = PAR[:, ROWS["conv_w"] + 2 * k + j:ROWS["conv_w"] + 2 * k + j + 1]
                    src = UPAD[:, j, k:k + T]
                    if k == 0:
                        ins = V.tensor_scalar(CACC[:, j, :], src, w, None, ALU.mult)
                    else:
                        ins = V.scalar_tensor_tensor(CACC[:, j, :], src, w, CACC[:, j, :], ALU.mult, ALU.add)
                    ins.then_inc(s.conv_acc, 1)
                    steps[0] += 1

            split_lo(0)
            split_lo(1)
            split_lo(2)
            dve.wait_ge(s.conv_t, 1)
            dve.wait_ge(s.zeros_ready, 6)
            V.scalar_tensor_tensor(UPAD[:, :, 30:286], TMPA.rearrange("p (j t) -> p j t", j=2), 1.0,
                                   PA[:, :].rearrange("p (j t) -> p j t", j=2), ALU.add, ALU.mult).then_inc(s.conv_u, 1)
            split_lo(3)
            dve.wait_ge(s.conv_u, 1)
            conv_steps(12)
            dve.wait_ge(s.cq_sum, 1)
            dve.wait_ge(s.ckv_sum, 1)
            V.tensor_scalar(TMPA[:, 0:T], MISC[:, 0:T], 1.0 / 256, EPS, ALU.mult, ALU.add).then_inc(s.cq_ve, 1)
            dve.wait_ge(s.ckv_sum, 1)
            V.tensor_scalar(TMPB[:, 0:T], MISC[:, T:2 * T], 1.0 / 128, EPS, ALU.mult, ALU.add).then_inc(s.ckv_ve, 1)
            dve.wait_ge(s.unit_done, 4)
            dve.wait_ge(s.tables_in, 16)
            V.tensor_tensor(TMPB[64:128, T:2 * T], PB[64:128, T:2 * T], TABS[64:128, TAB["kcs"][0]:TAB["kcs"][1]], ALU.mult)\
                .then_inc(s.krope_sb, 1)
            split_lo(4)
            dve.wait_ge(s.cq_root, 1)
            link(V.reciprocal(TMPA[:, 0:T], TMPA[:, 0:T]))
            for j in range(2):
                V.scalar_tensor_tensor(CQ[:, j, :], CQ[:, j, :], par("gq", j), TMPA[:, 0:T], ALU.mult, ALU.mult)\
                    .then_inc(s.cq_ready, 1)
            dve.wait_ge(s.ckv_root, 1)
            link(V.reciprocal(TMPB[:, 0:T], TMPB[:, 0:T]))
            V.scalar_tensor_tensor(CKV, CKV, par("gkv"), TMPB[:, 0:T], ALU.mult, ALU.mult).then_inc(s.ckv_ready, 1)
            split_lo(5)
            conv_steps(12)
            dve.wait_ge(s.unit_done, 5)
            for t in range(TT):
                link(V.tensor_copy(VF[:, t, :], (PA, S0)[t][:, 0:260]))
            dve.wait_ge(s.bias_in, 48)
            fw = FW[:, 0:8].rearrange("p (t h) -> p t h", t=TT)
            link(V.tensor_tensor(fw, VF[:, :, 256:260], BF.unsqueeze(1).to_broadcast([P, TT, HEADS]), ALU.add))
            V.scalar_tensor_tensor(FW[:, 8:16], FW[:, 0:8], -1.0, FW[:, 0:8], ALU.mult, ALU.max).then_inc(s.fox_f, 1)
            split_lo(6)
            conv_steps(12)
            dve.wait_ge(s.fox_ln, 1)
            V.scalar_tensor_tensor(FLOG.rearrange("p t h -> p (t h)"), FW[:, 0:8], 0.0, FW[:, 24:32], ALU.min, ALU.subtract)\
                .then_inc(s.fox_ready, 1)
            dve.wait_ge(s.mla_ps, 1)
            V.tensor_copy(Q[3].rearrange("p j t -> p (j t)"), S1[:, :]).then_inc(s.mla_evac, 1)
            dve.wait_ge(s.mla_ps, 2)
            dve.wait_ge(s.ckv_ready, 1)
            dve.wait_ge(s.cq_ready, 2)
            V.tensor_tensor(TMPA[:, 0:T], PT[:, 0:T], tab("cos"), ALU.mult).then_inc(s.rope_mul, 1)
            V.tensor_tensor(TMPA[:, T:2 * T], PT[:, T:2 * T], tab("sin"), ALU.mult).then_inc(s.rope_mul, 1)
            dve.wait_ge(s.rope_mul, 2)
            V.tensor_tensor(QPE, TMPA[:, 0:T], TMPA[:, T:2 * T], ALU.add).then_inc(s.mla_evac, 1)
            split_lo(7)
            conv_steps(12)
            dve.wait_ge(s.mla_ps, 3)
            for h in range(HEADS):
                r = slice(64 * (h % 2), 64 * (h % 2) + 64)
                ins = V.tensor_copy(KB[3][r, h, :], PV[r, (h // 2) * T:(h // 2 + 1) * T])
            ins.then_inc(s.mla_evac, 1)
            dve.wait_ge(s.mla_ps, 4)
            V.tensor_copy(VMLA.rearrange("p t c -> p (t c)"), BRB[:, :]).then_inc(s.mla_evac, 1)
            split_lo(8)
            conv_steps(62)
            dve.wait_ge(s.conv_acc, 2 * CONV_K)
            for j in range(2):
                V.tensor_scalar(CACC[:, j, :], CACC[:, j, :], 0.5, par("conv_b", j), ALU.mult, ALU.add).then_inc(s.conv_out, 1)
            dve.wait_ge(s.kpe_ps, 1)
            for h in range(HEADS):
                r = slice(32 * h, 32 * h + 32)
                ins = V.tensor_copy(KPE[r, h, :], S1[r, 0:T])
            ins.then_inc(s.kpe_ready, 1)
            dve.wait_ge(s.fox_ps, 1)
            V.tensor_scalar(CTOK.rearrange("p t h -> p (t h)"), MISC[:, 0:8], 8.0, None, ALU.mult).then_inc(s.cum_ready, 1)
            for h in range(HEADS):
                ins = V.tensor_scalar(CB[:, h, :], MISC[0:HEADS, T:2 * T], TABS[0:HEADS, h:h + 1], -8.0, ALU.mult, ALU.mult)
            ins.then_inc(s.cum_ready, 1)
            split_lo(9)
            dve.wait_ge(s.ln_sum, 1)
            V.scalar_tensor_tensor(CACC, MISC[:, 0:T].unsqueeze(1).to_broadcast([P, 2, T]), -1.0 / 256, CACC, ALU.mult, ALU.add)\
                .then_inc(s.ln_cent, 1)
            split_lo(10)
            dve.wait_ge(s.ln_var, 1)
            V.tensor_scalar(TMPA[:, 0:T], MISC[:, 0:T], 1.0 / 256, EPS, ALU.mult, ALU.add).then_inc(s.ln_ve, 1)
            dve.wait_ge(s.ln_root, 1)
            link(V.reciprocal(TMPA[:, 0:T], TMPA[:, 0:T]))
            link(V.tensor_tensor(CACC, CACC, TMPA[:, 0:T].unsqueeze(1).to_broadcast([P, 2, T]), ALU.mult))
            for j in range(2):
                ins = V.tensor_scalar(CACC[:, j, :], CACC[:, j, :], HPAR[:, j:j + 1], HPAR[:, 2 + j:3 + j], ALU.mult, ALU.add)
            ins.then_inc(s.ln_z, 1)
            dve.wait_ge(s.ln_t, 1)
            V.scalar_tensor_tensor(YT[2].rearrange("p j t -> p (j t)"), TMPA, 1.0, CACC.rearrange("p j t -> p (j t)"),
                                   ALU.add, ALU.mult).then_inc(s.yc_ready, 1)

            def logits(p):
                b, hp = PAIRS[p]
                scale = (96.0 if b == 3 else 64.0) ** -0.5
                dve.wait_ge(s.score_ps, p + 1)
                if p:
                    dve.wait_ge(s.pt_ps, 2 * p)
                else:
                    dve.wait_ge(s.mla_ps, 4)
                for qt in range(2):
                    for h in range(2):
                        c = slice(0, P) if qt == 0 else slice(P, 384)
                        n = P if qt == 0 else T
                        sc = (S0, S1)[qt][:, h * n:(h + 1) * n]
                        head = 2 * hp + h
                        if b == 0:
                            slope = 2.0 ** (-8.0 * (head + 1) / HEADS)
                            V.scalar_tensor_tensor(PR[:, h, c], tab("dist")[:, c], slope / scale, sc, ALU.mult, ALU.add)\
                                .then_inc(s.logit_ready, 1)
                        elif b == 1:
                            V.scalar_tensor_tensor(PR[:, h, c], sc, CTOK[:, qt, head:head + 1], tab("mask")[:, c],
                                                   ALU.add, ALU.add).then_inc(s.logit_ready, 1)
                        else:
                            V.tensor_tensor(PR[:, h, c], sc, tab("mask")[:, c], ALU.add).then_inc(s.logit_ready, 1)
                mv = MAXV.rearrange("p (h q) -> p h q", h=2)
                for qt in range(2):
                    dve.wait_ge(s.logit_ready, 4 * p + 2 * qt + 2)
                    c = slice(0, P) if qt == 0 else slice(P, 384)
                    V.reduce_max(mv[:, :, qt:qt + 1], PR[:, :, c], AXX).then_inc(s.row_max, 1)
                dve.wait_ge(s.row_max, 2 * p + 2)
                V.tensor_scalar(NMAX, MAXV, -scale, None, ALU.mult).then_inc(s.neg_max, 1)

            def normalise(p):
                dve.wait_ge(s.prob_exp, 4 * p + 4)
                link(V.reciprocal(RECV, SUMV))
                for h in range(2):
                    for qt in range(2):
                        c = slice(0, P) if qt == 0 else slice(P, 384)
                        i = 2 * h + qt
                        ins = V.tensor_scalar(PR[:, h, c], PR[:, h, c], RECV[:, i:i + 1], None, ALU.mult)
                    ins.then_inc(s.prob_ready, 1)

            def attend(p):
                b, hp = PAIRS[p]
                for h in range(2):
                    dve.wait_ge(s.pt_ps, 2 * p + h + 1)
                    if 2 * p + h >= 1:
                        dve.wait_ge(s.pv_ps, 2 * p + h)
                    V.tensor_copy(PTS, PT[:, 0:384]).then_inc(s.pt_sb, 1)
                dve.wait_ge(s.pv_ps, 2 * p + 2)
                V.tensor_copy(YT[b][:, hp, :], PV[:, 0:T]).then_inc(s.attn_ready, 1)

            for g in range(NGATE):
                if g % 2 == 0 and 0 < g // 2 <= len(PAIRS):
                    attend(g // 2 - 1)
                if g % 2 == 0 and g // 2 < len(PAIRS):
                    logits(g // 2)
                if NIN + g + 1 < UNITS:
                    split_lo(NIN + g + 1)
                if g % 2 == 0 and g // 2 < len(PAIRS):
                    normalise(g // 2)
                dve.wait_ge(s.gate_t, 2 * g + 2)
                dve.wait_ge(s.unit_done, NIN + g + 1)
                u = g % 4
                mc = M[:, u * 512:(u + 1) * 512]
                if g < 4:
                    V.scalar_tensor_tensor(mc, TMPB, 1.0, BRB[:, :], ALU.add, ALU.mult).then_inc(s.tmp_mul, 1)
                else:
                    if g > 4:
                        dve.wait_ge(s.merged, g - 4)
                    V.scalar_tensor_tensor(TMPA, TMPB, 1.0, BRB[:, :], ALU.add, ALU.mult).then_inc(s.tmp_mul, 1)
                    dve.wait_ge(s.tmp_mul, g + 1)
                    V.tensor_tensor(mc, mc, TMPA, ALU.add).then_inc(s.merged, 1)
            for m in range(KD):
                dve.wait_ge(s.merge_hi, m + 1)
                V.scalar_tensor_tensor(XL[:, m * T:(m + 1) * T], M[:, m * T:(m + 1) * T], 0.5,
                                       f32(XH[:, m * T:(m + 1) * T]), ALU.mult, ALU.subtract).then_inc(s.merge_split, 1)
            for n in range(NIN + NGATE + 1, UNITS):
                split_lo(n)
            dve.wait_ge(s.unit_done, UNITS)
            for t in range(TT):
                for half in range(2):
                    c = slice(half * 512, half * 512 + 512)
                    V.tensor_tensor(H[:, t, c], H[:, t, c], bank[2 * t + half][:, :], ALU.add).then_inc(s.h_ready, 1)
            dve.wait_ge(s.h_sq, TT)
            V.tensor_scalar(SS, SS, 1.0 / D, EPS, ALU.mult, ALU.add).then_inc(s.h_var, 1)
            dve.wait_ge(s.h_root, 1)
            link(V.reciprocal(RS, RS))
            for t in range(TT):
                V.tensor_scalar(HS[:, t, :], H[:, t, :], RS[:, t:t + 1], None, ALU.mult).then_inc(s.h_scaled, 1)
            for b in range(4):
                dve.wait_ge(s.hst_ps, b + 1)
                for k in (2 * b, 2 * b + 1):
                    V.tensor_scalar(M[:, k * T:(k + 1) * T], bank[b][:, (k % 2) * T:(k % 2 + 1) * T], G2[:, k:k + 1], None,
                                    ALU.mult).then_inc(s.hst_sb, 1)
            for t in range(TT):
                dve.wait_ge(s.hs_hi, t + 1)
                V.tensor_tensor(XL[:, t * D:(t + 1) * D], HS[:, t, :], f32(XH[:, t * D:(t + 1) * D]), ALU.subtract)\
                    .then_inc(s.hs_split, 1)

            rc = [0]

            def rlink(ins):
                rc[0] += 1
                ins.then_inc(s.router_chain, 1)
                dve.wait_ge(s.router_chain, rc[0])

            rb = carver(RB, 800)
            GD = rb(8).rearrange("p (t g) -> p t g", t=TT)
            GE = rb(8).rearrange("p (t g) -> p t g", t=TT)
            DM = rb(2)
            EX2 = rb(2)
            one = lambda: rb(2)
            grp = lambda: rb(8).rearrange("p (t g) -> p t g", t=TT)
            exl = lambda: rb(16).rearrange("p (t e) -> p t e", t=TT)
            all_ = lambda: rb(64).rearrange("p (t g e) -> p t g e", t=TT, g=NG)
            GMAX, PG, IDX, M1, M2, W1, W2 = (one() for _ in range(7))
            GC, OG = grp(), grp()
            EIN, ED, OE1, OE2, O8, W8, E2 = (exl() for _ in range(7))
            EALL, O32 = all_(), all_()

            def spread(v, n):
                return v.unsqueeze(2).to_broadcast([P, TT, n])

            def iota(n):
                return tab("iota")[:, 0:n].unsqueeze(1).to_broadcast([P, TT, n])

            def first_of_max(onehot, dist, work, n):
                rlink(V.tensor_scalar(work, dist, 0.0, 100.0, ALU.is_lt, ALU.mult))
                rlink(V.tensor_tensor(work, work, iota(n), ALU.add))
                rlink(V.tensor_reduce(IDX, work, AXX, ALU.min))
                rlink(V.tensor_tensor(onehot, iota(n), spread(IDX, n), ALU.is_equal))

            dve.wait_ge(s.logits_ps, 1)
            rlink(V.tensor_tensor(LG, MISC[:, 0:72].rearrange("p (t n) -> p t n", t=TT),
                                  BR.unsqueeze(1).to_broadcast([P, TT, 36]), ALU.add))
            rlink(V.reduce_max(GMAX, LG[:, :, 0:NG], AXX))
            V.tensor_tensor(GD, LG[:, :, 0:NG], spread(GMAX, NG), ALU.subtract).then_inc(s.router_exp, 1)
            dve.wait_ge(s.router_exp, 1)
            first_of_max(OG, GD, GC, NG)
            rlink(V.tensor_tensor(EALL, LG[:, :, NG:36].rearrange("p t (g e) -> p t g e", g=NG),
                                  OG.unsqueeze(3).to_broadcast([P, TT, NG, EG]), ALU.mult))
            rlink(V.reduce_sum(EIN, EALL.rearrange("p t g e -> p t e g"), AXX))
            rlink(V.reduce_max(M1, EIN, AXX))
            rlink(V.tensor_tensor(ED, EIN, spread(M1, EG), ALU.subtract))
            first_of_max(OE1, ED, E2, EG)
            rlink(V.scalar_tensor_tensor(EIN, OE1, -3e38, EIN, ALU.mult, ALU.add))
            rlink(V.reduce_max(M2, EIN, AXX))
            dve.wait_ge(s.router_exp, 2)
            V.tensor_tensor(DM, M2, M1, ALU.subtract).then_inc(s.router_exp, 1)
            rlink(V.tensor_tensor(ED, EIN, spread(M2, EG), ALU.subtract))
            first_of_max(OE2, ED, E2, EG)
            rlink(V.reduce_sum(PG, GE, AXX))
            rlink(V.reciprocal(PG, PG))
            dve.wait_ge(s.router_exp, 4)
            rlink(V.tensor_scalar(W1, EX2, 1.0, None, ALU.add))
            rlink(V.reciprocal(W1, W1))
            rlink(V.tensor_tensor(W1, W1, PG, ALU.mult))
            rlink(V.tensor_tensor(W2, W1, EX2, ALU.mult))
            rlink(V.tensor_tensor(O8, OE1, OE2, ALU.add))
            rlink(V.tensor_tensor(OE1, OE1, spread(W1, EG), ALU.mult))
            rlink(V.tensor_tensor(OE2, OE2, spread(W2, EG), ALU.mult))
            rlink(V.tensor_tensor(W8, OE1, OE2, ALU.add))

            def outer(dst, a8):
                V_in = a8.unsqueeze(2).to_broadcast([P, TT, NG, EG])
                return V.tensor_tensor(dst, OG.unsqueeze(3).to_broadcast([P, TT, NG, EG]), V_in, ALU.mult)

            rlink(outer(WT.rearrange("p t (g e) -> p t g e", g=NG), W8))
            outer(O32, O8).then_inc(s.sel_ready, 1)
            dve.wait_ge(s.rank_ps, 1)
            o32 = O32.rearrange("p t g e -> p t (g e)")
            rlink(V.tensor_tensor(RANK[:, :, 0:NE], S0[:, 0:2 * NE].rearrange("p (t e) -> p t e", t=TT), o32, ALU.mult))
            for r in range(ROUNDS, -1, -1):
                rlink(V.tensor_scalar(RANK[:, :, r * NE:(r + 1) * NE], RANK[:, :, 0:NE], -1.0 - CAP * r, None, ALU.add))

            oc = [0]

            def olink(ins):
                oc[0] += 1
                ins.then_inc(s.over_chain, 1)
                dve.wait_ge(s.over_chain, oc[0])

            NC = ROUNDS * NQ
            ov = carver(OV, 700)
            CMAX, FLAG, POS = ov(NQ), ov(NC), ov(NC)
            EQ = ov(8 * NC).rearrange("p (j c) -> p j c", j=8)
            EQC = ov(8 * NC).rearrange("p (j c) -> p j c", j=8)
            LF = ov(17)
            olink(V.reduce_max(CMAX, S0[:, 2 * NE:3 * NE].rearrange("p (q e) -> p q e", q=NQ), AXX))
            for r in range(ROUNDS):
                olink(V.tensor_scalar(FLAG[:, r * NQ:(r + 1) * NQ], CMAX, float(CAP * (r + 1)), None, ALU.is_gt))
            olink(V.tensor_tensor_scan(POS, ones_mat[:, 0:NC], FLAG, 0.0, ALU.mult, ALU.add))
            olink(V.reduce_max(LF[:, 0:1], POS, AXX))
            olink(V.tensor_tensor(POS, POS, FLAG, ALU.mult))
            jota = tab("iota")[:, 1:9].unsqueeze(2).to_broadcast([P, 8, NC])
            olink(V.tensor_tensor(EQ, POS.unsqueeze(1).to_broadcast([P, 8, NC]), jota, ALU.is_equal))
            for i in range(2):
                code = tab("code")[:, i * NC:(i + 1) * NC].unsqueeze(1).to_broadcast([P, 8, NC])
                olink(V.tensor_tensor(EQC, EQ, code, ALU.mult))
                olink(V.reduce_sum(LF[:, 1 + 8 * i:9 + 8 * i], EQC, AXX))
            V.tensor_copy(LIST[0:1, 0:17], LF[0:1, :]).then_inc(s.over_ready, 1)

            def select(n, col):
                after(dve, s.wselt_ps, n * 2)
                after(dve, s.gather_ps, n * 4)
                slot = tab("iota").unsqueeze(1).to_broadcast([P, QUAD, CAP])
                for t in range(TT):
                    V.tensor_tensor(SEL[:, t, :, :], RANK[:, t, bass.ds(col, QUAD)].unsqueeze(2).to_broadcast([P, QUAD, CAP]),
                                    slot, ALU.is_equal).then_inc(s.sel_chain, 1)
                after(dve, s.sel_chain, n * 2 + 2)

            def weigh(n, expert):
                for t in range(TT):
                    V.tensor_tensor(WSEL[:, t, :, :], f32(SEL[:, t, :, :]),
                                    WT[:, t, bass.ds(expert, QUAD)].unsqueeze(2).to_broadcast([P, QUAD, CAP]), ALU.mult)\
                        .then_inc(s.over_sel, 1)

            def take_gathered(n):
                for b in range(4):
                    after(dve, s.gather_ps, n * 4 + b + 1)
                    for k in (2 * b, 2 * b + 1):
                        V.tensor_scalar(M[:, k * T:(k + 1) * T], bank[6][:, (k % 2) * T:(k % 2 + 1) * T], G2[:, k:k + 1], None,
                                        ALU.mult).then_inc(s.xe_ready, 1)

            def y_low(n, pair):
                for half in range(2):
                    after(dve, s.y_hi, n * 4 + 2 * pair + half + 1)
                    V.scalar_tensor_tensor(WL[:, pair, half * 512:half * 512 + 512], bank[2 + half][:, :],
                                           WS[:, pair:pair + 1], f32(WH[:, pair, half * 512:half * 512 + 512]),
                                           ALU.mult, ALU.subtract).then_inc(s.y_split, 1)

            def hidden(n, pair):
                hb = bank[pair]
                after(dve, s.hid_t, n * 2 + pair + 1)
                V.scalar_tensor_tensor(TH[:, pair, :], TH[:, pair, :], 1.0, hb[:, 0:FF], ALU.add, ALU.mult)\
                    .then_inc(s.step_chain, 1)
                after(dve, s.step_chain, n * 2 + pair + 1)
                V.scalar_tensor_tensor(HT_[:, pair, :], TH[:, pair, :], 0.5, hb[:, FF:2 * FF], ALU.mult, ALU.mult)\
                    .then_inc(s.hid_ready, 1)

            def hidden_t(n, pair):
                after(dve, s.hidt_ps, n * 2 + pair + 1)
                V.tensor_copy(HTT[:, pair, :, :], bank[7][:, T:2 * T].rearrange("p (j c) -> p j c", j=2)).then_inc(s.hidt_sb, 1)

            def step(n, gather_next):
                for pair in range(2):
                    after(dve, s.wselt_ps, n * 2 + pair + 1)
                    if pair == 0:
                        after(dve, s.o_ps, n * 4)
                    V.reduce_max(WS[:, pair:pair + 1], bank[7][:, 0:T], AXX).then_inc(s.over_w, 1)
                    after(dve, s.over_w, n * 2 + pair + 1)
                    V.tensor_scalar(SELT[:, pair, :], bank[7][:, 0:T], 0.0, None, ALU.is_gt).then_inc(s.selt_sb, 1)
                if gather_next is not None:
                    gather_next()
                hidden(n, 0)
                hidden_t(n, 0)
                hidden(n, 1)
                if gather_next is not None:
                    take_gathered(n + 1)
                hidden_t(n, 1)
                y_low(n, 0)
                y_low(n, 1)
                for t in range(TT):
                    for half in range(2):
                        c = slice(half * 512, half * 512 + 512)
                        after(dve, s.o_ps, n * 4 + 2 * t + half + 1)
                        V.tensor_tensor(H[:, t, c], H[:, t, c], bank[4 + half][:, :], ALU.add).then_inc(s.o_added, 1)

            def select_static(n, col, expert):
                select(n, col)
                weigh(n, expert)

            select_static(0, 0, 0)
            take_gathered(0)
            step(0, lambda: select_static(1, QUAD, QUAD))
            with dve.Fori(1, NQ - 1) as i:
                step(i, lambda: select_static(i + 1, i * QUAD + QUAD, i * QUAD + QUAD))
            step(NQ - 1, None)
            count = dve.value_load(LIST[0:1, 0:1], min_val=0, max_val=MAXOVER)
            with dve.If(count > 0):
                with dve.Fori(0, count) as j:
                    col = dve.value_load(LIST[0:1, bass.ds(j + 1, 1)], min_val=0, max_val=(ROUNDS + 1) * NE - QUAD)
                    q = dve.value_load(LIST[0:1, bass.ds(j + 9, 1)], min_val=0, max_val=NQ - 1)
                    select_static(j + NQ, col, q * QUAD)
                    take_gathered(j + NQ)
                    step(j + NQ, None)
            dve.end_ifs()
            dve.drain().then_inc(s.final_sq, 1)
            dve.wait_ge(s.final_sq, 1 + TT)
            V.tensor_scalar(SS, SS, 1.0 / D, EPS, ALU.mult, ALU.add).then_inc(s.final_var, 1)
            dve.wait_ge(s.final_root, 1)
            link(V.reciprocal(RS, RS))
            dve.wait_ge(s.final_in, 16)
            for t in range(TT):
                V.scalar_tensor_tensor(YOUT[:, t, :], H[:, t, :], RS[:, t:t + 1], FG, ALU.mult, ALU.mult)\
                    .then_inc(s.out_ready, 1)

        @block.tensor
        def _(pe):
            mm = nc.tensor.matmul

            def transpose(dst, src):
                k = src.shape[0]
                return nc.tensor.transpose(dst, src, ident[0:k, 0:k])

            pe.wait_ge(s.tables_in, 16)
            pe.wait_ge(s.params_in, 16 * 7)
            transpose(MISC[:, 0:NROWS], ROWP[0:NROWS, :]).then_inc(s.params_ps, 1)
            pe.wait_ge(s.xscaled, TT)
            xs = M[:, :].rearrange("p (t q k) -> p t q k", t=TT, k=KD)
            for k in range(KD):
                for t in range(TT):
                    ins = transpose(bank[k // 2][:, (k % 2) * T + t * P:(k % 2) * T + (t + 1) * P], xs[:, t, :, k])
                if k % 2:
                    ins.then_inc(s.xt_ps, 1)

            def three(dst, wh, wl, xh, xl, first, last):
                mm(dst, wh, xh, start=first, stop=False)
                mm(dst, wl, xh, start=False, stop=False)
                return mm(dst, wh, xl, start=False, stop=last)

            def act_tile(k, c=slice(0, T)):
                a = slice(k * T + c.start, k * T + c.stop)
                return XH[:, a], XL[:, a]

            def project(n, dst, c0, ncol, width=128):
                for k in range(KD):
                    c = slice(k * ncol + c0, k * ncol + c0 + width)
                    ins = three(dst, WH[:, n % 2, c], WL[:, n % 2, c], *act_tile(k), k == 0, k == KD - 1)
                return ins

            def project_tokens(n, dsts, ncol):
                for t in range(TT):
                    for k in range(KD):
                        xh, xl = act_tile(k, slice(t * P, (t + 1) * P))
                        c = slice(k * ncol, (k + 1) * ncol)
                        wh, wl = WH[:, n % 2, c], WL[:, n % 2, c]
                        mm(dsts[t], xh, wh, start=(k == 0), stop=False)
                        mm(dsts[t], xl, wh, start=False, stop=False)
                        ins = mm(dsts[t], xh, wl, start=False, stop=(k == KD - 1))
                return ins

            pe.wait_ge(s.x_split, KD)
            pe.wait_ge(s.w_lo, 1)
            for m in range(2):
                ins = project(0, PA[:, m * T:(m + 1) * T], m * 128, 256)
            ins.then_inc(s.unit_done, 1)
            pe.wait_ge(s.w_lo, 2)
            for m in range(2):
                ins = project(1, PB[:, m * T:(m + 1) * T], m * 128, 256)
            ins.then_inc(s.unit_done, 1)
            pe.wait_ge(s.w_lo, 3)
            pe.wait_ge(s.conv_u, 1)
            for m in range(2):
                ins = project(2, PA[:, m * T:(m + 1) * T], m * 128, 256)
            ins.then_inc(s.unit_done, 1)
            pe.wait_ge(s.w_lo, 4)
            project(3, PB[:, 0:T], 0, 192)
            project(3, PB[:, T:2 * T], 64, 192).then_inc(s.unit_done, 1)
            pe.wait_ge(s.params_sb, 1)
            pe.wait_ge(s.cq_sq, 1)
            for j in range(2):
                ins = mm(MISC[:, 0:T], ones_mat, TMPA[:, j * T:(j + 1) * T], start=(j == 0), stop=(j == 1))
            ins.then_inc(s.cq_sum, 1)
            pe.wait_ge(s.ckv_sq, 1)
            mm(MISC[:, T:2 * T], ones_mat, TMPB[:, 0:T], start=True, stop=True).then_inc(s.ckv_sum, 1)
            pe.wait_ge(s.w_lo, 5)
            pe.wait_ge(s.cq_sq, 1)
            project_tokens(4, [PA[:, 0:260], S0[:, 0:260]], 260).then_inc(s.unit_done, 1)
            pe.wait_ge(s.cq_ready, 2)
            pe.wait_ge(s.wmla_in, 96)
            pe.wait_ge(s.wrot_ready, 4)
            for m in range(2):
                for j in range(2):
                    ins = mm(S1[:, m * T:(m + 1) * T], WUQ[:, j, m * P:(m + 1) * P], CQ[:, j, :], start=(j == 0), stop=(j == 1))
            ins.then_inc(s.mla_ps, 1)
            for j in range(2):
                mm(PT[:, 0:T], WUQ[:, j, 256:384], CQ[:, j, :], start=(j == 0), stop=(j == 1))
            for j in range(2):
                ins = mm(PT[:, T:2 * T], WROT[:, j, :, :].rearrange("p h c -> p (h c)"), CQ[:, j, :], start=(j == 0), stop=(j == 1))
            ins.then_inc(s.mla_ps, 1)
            pe.wait_ge(s.w_lo, 6)
            pe.wait_ge(s.ckv_sq, 1)
            pe.wait_ge(s.krope_sb, 1)
            for m in range(2):
                ins = project(5, PB[:, m * T:(m + 1) * T], m * 128, 256)
            ins.then_inc(s.unit_done, 1)
            pe.wait_ge(s.ckv_ready, 1)
            for m in range(2):
                ins = mm(PV[:, m * T:(m + 1) * T], WUKV[:, m * P:(m + 1) * P], CKV, start=True, stop=True)
            ins.then_inc(s.mla_ps, 1)
            for t in range(TT):
                ins = mm(BRB[:, t * T:(t + 1) * T], CKV[:, t * P:(t + 1) * P], WUKV[:, 256:512], start=True, stop=True)
            ins.then_inc(s.mla_ps, 1)
            pe.wait_ge(s.w_lo, 7)
            pe.wait_ge(s.fox_f, 1)
            for m in range(2):
                ins = project(6, PA[:, m * T:(m + 1) * T], m * 128, 256)
            ins.then_inc(s.unit_done, 1)
            pe.wait_ge(s.mla_evac, 1)
            mm(S1[:, 0:T], TABS[64:128, TAB["rep"][0]:TAB["rep"][1]], TMPB[64:128, T:2 * T], start=True, stop=True)\
                .then_inc(s.kpe_ps, 1)
            pe.wait_ge(s.fox_ready, 1)
            pe.wait_ge(s.ckv_ve, 1)
            pe.wait_ge(s.cq_ve, 1)
            tri0 = tri[:, 0:P]
            mm(MISC[:, 0:4], tri0, FLOG[:, 0, :], start=True, stop=True)
            mm(MISC[:, 4:8], ones_mat, FLOG[:, 0, :], start=True, stop=False)
            mm(MISC[:, 4:8], tri0, FLOG[:, 1, :], start=False, stop=True)
            mm(MISC[0:HEADS, T:T + P], FLOG[:, 0, :], tri0, start=True, stop=True)
            mm(MISC[0:HEADS, T + P:2 * T], FLOG[:, 0, :], ones_mat, start=True, stop=False)
            mm(MISC[0:HEADS, T + P:2 * T], FLOG[:, 1, :], tri0, start=False, stop=True)\
                .then_inc(s.fox_ps, 1)
            def layer_norm_sum(src, ready, done):
                pe.wait_ge(*ready)
                for j in range(2):
                    ins = mm(MISC[:, 0:T], ones_mat, src(j), start=(j == 0), stop=(j == 1))
                ins.then_inc(done, 1)

            for n in (7, 8, 9):
                if n == 9:
                    pe.wait_ge(s.cum_ready, 2)
                    layer_norm_sum(lambda j: CACC[:, j, :], (s.conv_out, 2), s.ln_sum)
                pe.wait_ge(s.w_lo, n + 1)
                pe.wait_ge(s.proj_evac, n - 6)
                b = (PA, PB)[n % 2] if n < 9 else PB
                if n < 9:
                    b = (PB, PA)[n % 2 == 0]
                    for m in range(2):
                        ins = project(n, b[:, m * T:(m + 1) * T], m * 128, 256)
                else:
                    ins = project_tokens(n, [PB[:, 0:T], PB[:, T:2 * T]], 256)
                ins.then_inc(s.unit_done, 1)

            def scores(p):
                b, hp = PAIRS[p]
                if p:
                    pe.wait_ge(s.logit_ready, 4 * p)
                else:
                    pe.wait_ge(s.kpe_ready, 1)
                    pe.wait_ge(s.mla_evac, 4)
                if b != 3:
                    pe.wait_ge(s.proj_evac, 2 if b == 1 else 5)
                if b == 1:
                    pe.wait_ge(s.cum_ready, 2)
                for qt in range(2):
                    n = P if qt == 0 else T
                    dst = (S0, S1)[qt][:, 0:2 * n]
                    q = slice(qt * P, (qt + 1) * P)
                    ins = mm(dst, Q[b][:, hp, q], KB[b][:, 2 * hp:2 * hp + 2, 0:n], start=True, stop=(b == 0))
                    if b == 3:
                        ins = mm(dst, QPE[:, q], KPE[:, 2 * hp:2 * hp + 2, 0:n], start=False, stop=True)
                    if b == 1:
                        ins = mm(dst, ones_mat[0:HEADS, :], CB[:, 2 * hp:2 * hp + 2, 0:n], start=False, stop=True)
                ins.then_inc(s.score_ps, 1)

            def attend(p):
                b, hp = PAIRS[p]
                V = VMAP[b]
                for h in range(2):
                    pe.wait_ge(s.prob_ready, 2 * p + h + 1)
                    if 2 * p + h:
                        pe.wait_ge(s.pt_sb, 2 * p + h)
                    for i in range(3):
                        ins = transpose(PT[:, i * P:(i + 1) * P], PR[:, h, i * P:(i + 1) * P])
                    ins.then_inc(s.pt_ps, 1)
                    if h == 0 and p:
                        pe.wait_ge(s.attn_ready, p)
                    pe.wait_ge(s.pt_sb, 2 * p + h + 1)
                    head = 2 * hp + h
                    r = slice(64 * h, 64 * h + 64)
                    vc = slice(head * HD, (head + 1) * HD)
                    mm(PV[r, 0:P], V[:, 0, vc], PTS[:, 0:P], start=True, stop=True)
                    mm(PV[r, P:T], V[:, 0, vc], PTS[:, P:T], start=True, stop=False)
                    mm(PV[r, P:T], V[:, 1, vc], PTS[:, T:384], start=False, stop=True).then_inc(s.pv_ps, 1)

            for g in range(NGATE):
                n = NIN + g
                if g % 2 == 0 and 0 < g // 2 <= len(PAIRS):
                    attend(g // 2 - 1)
                if g == 0:
                    layer_norm_sum(lambda j: TMPA[:, j * T:(j + 1) * T], (s.ln_sq, 1), s.ln_var)
                if g % 2 == 0 and g // 2 < len(PAIRS):
                    scores(g // 2)
                pe.wait_ge(s.w_lo, n + 1)
                if g >= 2:
                    pe.wait_ge(s.gate_t, 2 * (g - 1))
                else:
                    pe.wait_ge(s.proj_evac, 4 if g == 0 else 5)
                pg = (PA, PB)[g % 2]
                for m in range(2):
                    ins = project(n, pg[:, m * T:(m + 1) * T], m * 128, 256)
                ins.then_inc(s.gate_ps, 1)
                b = BRANCHES[g // 4]
                if g % 4 == 0:
                    if b == 2:
                        pe.wait_ge(s.yc_ready, 1)
                    else:
                        pe.wait_ge(s.attn_ready, {3: 2, 1: 4, 0: 6}[b])
                if g:
                    pe.wait_ge(s.tmp_mul, g)
                else:
                    pe.wait_ge(s.mla_evac, 4)
                wb = RAW[n % NRAW][:, 2048:2560].rearrange("p (j n) -> p j n", j=2)
                for m in range(2):
                    for j in range(2):
                        ins = mm(BRB[:, m * T:(m + 1) * T], wb[:, j, m * 128:(m + 1) * 128], YT[b][:, j, :],
                                 start=(j == 0), stop=(j == 1))
                ins.then_inc(s.unit_done, 1)
            pe.wait_ge(s.gate_t, 2 * NGATE)
            pe.wait_ge(s.tmp_mul, NGATE)
            for u in range(NOUT):
                n = NIN + NGATE + u
                pe.wait_ge(s.w_lo, n + 1)
                pe.wait_ge(s.merge_split, 2 * u + 2)
                for mm_ in range(2):
                    m = 2 * u + mm_
                    for t in range(TT):
                        xh, xl = act_tile(m, slice(t * P, (t + 1) * P))
                        for half in range(2):
                            c = slice(mm_ * D + half * 512, mm_ * D + half * 512 + 512)
                            dst = bank[2 * t + half][:, :]
                            mm(dst, xh, WH[:, n % 2, c], start=(m == 0), stop=False)
                            mm(dst, xl, WH[:, n % 2, c], start=False, stop=False)
                            ins = mm(dst, xh, WL[:, n % 2, c], start=False, stop=(m == KD - 1))
                ins.then_inc(s.unit_done, 1)
            pe.wait_ge(s.h_scaled, TT)
            pe.wait_ge(s.h_ready, 2 * TT)
            hs = HS.rearrange("p t (q k) -> p t q k", k=KD)
            for k in range(KD):
                for t in range(TT):
                    ins = transpose(bank[k // 2][:, (k % 2) * T + t * P:(k % 2) * T + (t + 1) * P], hs[:, t, :, k])
                if k % 2:
                    ins.then_inc(s.hst_ps, 1)
            pe.wait_ge(s.router_in, 32)
            for t in range(TT):
                for k in range(KD):
                    if t == 0:
                        pe.wait_ge(s.hst_sb, k + 1)
                    ins = mm(MISC[:, t * 36:(t + 1) * 36], M[:, k * T + t * P:k * T + (t + 1) * P], WR[:, k, :],
                             start=(k == 0), stop=(k == KD - 1))
            ins.then_inc(s.logits_ps, 1)
            pe.wait_ge(s.sel_ready, 1)
            o32 = RB_view(RB)
            mm(S0[:, 0:NE], tri0, o32[:, 0, :], start=True, stop=True)
            mm(S0[:, NE:2 * NE], ones_mat, o32[:, 0, :], start=True, stop=False)
            mm(S0[:, NE:2 * NE], tri0, o32[:, 1, :], start=False, stop=True)
            mm(S0[:, 2 * NE:3 * NE], ones_mat, o32[:, 0, :], start=True, stop=False)
            mm(S0[:, 2 * NE:3 * NE], ones_mat, o32[:, 1, :], start=False, stop=True).then_inc(s.rank_ps, 1)

            xe = M[:, :].rearrange("p (k c) -> p k c", k=KD)
            xh4 = XH[:, :].rearrange("p (t q k) -> p t q k", t=TT, k=KD)
            xl4 = XL[:, :].rearrange("p (t q k) -> p t q k", t=TT, k=KD)

            def gather_part(n, b):
                if b == 0:
                    after(pe, s.sel_chain, n * 2 + 2)
                    after(pe, s.hid_ps, n * 2)
                after(pe, s.xe_ready, n * 8 + 2 * b)
                for k in (2 * b, 2 * b + 1):
                    dst = bank[6][:, (k % 2) * T:(k % 2 + 1) * T]
                    for t in range(TT):
                        sel = SEL[:, t, :, :]
                        mm(dst, xh4[:, t, :, k], sel, start=(t == 0), stop=False)
                        ins = mm(dst, xl4[:, t, :, k], sel, start=False, stop=(t == TT - 1))
                ins.then_inc(s.gather_ps, 1)

            def select_t(n, pair):
                if pair == 0:
                    after(pe, s.over_sel, n * 2 + 2)
                after(pe, s.selt_sb, n * 2 + pair)
                if pair == 0:
                    after(pe, s.hidt_sb, n * 2)
                for t in range(TT):
                    ins = transpose(bank[7][:, t * P:(t + 1) * P],
                                    WSEL[:, t, 2 * pair:2 * pair + 2, :].rearrange("p e c -> p (e c)"))
                ins.then_inc(s.wselt_ps, 1)

            def hidden(n, pair, wait_slot):
                after(pe, s.xe_ready, n * 8 + 8)
                after(pe, s.hidt_sb, n * 2 + pair)
                for kind in range(2):
                    for e in range(2):
                        wait_slot(pair, kind, e)
                    for k in range(KD):
                        for e in range(2):
                            w = expert_slot(pair, kind, e)[:, k * FF:(k + 1) * FF]
                            x = xe[:, k, (2 * pair + e) * CAP:(2 * pair + e + 1) * CAP]
                            ins = mm(bank[pair][64 * e:64 * e + 64, kind * FF:(kind + 1) * FF], x, w,
                                     start=(k == 0), stop=(k == KD - 1), skip_group_check=True)
                ins.then_inc(s.hid_ps, 1)

            def hidden_t(n, pair):
                after(pe, s.hid_ready, n * 2 + pair + 1)
                after(pe, s.hidt_sb, n * 2 + pair)
                h2 = HT_[:, pair, :].rearrange("p (f j) -> p f j", j=2)
                for j in range(2):
                    ins = transpose(bank[7][:, T + j * P:T + (j + 1) * P], h2[:, :, j])
                ins.then_inc(s.hidt_ps, 1)

            def down(n, pair, half, wait_slot):
                if half == 0:
                    after(pe, s.hidt_sb, n * 2 + pair + 1)
                    for e in range(2):
                        wait_slot(pair, 2, e)
                after(pe, s.y_split, n * 4 + (half + 1 if pair else 0))
                for j in range(2):
                    for e in range(2):
                        w = expert_slot(pair, 2, e)[:, j * D + half * 512:j * D + half * 512 + 512]
                        ins = mm(bank[2 + half][64 * e:64 * e + 64, :], HTT[:, pair, j, 64 * e:64 * e + 64], w,
                                 start=(j == 0), stop=(j == 1), skip_group_check=True)
                ins.then_inc(s.y_ps, 1)

            def scatter(n):
                for t in range(TT):
                    for half in range(2):
                        i = 2 * t + half
                        after(pe, s.o_added, n * 4 + i - 1)
                        for pair in range(2):
                            after(pe, s.y_split, n * 4 + 2 * pair + half + 1)
                            lhs = SELT[:, pair, t * P:(t + 1) * P]
                            c = slice(half * 512, half * 512 + 512)
                            mm(bank[4 + half][:, :], lhs, WH[:, pair, c], start=(pair == 0), stop=False)
                            ins = mm(bank[4 + half][:, :], lhs, WL[:, pair, c], start=False, stop=(pair == 1))
                        ins.then_inc(s.o_ps, 1)

            def step(n, gather_next):
                def wait_slot(pair, kind, e):
                    pe.wait_ge(exp_in[slot_plan.index((pair, kind, e))], n * 16 + 16)

                select_t(n, 0)
                hidden(n, 0, wait_slot)
                select_t(n, 1)
                hidden_t(n, 0)
                hidden(n, 1, wait_slot)
                if gather_next:
                    gather_part(n + 1, 0)
                down(n, 0, 0, wait_slot)
                if gather_next:
                    gather_part(n + 1, 1)
                down(n, 0, 1, wait_slot)
                if gather_next:
                    gather_part(n + 1, 2)
                hidden_t(n, 1)
                if gather_next:
                    gather_part(n + 1, 3)
                down(n, 1, 0, wait_slot)
                down(n, 1, 1, wait_slot)
                scatter(n)

            pe.wait_ge(s.hs_split, TT)
            pe.wait_ge(s.over_ready, 1)
            for b in range(4):
                gather_part(0, b)
            step(0, True)
            with pe.Fori(1, NQ - 1) as i:
                step(i, True)
            step(NQ - 1, False)
            count = pe.value_load(LIST[0:1, 0:1], min_val=0, max_val=MAXOVER)
            with pe.If(count > 0):
                with pe.Fori(0, count) as j:
                    for b in range(4):
                        gather_part(j + NQ, b)
                    step(j + NQ, False)
            pe.end_ifs()


def RB_view(RB):
    at = 20 + 7 * 2 + 2 * 8 + 7 * 16 + 64
    return RB[:, at:at + 64].rearrange("p (t e) -> p t e", t=TT)


_INS = ["x", "norm1_g", "w_in", "b_forget", "conv_w", "conv_b", "conv_ln_g", "conv_ln_b", "mla_gq", "mla_wuq", "mla_gkv",
        "mla_wukv", "w_gate", "b_gate", "w_branch", "w_out", "norm2_g", "w_router_group", "b_router_group",
        "w_router_expert", "b_router_expert", "w_exp_gate", "w_exp_up", "w_exp_down", "final_g"]


def kernel(**inputs):
    import concourse.bacc as bacc
    from concourse.bass_utils import run_bass_kernel_spmd

    nc = bacc.Bacc("TRN2", target_bir_lowering=False, num_devices=1)
    arrays, aps = {}, {}
    for name in _INS:
        a = np.ascontiguousarray(inputs[name])
        arrays[f"in_{name}"] = a
        aps[name] = nc.dram_tensor(f"in_{name}", a.shape, mybir.dt.from_np(a.dtype), kind="ExternalInput").ap()
    arrays["in_tables"] = shape_tables()
    aps["tables"] = nc.dram_tensor("in_tables", (P, NTAB), F32, kind="ExternalInput").ap()
    out = nc.dram_tensor("out_y", (1, T, D), F32, kind="ExternalOutput").ap()
    trunk_kernel(nc, aps, out)
    r = run_bass_kernel_spmd(nc, [arrays], core_ids=[0])
    return r.results[0]["out_y"]
```

```python
from contextlib import ExitStack

import numpy as np

import concourse.bass as bass
from concourse import mybir

F32 = mybir.dt.float32
F32R = mybir.dt.float32r
I32 = mybir.dt.int32
ALU = mybir.AluOpType
ACT = mybir.ActivationFunctionType
AXX = mybir.AxisListType.X

P = 128
D = 1024
T = 256
TT = T // P
KD = D // P
HD = 64
HEADS = 4
NE = 32
EG = 8
NG = 4
FF = 256
CONV_K = 31
EPS = 1e-6
NEG = -1e30
CAP = 64
QUAD = 4
NQ = NE // QUAD
ROUNDS = T // CAP - 1
MAXOVER = 2 * T // (CAP + 1)
SLOT = 2 * D
RAWW = 10 * 256
NRAW = 3
PARTW = 4 * 260
NPART = 4

W_IN_UNITS = [("cq", 2052, 2308), ("ckv", 2308, 2468), ("fox_v", 1280, 1540), ("fox_q", 768, 1024),
              ("fox_k", 1024, 1280), ("conv_a", 1540, 1796), ("conv_g", 1796, 2052), ("moba_q", 0, 256),
              ("moba_k", 256, 512), ("moba_v", 512, 768)]
BRANCHES = [3, 1, 0, 2]
NIN = len(W_IN_UNITS)
NGATE = 4 * len(BRANCHES)
NOUT = 4
UNITS = NIN + NGATE + NOUT
PREFETCH_AT = NIN + 2
FIRST_SCORES = 6
CONV_FROM, CONV_TAPS = 8, 6
LN_AT = CONV_FROM + -(-2 * CONV_K // CONV_TAPS)

ROWS = {}
_r = 0
for _n, _c in (("conv_w", 2 * CONV_K), ("conv_b", 2), ("ln_g", 2), ("ln_b", 2), ("gq", 2), ("gkv", 1), ("b_gate", 32)):
    ROWS[_n] = _r
    _r += _c
NROWS = _r

TAB = {}
_r = 0
for _n, _c in (("ident", P), ("dist", 384), ("mask", 384), ("tri", 256), ("cos", T), ("sin", T), ("kcs", T),
               ("rep", P), ("iota", CAP), ("code", 2 * ROUNDS * NQ)):
    TAB[_n] = (_r, _r + _c)
    _r += _c
NTAB = _r


def shape_tables():
    t = np.zeros((P, NTAB), np.float32)

    def put(name, a):
        t[:, TAB[name][0]:TAB[name][1]] = a

    p = np.arange(P)[:, None]
    put("ident", np.eye(P))
    q = np.concatenate([np.broadcast_to(p, (P, P)), np.broadcast_to(p + P, (P, T))], 1)
    s = np.concatenate([np.arange(P), np.arange(T)])[None, :]
    put("dist", np.where(q >= s, -(q - s), NEG))
    put("mask", np.where(q >= s, 0.0, NEG))
    put("tri", np.arange(T)[None, :] >= p)
    inv = (np.float32(10000.0) ** (-np.arange(0, 32, 2, dtype=np.float32) / np.float32(32))).astype(np.float32)
    ang = (np.arange(T, dtype=np.float32)[:, None] * inv[None, :]).astype(np.float32)
    cos, sin = np.cos(ang).T, np.sin(ang).T
    cos32, sin32 = np.concatenate([cos, cos]), np.concatenate([-sin, sin])
    put("cos", np.tile(cos32, (4, 1)))
    put("sin", np.tile(sin32, (4, 1)))
    put("kcs", np.concatenate([cos32, sin32, cos32, sin32]))
    put("rep", (p % 32) == (np.arange(P) % 32)[None, :])
    put("iota", np.arange(CAP))
    r, qd = np.divmod(np.arange(ROUNDS * NQ), NQ)
    put("code", np.concatenate([(r + 1) * NE + qd * QUAD, qd]))
    return t


def after(engine, semaphore, value):
    if not isinstance(value, int) or value > 0:
        engine.wait_ge(semaphore, value)


def trunk_kernel(nc, A, out):
    ctx = ExitStack()
    with ctx:
        def sb(name, shape, dt=F32):
            return ctx.enter_context(nc.sbuf_tensor(name, shape, dt))

        names = """params_in ident_in tables_in norm_in wmla_in bias_in router_in final_in
            sumsq xvar xroot xscaled params_ps params_sb half_params xt_ps x_hi x_split
            w_hi w_lo part_done proj_evac branch_ps
            conv_t conv_u conv_acc conv_out ln_sum ln_cent ln_sq ln_var ln_ve ln_root ln_rec ln_z ln_t yc_ready
            cq_sb cq_sq cq_sum cq_ve cq_root cq_rec cq_ready
            ckv_sb ckv_sq ckv_sum ckv_ve ckv_root ckv_rec ckv_ready krope_sb kpe_ps kpe_ready
            wrot_ready zeros_ready mla_ps mla_evac rope_mul
            fox_f fox_exp fox_ln fox_ready fox_ps cum_ready
            score_ps conv_a_sb logit_ready row_max neg_max prob_exp row_sum prob_ready pt_ps pt_sb pv_ps attn_ready
            gate_t merged tmp_mul merge_hi merge_split
            h_ready h_sq h_var h_root h_scaled hs_hi hs_split hst_ps hst_sb logits_ps router_exp
            rank_ps sel_ready gather_ps xe_ready over_ready over_ps
            wselt_ps selt_sb gates_ps hid_ps hid_t hid_ready hidt_ps hidt_sb y_ps y_hi y_split o_ps o_free
            final_sq final_var final_root out_ready stored router_chain sel_chain step_chain x_chain over_chain
            slot_weight wsel_ready""".split()
        s = type("Semaphores", (), {n: ctx.enter_context(nc.semaphore(n)) for n in names})
        raw_in = [ctx.enter_context(nc.semaphore(f"raw_in{i}")) for i in range(NRAW)]
        x_tile_in = [ctx.enter_context(nc.semaphore(f"x_tile_in{i}")) for i in range(TT)]
        exp_in = [ctx.enter_context(nc.semaphore(f"exp_in{i}")) for i in range(12)]

        EX = sb("expert_slots", [P, 12 * SLOT])
        mixer_area = 6 * SLOT

        def ex(slot):
            return EX[:, slot * SLOT:(slot + 1) * SLOT]

        def area(at, n):
            return EX[:, mixer_area + at:mixer_area + at + n]

        RAW = [area(i * RAWW, RAWW) for i in range(NRAW)]
        kb_at = NRAW * RAWW
        KB = {b: area(kb_at + i * 1024, 1024).rearrange("p (h t) -> p h t", h=HEADS) for i, b in enumerate((3, 1, 0))}
        KPE = area(kb_at + 3072, 1024).rearrange("p (h t) -> p h t", h=HEADS)
        VMLA = area(kb_at + 4096, 512).rearrange("p (t c) -> p t c", t=TT)
        HS = EX[:, 10 * SLOT:11 * SLOT].rearrange("p (t d) -> p t d", t=TT)

        XH = sb("act_hi", [P, KD * T], F32R)
        XL = sb("act_lo", [P, KD * T], F32R)
        WH = sb("w_high", [P, NPART * PARTW], F32R)
        WL = sb("w_low", [P, NPART * PARTW], F32R)
        H = sb("residual", [P, TT, D])
        M = sb("merged_t", [P, KD * T])
        SEL = sb("select", [P, TT, QUAD, CAP], F32R)
        SELT = sb("select_t", [P, 2, T], F32R)
        TABS = sb("shape_tables", [P, NTAB])
        VEC = sb("vectors", [P, 272])
        SCR_N = 8900 - 384
        SCR = sb("scratch", [P, SCR_N])

        def tab(name):
            return TABS[:, TAB[name][0]:TAB[name][1]]

        ident = tab("ident")
        LNV = tab("cos")
        ones_mat = TABS[:, TAB["tri"][0] + P:TAB["tri"][0] + 2 * P]
        tri = tab("tri")

        def carver(area_ap, size):
            used = [0]

            def carve(n, start=None):
                if start is not None:
                    used[0] = start
                a = area_ap[:, used[0]:used[0] + n]
                used[0] += n
                assert used[0] <= size, used[0]
                return a
            return carve

        mx = carver(SCR[:, :], SCR_N)
        Q = {b: mx(512).rearrange("p (j t) -> p j t", j=2) for b in (3, 1, 0)}
        QPE = mx(T)
        VF = mx(2 * 260).rearrange("p (t c) -> p t c", t=TT)
        UPAD = mx(2 * 286).rearrange("p (j t) -> p j t", j=2)
        CACC = mx(512).rearrange("p (j t) -> p j t", j=2)
        YT = {b: mx(512).rearrange("p (j t) -> p j t", j=2) for b in (1, 3)}
        YT[2] = CACC
        YT[0] = Q[3]
        CQV = mx(512)
        CQ = CQV.rearrange("p (j t) -> p j t", j=2)
        VM = CQV.rearrange("p (t c) -> p t c", t=TT)
        PTS = mx(384)
        TMPA = mx(512)
        TMPB = mx(512)
        CBW = mx(1024)
        WUKV = CBW[:, 0:512]
        WROT = CBW[:, 512:768].rearrange("p (j h c) -> p j h c", j=2, h=HEADS)
        CKV = CBW[:, 768:1024]
        CB = CBW[0:HEADS, :].rearrange("p (h t) -> p h t", h=HEADS)
        PTS2 = mx(384)
        ROWP = PTS[:, 0:P]
        PRB = mx(768)
        PR = PRB.rearrange("p (h c) -> p h c", h=2)
        LNT = PRB[:, 0:512]
        WUQ = PRB.rearrange("p (j n) -> p j n", j=2)
        VMAP = {3: VMLA, 1: VF, 0: VM}

        mo = carver(SCR[:, :], SCR_N)
        WSEL = mo(512).rearrange("p (t e c) -> p t e c", t=TT, e=QUAD)
        HT_ = mo(512).rearrange("p (a f) -> p a f", a=2)
        TH = mo(512).rearrange("p (a f) -> p a f", a=2)
        HTT = mo(512).rearrange("p (a j c) -> p a j c", a=2, j=2)
        FG = mo(D)
        WR = mo(KD * 36).rearrange("p (k n) -> p k n", k=KD)
        LG = mo(72).rearrange("p (t n) -> p t n", t=TT)
        RB = mo(800)
        RANK = mo(TT * (ROUNDS + 1) * NE).rearrange("p (t r) -> p t r", t=TT)
        WT = mo(TT * NE).rearrange("p (t e) -> p t e", t=TT)
        OV = mo(700)
        YOUT = mo(2 * D).rearrange("p (t d) -> p t d", t=TT)

        vv = carver(VEC[:, :], 272)
        PAR = vv(NROWS)
        HPAR = vv(4)
        G1 = vv(KD)
        G2 = vv(KD)
        BF = vv(HEADS)
        BR = vv(36)
        SS = vv(2)
        RS = vv(2)
        FW = vv(4 * 8)
        FLOG = vv(8).rearrange("p (t h) -> p t h", t=TT)
        CTOK = vv(8).rearrange("p (t h) -> p t h", t=TT)
        MAXV = vv(4)
        NMAX = vv(4)
        SUMV = vv(4)
        RECV = vv(4)
        WS = vv(2)
        HGB = vv(32)
        LIST = sb("overflow_list", [1, 24], I32)

        def par(name, i=0):
            c = ROWS[name] + i
            return PAR[:, c:c + 1]

        bank = [ctx.enter_context(nc.psum_tensor(f"bank{i}", [P, 512], F32)) for i in range(8)]
        PA, PB, BRB, S0, S1, PT, PV, MISC = bank

        x_v = A["x"][0].rearrange("(t p) d -> p t d", p=P)
        out_v = out[0].rearrange("(t p) d -> p t d", p=P)
        w_in_v = A["w_in"][0].rearrange("(p k) n -> p k n", k=KD)
        w_out_v = A["w_out"][0].rearrange("(m p) n -> p m n", p=P)
        e_gate = A["w_exp_gate"][0].rearrange("e (p k) f -> e p (k f)", k=KD)
        e_up = A["w_exp_up"][0].rearrange("e (p k) f -> e p (k f)", k=KD)
        e_down = A["w_exp_down"][0].rearrange("e (p j) d -> e p (j d)", j=2)

        def unit_dmas(n):
            raw = RAW[n % NRAW]
            if n < NIN:
                _, a, b = W_IN_UNITS[n]
                return [(raw[:, 0:8 * (b - a)].rearrange("p (k n) -> p k n", k=8), w_in_v[:, :, a:b])]
            if n < NIN + NGATE:
                g = n - NIN
                i, u = BRANCHES[g // 4], g % 4
                cols = slice(u * 256, u * 256 + 256)
                return [(raw[:, 0:2048].rearrange("p (k n) -> p k n", k=8),
                         A["w_gate"][0, i].rearrange("(p k) n -> p k n", k=8)[:, :, cols]),
                        (raw[:, 2048:2560].rearrange("p (j n) -> p j n", j=2),
                         A["w_branch"][0, i].rearrange("(j p) n -> p j n", p=P)[:, :, cols])]
            u = n - NIN - NGATE
            return [(raw[:, 0:2048].rearrange("p (m n) -> p m n", m=2), w_out_v[:, 2 * u:2 * u + 2, :])]

        def raw_count(n):
            return sum(16 * (2 if NIN <= m < NIN + NGATE else 1) for m in range(n % NRAW, n + 1, NRAW))

        def part(w, q, cols=slice(0, 1024)):
            at = (q % NPART) * PARTW
            return w[:, at + cols.start:at + cols.stop]

        def part_copies(q):
            n, h = divmod(q, 2)
            raw = RAW[n % NRAW]
            if n >= NIN + NGATE:
                return [((0, 1024, None), raw[:, h * 1024:(h + 1) * 1024])]
            if n < NIN and W_IN_UNITS[n][0].endswith("_v"):
                w = 4 * (W_IN_UNITS[n][2] - W_IN_UNITS[n][1])
                return [((0, w, None), raw[:, h * w:(h + 1) * w])]
            if n < NIN and W_IN_UNITS[n][0] == "ckv":
                r = raw[:, 0:8 * 160].rearrange("p (k n) -> p k n", k=8)
                if h == 0:
                    return [((0, 128, 8), r[:, :, 0:128])]
                return [((0, 64, 8), r[:, :, 0:64]), ((64, 96, 8), r[:, :, 128:160]), ((96, 112, 8), r[:, :, 144:160]),
                        ((112, 128, 8), r[:, :, 128:144])]
            r = raw[:, 0:2048].rearrange("p (k n) -> p k n", k=8)
            return [((0, 128, 8), r[:, :, h * 128:(h + 1) * 128])]

        def part_slice(w, q, where):
            a, b, k = where
            if k is None:
                return part(w, q, slice(a, b))
            return part(w, q).rearrange("p (k n) -> p k n", k=k)[:, :, a:b]

        slot_plan = [(pair, kind, e) for pair, kind in ((0, 0), (0, 1), (1, 0), (1, 1), (0, 2), (1, 2)) for e in range(2)]

        def expert_slot(pair, kind, e):
            return ex(slot_plan.index((pair, kind, e)))

        def y_part(w, pair, half):
            at = pair * D + half * 512
            return w[:, at:at + 512]

        PAIRS = [(3, 0), (3, 1), (1, 0), (1, 1), (0, 0), (0, 1)]

        block = ctx.enter_context(nc.Block())

        @block.sync
        def _(sp):
            for t in range(TT):
                sp.dma_start(H[:, t, :], x_v[:, t, :]).then_inc(x_tile_in[t], 16)

            def load_unit(n):
                if n >= NRAW:
                    m = n - NRAW
                    sp.wait_ge(s.w_lo, 2 * m + 2)
                    if NIN <= m < NIN + NGATE:
                        sp.wait_ge(s.branch_ps, m - NIN + 1)
                for dst, src in unit_dmas(n):
                    sp.dma_start(dst, src).then_inc(raw_in[n % NRAW], 16)

            def load_expert(slot, q):
                pair, kind, e = slot_plan[slot]
                src = (e_gate, e_up, e_down)[kind]
                sp.dma_start(ex(slot), src[q * QUAD + 2 * pair + e]).then_inc(exp_in[slot], 16)

            for n in range(UNITS):
                load_unit(n)
                if n == PREFETCH_AT:
                    for slot in range(6):
                        load_expert(slot, 0)
            sp.wait_ge(s.w_lo, 2 * UNITS)
            for slot in range(6, 10):
                load_expert(slot, 0)
            sp.wait_ge(s.hs_split, TT)
            sp.wait_ge(s.hst_ps, 4)
            for slot in range(10, 12):
                load_expert(slot, 0)

            def free_slot(slot, n):
                pair, kind, _ = slot_plan[slot]
                if kind < 2:
                    after(sp, (s.gates_ps, s.hid_ps)[kind], n * 2 - 1 + pair)
                else:
                    after(sp, s.y_ps, n * 4 - 2 + 2 * pair)

            with sp.Fori(1, NQ) as i:
                for slot in range(12):
                    if slot_plan[slot][2] == 0:
                        free_slot(slot, i)
                    load_expert(slot, i)
            sp.wait_ge(s.over_ready, 1)
            count = sp.value_load(LIST[0:1, 0:1], min_val=0, max_val=MAXOVER)
            with sp.If(count > 0):
                with sp.Fori(0, count) as j:
                    q = sp.value_load(LIST[0:1, bass.ds(j + 9, 1)], min_val=0, max_val=NQ - 1)
                    for slot in range(12):
                        if slot_plan[slot][2] == 0:
                            free_slot(slot, j + NQ)
                        load_expert(slot, q)
            sp.end_ifs()
            for t in range(TT):
                sp.wait_ge(s.out_ready, t + 1)
                sp.dma_start(out_v[:, t, :], YOUT[:, t, :]).then_inc(s.stored, 16)
            sp.wait_ge(s.stored, 16 * TT)

        @block.gpsimd
        def _(pool):
            for b in (3, 1, 0):
                nc.gpsimd.memset(KB[b], 0.0).then_inc(s.zeros_ready, 1)
            nc.gpsimd.memset(KPE, 0.0).then_inc(s.zeros_ready, 1)
            nc.gpsimd.memset(UPAD[:, :, 0:30], 0.0).then_inc(s.zeros_ready, 1)
            pool.wait_ge(s.wmla_in, 96)
            wq = WUQ[:, :, 256:384].rearrange("p j (h c) -> p j h c", h=HEADS)
            for j in range(2):
                nc.gpsimd.tensor_copy(WROT[:, j, :, 0:16], wq[:, j, :, 16:32]).then_inc(s.wrot_ready, 1)
                nc.gpsimd.tensor_copy(WROT[:, j, :, 16:32], wq[:, j, :, 0:16]).then_inc(s.wrot_ready, 1)

        @block.scalar
        def _(act):
            def rows(name):
                return ROWP[ROWS[name]:ROWS[name] + {"conv_w": 62, "b_gate": 32, "gkv": 1}.get(name, 2), :]

            act.dma_start(ident, A["tables"][:, 0:P]).then_inc(s.ident_in, 16)
            act.dma_start(G1, A["norm1_g"][0].rearrange("(p k) -> p k", k=KD)).then_inc(s.norm_in, 16)
            act.dma_start(rows("conv_w"), A["conv_w"][0].rearrange("k (j p) -> (k j) p", p=P)).then_inc(s.params_in, 16)
            for name, key in (("conv_b", "conv_b"), ("ln_g", "conv_ln_g"), ("ln_b", "conv_ln_b"), ("gq", "mla_gq"),
                              ("gkv", "mla_gkv")):
                act.dma_start(rows(name), A[key][0].rearrange("(j p) -> j p", p=P)).then_inc(s.params_in, 16)
            act.dma_start(rows("b_gate"), A["b_gate"][0].rearrange("i (m p) -> (i m) p", p=P)).then_inc(s.params_in, 16)
            act.dma_start(TABS[:, P:NTAB], A["tables"][:, P:NTAB]).then_inc(s.tables_in, 16)
            act.dma_start(G2, A["norm2_g"][0].rearrange("(p k) -> p k", k=KD)).then_inc(s.norm_in, 16)
            for j in range(2):
                wuq = A["mla_wuq"][0, j * P:(j + 1) * P, :].rearrange("p (h c) -> p h c", h=HEADS)
                act.dma_start(WUQ[:, j, 0:256].rearrange("p (h c) -> p h c", h=HEADS), wuq[:, :, 0:64]).then_inc(s.wmla_in, 16)
                act.dma_start(WUQ[:, j, 256:384].rearrange("p (h c) -> p h c", h=HEADS), wuq[:, :, 64:96]).then_inc(s.wmla_in, 16)
            wukv = A["mla_wukv"][0].rearrange("p (h a c) -> p h a c", h=HEADS, a=2)
            for a in range(2):
                act.dma_start(WUKV[:, a * 256:(a + 1) * 256].rearrange("p (h c) -> p h c", h=HEADS), wukv[:, :, a, :])\
                    .then_inc(s.wmla_in, 16)
            act.dma_start(BF, A["b_forget"][0].partition_broadcast(P)).then_inc(s.bias_in, 16)
            act.dma_start(BR[:, 0:4], A["b_router_group"][0].partition_broadcast(P)).then_inc(s.bias_in, 16)
            act.dma_start(BR[:, 4:36], A["b_router_expert"][0].partition_broadcast(P)).then_inc(s.bias_in, 16)

            for t in range(TT):
                act.wait_ge(x_tile_in[t], 16)
                nc.scalar.activation(M[:, t * D:(t + 1) * D], H[:, t, :], ACT.Square, accum_out=SS[:, t:t + 1]).then_inc(s.sumsq, 1)
            act.wait_ge(s.xvar, 1)
            nc.scalar.activation(RS, SS, ACT.Sqrt).then_inc(s.xroot, 1)
            act.wait_ge(s.norm_in, 32)
            for b in range(4):
                act.wait_ge(s.xt_ps, b + 1)
                for k in (2 * b, 2 * b + 1):
                    nc.scalar.activation(XH[:, k * T:(k + 1) * T], bank[b][:, (k % 2) * T:(k % 2 + 1) * T], ACT.Copy,
                                         scale=G1[:, k:k + 1]).then_inc(s.x_hi, 1)

            def split_hi(q):
                n = q // 2
                act.wait_ge(raw_in[n % NRAW], raw_count(n))
                if q >= NPART:
                    act.wait_ge(s.part_done, q - NPART + 1)
                    act.wait_ge(s.w_lo, q - NPART + 1)
                for where, raw in part_copies(q):
                    ins = nc.scalar.activation(part_slice(WH, q, where), raw, ACT.Copy)
                ins.then_inc(s.w_hi, 1)

            def flat(ap):
                return ap.rearrange("p j t -> p (j t)")

            def exp_pair(p):
                b = PAIRS[p][0]
                scale = (96.0 if b == 3 else 64.0) ** -0.5
                act.wait_ge(s.neg_max, p + 1)
                for h in range(2):
                    for qt in range(2):
                        c = slice(0, P) if qt == 0 else slice(P, 384)
                        i = 2 * h + qt
                        nc.scalar.activation(PR[:, h, c], PR[:, h, c], ACT.Exp, bias=NMAX[:, i:i + 1], scale=scale,
                                             accum_out=SUMV[:, i:i + 1]).then_inc(s.prob_exp, 1)

            def attend(p):
                b, hp = PAIRS[p]
                for h in range(2):
                    act.wait_ge(s.pt_ps, 2 * p + h + 1)
                    if p:
                        act.wait_ge(s.pv_ps, 2 * p - 1 + h)
                    nc.scalar.activation((PTS, PTS2)[h], (PT, MISC)[h][:, 0:384], ACT.Copy).then_inc(s.pt_sb, 1)
                act.wait_ge(s.pv_ps, 2 * p + 2)
                nc.scalar.activation(YT[b][:, hp, :], PV[:, 0:T], ACT.Copy).then_inc(s.attn_ready, 1)

            def projection(n):
                kind = W_IN_UNITS[n][0]
                pb = (PA, PB)[n % 2]
                b = 1 if kind.startswith("fox") else 0
                act.wait_ge(s.part_done, 2 * n + 2)
                if kind.endswith("q"):
                    nc.scalar.activation(flat(Q[b]), pb[:, :], ACT.Copy).then_inc(s.proj_evac, 1)
                else:
                    act.wait_ge(s.zeros_ready, 5)
                    for h in range(HEADS):
                        r = slice(64 * (h % 2), 64 * (h % 2) + 64)
                        ins = nc.scalar.activation(KB[b][r, h, :], pb[r, (h // 2) * T:(h // 2 + 1) * T], ACT.Copy)
                    ins.then_inc(s.proj_evac, 1)

            split_hi(0)
            split_hi(1)
            for n in range(NIN + NGATE + 1):
                if n < NIN + NGATE:
                    split_hi(2 * n + 2)
                if n == 1:
                    act.wait_ge(s.part_done, 2)
                    nc.scalar.activation(flat(CQ), PA[:, :], ACT.Copy).then_inc(s.cq_sb, 1)
                    nc.scalar.activation(TMPA, PA[:, :], ACT.Square).then_inc(s.cq_sq, 1)
                if n == 2:
                    act.wait_ge(s.part_done, 4)
                    nc.scalar.activation(CKV, PB[:, 0:T], ACT.Copy).then_inc(s.ckv_sb, 1)
                    nc.scalar.activation(TMPB[:, 0:T], PB[:, 0:T], ACT.Square).then_inc(s.ckv_sq, 1)
                if n == 3:
                    act.wait_ge(s.cq_ve, 1)
                    nc.scalar.activation(TMPA[:, 0:T], TMPA[:, 0:T], ACT.Sqrt).then_inc(s.cq_root, 1)
                    act.wait_ge(s.ckv_ve, 1)
                    nc.scalar.activation(TMPB[:, 0:T], TMPB[:, 0:T], ACT.Sqrt).then_inc(s.ckv_root, 1)
                    act.wait_ge(s.fox_f, 1)
                    nc.scalar.activation(FW[:, 16:24], FW[:, 8:16], ACT.Exp, scale=-1.0).then_inc(s.fox_exp, 1)
                    act.wait_ge(s.fox_exp, 1)
                    nc.scalar.activation(FW[:, 24:32], FW[:, 16:24], ACT.Ln, bias=1.0).then_inc(s.fox_ln, 1)
                if n in (4, 5, 8, 9):
                    projection(n - 1)
                if n == 6:
                    act.wait_ge(s.part_done, 12)
                    act.wait_ge(s.kpe_ps, 1)
                    nc.scalar.activation(TMPB, PB[:, :], ACT.Copy).then_inc(s.conv_a_sb, 1)
                if n == 7:
                    act.wait_ge(s.part_done, 14)
                    act.wait_ge(s.mla_evac, 2)
                    nc.scalar.activation(TMPA, PA[:, :], ACT.Tanh, scale=0.5).then_inc(s.conv_t, 1)
                if n == 10:
                    act.wait_ge(s.part_done, 20)
                    nc.scalar.activation(VM[:, 0, :], PB[:, 0:T], ACT.Copy)
                    nc.scalar.activation(VM[:, 1, :], MISC[:, 0:T], ACT.Copy).then_inc(s.proj_evac, 1)
                if n < NIN + NGATE:
                    split_hi(2 * n + 3)
                p = (n - FIRST_SCORES) // 2
                if (n - FIRST_SCORES) % 2 == 0:
                    if 1 <= p <= len(PAIRS):
                        attend(p - 1)
                    if 0 <= p < len(PAIRS):
                        exp_pair(p)
                g = n - 1 - NIN
                if g >= 0:
                    act.wait_ge(s.part_done, 2 * (NIN + g) + 2)
                    if g >= 1:
                        act.wait_ge(s.tmp_mul, g)
                    i, u = BRANCHES[g // 4], g % 4
                    for m in range(2):
                        c = i * 8 + u * 2 + m
                        nc.scalar.activation(TMPB[:, m * T:(m + 1) * T], (PA, PB)[g % 2][:, m * T:(m + 1) * T], ACT.Tanh,
                                             bias=HGB[:, c:c + 1], scale=0.5).then_inc(s.gate_t, 1)
                if n == LN_AT + 1:
                    act.wait_ge(s.ln_cent, 1)
                    nc.scalar.activation(LNT, flat(CACC), ACT.Square).then_inc(s.ln_sq, 1)
                if n == LN_AT + 2:
                    act.wait_ge(s.ln_ve, 1)
                    nc.scalar.activation(LNV, LNV, ACT.Sqrt).then_inc(s.ln_root, 1)
                    act.wait_ge(s.ln_z, 1)
                    nc.scalar.activation(LNT, flat(CACC), ACT.Tanh).then_inc(s.ln_t, 1)
            act.wait_ge(s.part_done, 2 * (NIN + NGATE))
            act.wait_ge(s.merged, NGATE - 4)
            for m in range(KD):
                nc.scalar.activation(XH[:, m * T:(m + 1) * T], M[:, m * T:(m + 1) * T], ACT.Copy, scale=0.5)\
                    .then_inc(s.merge_hi, 1)
                if m % 2:
                    split_hi(2 * (NIN + NGATE) + 2 + m // 2)
            for q in range(2 * (NIN + NGATE) + 6, 2 * UNITS):
                split_hi(q)
            act.wait_ge(s.h_ready, 2 * TT)
            wr = WR
            act.dma_start(wr[:, :, 0:NG], A["w_router_group"][0].rearrange("(p k) n -> p k n", k=KD)).then_inc(s.router_in, 16)
            act.dma_start(wr[:, :, NG:36], A["w_router_expert"][0].rearrange("(p k) n -> p k n", k=KD)).then_inc(s.router_in, 16)
            act.dma_start(FG, A["final_g"].partition_broadcast(P)).then_inc(s.final_in, 16)
            for t in range(TT):
                nc.scalar.activation(M[:, t * D:(t + 1) * D], H[:, t, :], ACT.Square, accum_out=SS[:, t:t + 1])\
                    .then_inc(s.h_sq, 1)
            act.wait_ge(s.h_var, 1)
            nc.scalar.activation(RS, SS, ACT.Sqrt).then_inc(s.h_root, 1)
            for t in range(TT):
                act.wait_ge(s.h_scaled, t + 1)
                nc.scalar.activation(XH[:, t * D:(t + 1) * D], HS[:, t, :], ACT.Copy).then_inc(s.hs_hi, 1)
            act.wait_ge(s.router_exp, 1)
            nc.scalar.activation(RB[:, 8:16], RB[:, 0:8], ACT.Exp).then_inc(s.router_exp, 1)
            act.wait_ge(s.router_exp, 3)
            nc.scalar.activation(RB[:, 18:20], RB[:, 16:18], ACT.Exp).then_inc(s.router_exp, 1)

            def step(n):
                for pair in range(2):
                    after(act, s.hid_ps, n * 2 + pair + 1)
                    after(act, s.hid_ready, n * 2 + pair)
                    nc.scalar.activation(TH[:, pair, :], bank[0 + pair][:, 0:FF], ACT.Tanh, scale=0.5)\
                        .then_inc(s.hid_t, 1)
                for pair in range(2):
                    for half in range(2):
                        after(act, s.y_ps, n * 4 + 2 * pair + half + 1)
                        after(act, s.o_ps, n * 4)
                        after(act, s.selt_sb, n * 2 + pair + 1)
                        nc.scalar.activation(y_part(WH, pair, half), bank[2 + half][:, :], ACT.Copy,
                                             scale=WS[:, pair:pair + 1]).then_inc(s.y_hi, 1)

            step(0)
            with act.Fori(1, NQ) as i:
                step(i)
            act.wait_ge(s.over_ready, 1)
            count = act.value_load(LIST[0:1, 0:1], min_val=0, max_val=MAXOVER)
            with act.If(count > 0):
                with act.Fori(0, count) as j:
                    step(j + NQ)
            act.end_ifs()
            act.wait_ge(s.final_sq, 1)
            for t in range(TT):
                nc.scalar.activation(YOUT[:, t, :], H[:, t, :], ACT.Square, accum_out=SS[:, t:t + 1])\
                    .then_inc(s.final_sq, 1)
            act.wait_ge(s.final_var, 1)
            nc.scalar.activation(RS, SS, ACT.Sqrt).then_inc(s.final_root, 1)

        @block.vector
        def _(dve):
            V = nc.vector
            chain = [0]

            def link(ins):
                chain[0] += 1
                ins.then_inc(s.x_chain, 1)
                dve.wait_ge(s.x_chain, chain[0])

            f32 = lambda ap: ap.bitcast(F32)

            dve.wait_ge(s.sumsq, TT)
            V.tensor_scalar(SS, SS, 1.0 / D, EPS, ALU.mult, ALU.add).then_inc(s.xvar, 1)
            dve.wait_ge(s.xroot, 1)
            link(V.reciprocal(RS, RS))
            for t in range(TT):
                V.tensor_scalar(M[:, t * D:(t + 1) * D], H[:, t, :], RS[:, t:t + 1], None, ALU.mult).then_inc(s.xscaled, 1)
            for k in range(KD):
                dve.wait_ge(s.x_hi, 2 * (k // 2) + 2)
                V.scalar_tensor_tensor(XL[:, k * T:(k + 1) * T], bank[k // 2][:, (k % 2) * T:(k % 2 + 1) * T],
                                       G1[:, k:k + 1], f32(XH[:, k * T:(k + 1) * T]), ALU.mult, ALU.subtract)\
                    .then_inc(s.x_split, 1)

            def split_lo(q):
                dve.wait_ge(s.w_hi, q + 1)
                for where, raw in part_copies(q):
                    ins = V.tensor_tensor(part_slice(WL, q, where), raw, f32(part_slice(WH, q, where)), ALU.subtract)
                ins.then_inc(s.w_lo, 1)

            steps = [0]

            def conv_steps(count):
                for _ in range(count):
                    k, j = divmod(steps[0], 2)
                    if k >= CONV_K:
                        return
                    if steps[0] >= 2:
                        dve.wait_ge(s.conv_acc, steps[0] - 1)
                    w = PAR[:, ROWS["conv_w"] + 2 * k + j:ROWS["conv_w"] + 2 * k + j + 1]
                    src = UPAD[:, j, k:k + T]
                    if k == 0:
                        ins = V.tensor_scalar(CACC[:, j, :], src, w, None, ALU.mult)
                    else:
                        ins = V.scalar_tensor_tensor(CACC[:, j, :], src, w, CACC[:, j, :], ALU.mult, ALU.add)
                    ins.then_inc(s.conv_acc, 1)
                    steps[0] += 1

            def logits(p):
                b, hp = PAIRS[p]
                scale = (96.0 if b == 3 else 64.0) ** -0.5
                dve.wait_ge(s.score_ps, p + 1)
                if p:
                    dve.wait_ge(s.pt_ps, 2 * p)
                else:
                    dve.wait_ge(s.mla_ps, 4)
                for qt in range(2):
                    for h in range(2):
                        c = slice(0, P) if qt == 0 else slice(P, 384)
                        n = P if qt == 0 else T
                        sc = (S0, S1)[qt][:, h * n:(h + 1) * n]
                        head = 2 * hp + h
                        if b == 0:
                            slope = 2.0 ** (-8.0 * (head + 1) / HEADS)
                            V.scalar_tensor_tensor(PR[:, h, c], tab("dist")[:, c], slope / scale, sc, ALU.mult, ALU.add)\
                                .then_inc(s.logit_ready, 1)
                        elif b == 1:
                            V.scalar_tensor_tensor(PR[:, h, c], sc, CTOK[:, qt, head:head + 1], tab("mask")[:, c],
                                                   ALU.add, ALU.add).then_inc(s.logit_ready, 1)
                        else:
                            V.tensor_tensor(PR[:, h, c], sc, tab("mask")[:, c], ALU.add).then_inc(s.logit_ready, 1)
                mv = MAXV.rearrange("p (h q) -> p h q", h=2)
                for qt in range(2):
                    dve.wait_ge(s.logit_ready, 4 * p + 2 * qt + 2)
                    c = slice(0, P) if qt == 0 else slice(P, 384)
                    V.reduce_max(mv[:, :, qt:qt + 1], PR[:, :, c], AXX).then_inc(s.row_max, 1)
                dve.wait_ge(s.row_max, 2 * p + 2)
                V.tensor_scalar(NMAX, MAXV, -scale, None, ALU.mult).then_inc(s.neg_max, 1)

            def normalise(p):
                dve.wait_ge(s.prob_exp, 4 * p + 4)
                link(V.reciprocal(RECV, SUMV))
                for h in range(2):
                    for qt in range(2):
                        c = slice(0, P) if qt == 0 else slice(P, 384)
                        i = 2 * h + qt
                        ins = V.tensor_scalar(PR[:, h, c], PR[:, h, c], RECV[:, i:i + 1], None, ALU.mult)
                    ins.then_inc(s.prob_ready, 1)

            def merge(g):
                dve.wait_ge(s.gate_t, 2 * g + 2)
                dve.wait_ge(s.branch_ps, g + 1)
                mc = M[:, (g % 4) * 512:(g % 4 + 1) * 512]
                if g < 4:
                    V.scalar_tensor_tensor(mc, TMPB, 1.0, BRB[:, :], ALU.add, ALU.mult).then_inc(s.tmp_mul, 1)
                else:
                    if g > 4:
                        dve.wait_ge(s.merged, g - 4)
                    if g + NIN > LN_AT + 1:
                        dve.wait_ge(s.yc_ready, 1)
                    V.scalar_tensor_tensor(TMPA, TMPB, 1.0, BRB[:, :], ALU.add, ALU.mult).then_inc(s.tmp_mul, 1)
                    dve.wait_ge(s.tmp_mul, g + 1)
                    V.tensor_tensor(mc, mc, TMPA, ALU.add).then_inc(s.merged, 1)

            split_lo(0)
            split_lo(1)
            for n in range(NIN + NGATE + 1):
                if n < NIN + NGATE:
                    split_lo(2 * n + 2)
                if n == 2:
                    dve.wait_ge(s.params_ps, 1)
                    V.tensor_copy(PAR, MISC[:, 0:NROWS]).then_inc(s.params_sb, 1)
                    dve.wait_ge(s.params_sb, 1)
                    V.tensor_scalar(HPAR, PAR[:, ROWS["ln_g"]:ROWS["ln_g"] + 4], 0.5, None, ALU.mult).then_inc(s.half_params, 1)
                    V.tensor_scalar(HGB, PAR[:, ROWS["b_gate"]:ROWS["b_gate"] + 32], 0.5, None, ALU.mult).then_inc(s.half_params, 1)
                if n == 3:
                    dve.wait_ge(s.cq_sum, 1)
                    dve.wait_ge(s.ckv_sum, 1)
                    V.tensor_scalar(TMPA[:, 0:T], MISC[:, 0:T], 1.0 / 256, EPS, ALU.mult, ALU.add).then_inc(s.cq_ve, 1)
                    V.tensor_scalar(TMPB[:, 0:T], MISC[:, T:2 * T], 1.0 / 128, EPS, ALU.mult, ALU.add).then_inc(s.ckv_ve, 1)
                    dve.wait_ge(s.part_done, 6)
                    for t in range(TT):
                        link(V.tensor_copy(VF[:, t, :], (PA, S0)[t][:, 0:260]))
                    dve.wait_ge(s.bias_in, 48)
                    fw = FW[:, 0:8].rearrange("p (t h) -> p t h", t=TT)
                    link(V.tensor_tensor(fw, VF[:, :, 256:260], BF.unsqueeze(1).to_broadcast([P, TT, HEADS]), ALU.add))
                    V.scalar_tensor_tensor(FW[:, 8:16], FW[:, 0:8], -1.0, FW[:, 0:8], ALU.mult, ALU.max).then_inc(s.fox_f, 1)
                    dve.wait_ge(s.cq_root, 1)
                    link(V.reciprocal(TMPA[:, 0:T], TMPA[:, 0:T]))
                    for j in range(2):
                        V.scalar_tensor_tensor(CQ[:, j, :], CQ[:, j, :], par("gq", j), TMPA[:, 0:T], ALU.mult, ALU.mult)\
                            .then_inc(s.cq_ready, 1)
                    dve.wait_ge(s.ckv_root, 1)
                    link(V.reciprocal(TMPB[:, 0:T], TMPB[:, 0:T]))
                    V.scalar_tensor_tensor(CKV, CKV, par("gkv"), TMPB[:, 0:T], ALU.mult, ALU.mult).then_inc(s.ckv_ready, 1)
                if n == 2:
                    dve.wait_ge(s.part_done, 4)
                    dve.wait_ge(s.ckv_sq, 1)
                    dve.wait_ge(s.tables_in, 16)
                    V.tensor_tensor(TMPB[64:128, T:2 * T], PB[64:128, T:2 * T],
                                    TABS[64:128, TAB["kcs"][0]:TAB["kcs"][1]], ALU.mult).then_inc(s.krope_sb, 1)
                if n == 4:
                    dve.wait_ge(s.fox_ln, 1)
                    V.scalar_tensor_tensor(FLOG.rearrange("p t h -> p (t h)"), FW[:, 0:8], 0.0, FW[:, 24:32], ALU.min,
                                           ALU.subtract).then_inc(s.fox_ready, 1)
                    dve.wait_ge(s.mla_ps, 1)
                    V.tensor_copy(Q[3].rearrange("p j t -> p (j t)"), S1[:, :]).then_inc(s.mla_evac, 1)
                    dve.wait_ge(s.mla_ps, 2)
                    dve.wait_ge(s.cq_ready, 2)
                    V.tensor_tensor(TMPA[:, 0:T], PT[:, 0:T], tab("cos"), ALU.mult).then_inc(s.rope_mul, 1)
                    V.tensor_tensor(TMPA[:, T:2 * T], PT[:, T:2 * T], tab("sin"), ALU.mult).then_inc(s.rope_mul, 1)
                    dve.wait_ge(s.rope_mul, 2)
                    V.tensor_tensor(QPE, TMPA[:, 0:T], TMPA[:, T:2 * T], ALU.add).then_inc(s.mla_evac, 1)
                    dve.wait_ge(s.mla_ps, 3)
                    dve.wait_ge(s.zeros_ready, 5)
                    for h in range(HEADS):
                        r = slice(64 * (h % 2), 64 * (h % 2) + 64)
                        ins = V.tensor_copy(KB[3][r, h, :], PV[r, (h // 2) * T:(h // 2 + 1) * T])
                    ins.then_inc(s.mla_evac, 1)
                    dve.wait_ge(s.mla_ps, 4)
                    V.tensor_copy(VMLA.rearrange("p t c -> p (t c)"), BRB[:, :]).then_inc(s.mla_evac, 1)
                if n == 5:
                    dve.wait_ge(s.kpe_ps, 1)
                    for h in range(HEADS):
                        r = slice(32 * h, 32 * h + 32)
                        ins = V.tensor_copy(KPE[r, h, :], S1[r, 0:T])
                    ins.then_inc(s.kpe_ready, 1)
                    dve.wait_ge(s.fox_ps, 1)
                    V.tensor_scalar(CTOK.rearrange("p t h -> p (t h)"), MISC[:, 0:8], 8.0, None, ALU.mult)\
                        .then_inc(s.cum_ready, 1)
                    for h in range(HEADS):
                        ins = V.tensor_scalar(CB[:, h, :], MISC[0:HEADS, T:2 * T], TABS[0:HEADS, h:h + 1], -8.0, ALU.mult, ALU.mult)
                    ins.then_inc(s.cum_ready, 1)
                if n == 7:
                    dve.wait_ge(s.conv_t, 1)
                    dve.wait_ge(s.conv_a_sb, 1)
                    V.scalar_tensor_tensor(UPAD[:, :, 30:286], TMPA.rearrange("p (j t) -> p j t", j=2), 1.0,
                                           TMPB.rearrange("p (j t) -> p j t", j=2), ALU.add, ALU.mult).then_inc(s.conv_u, 1)
                    dve.wait_ge(s.conv_u, 1)
                p = (n - FIRST_SCORES) // 2
                scoring = (n - FIRST_SCORES) % 2 == 0 and 0 <= p < len(PAIRS)
                if scoring:
                    logits(p)
                if n < NIN + NGATE:
                    split_lo(2 * n + 3)
                if scoring:
                    normalise(p)
                if CONV_FROM <= n < LN_AT:
                    conv_steps(CONV_TAPS)
                if n == LN_AT:
                    dve.wait_ge(s.conv_acc, 2 * CONV_K)
                    for j in range(2):
                        V.tensor_scalar(CACC[:, j, :], CACC[:, j, :], 0.5, par("conv_b", j), ALU.mult, ALU.add)\
                            .then_inc(s.conv_out, 1)
                if n == LN_AT + 1:
                    dve.wait_ge(s.ln_sum, 1)
                    V.scalar_tensor_tensor(CACC, MISC[:, 0:T].unsqueeze(1).to_broadcast([P, 2, T]), -1.0 / 256, CACC,
                                           ALU.mult, ALU.add).then_inc(s.ln_cent, 1)
                if n - 1 - NIN >= 0:
                    merge(n - 1 - NIN)
                if n == LN_AT + 2:
                    dve.wait_ge(s.ln_var, 1)
                    V.tensor_scalar(LNV, MISC[:, 0:T], 1.0 / 256, EPS, ALU.mult, ALU.add).then_inc(s.ln_ve, 1)
                    dve.wait_ge(s.ln_root, 1)
                    link(V.reciprocal(LNV, LNV))
                    link(V.tensor_tensor(CACC, CACC, LNV.unsqueeze(1).to_broadcast([P, 2, T]), ALU.mult))
                    for j in range(2):
                        ins = V.tensor_scalar(CACC[:, j, :], CACC[:, j, :], HPAR[:, j:j + 1], HPAR[:, 2 + j:3 + j], ALU.mult, ALU.add)
                    ins.then_inc(s.ln_z, 1)
                    dve.wait_ge(s.ln_t, 1)
                    V.scalar_tensor_tensor(YT[2].rearrange("p j t -> p (j t)"), LNT, 1.0, CACC.rearrange("p j t -> p (j t)"),
                                           ALU.add, ALU.mult).then_inc(s.yc_ready, 1)
            for m in range(KD):
                dve.wait_ge(s.merge_hi, m + 1)
                V.scalar_tensor_tensor(XL[:, m * T:(m + 1) * T], M[:, m * T:(m + 1) * T], 0.5,
                                       f32(XH[:, m * T:(m + 1) * T]), ALU.mult, ALU.subtract).then_inc(s.merge_split, 1)
                if m % 2:
                    split_lo(2 * (NIN + NGATE) + 2 + m // 2)
            for q in range(2 * (NIN + NGATE) + 6, 2 * UNITS):
                split_lo(q)
            dve.wait_ge(s.part_done, 2 * UNITS)
            for t in range(TT):
                for half in range(2):
                    c = slice(half * 512, half * 512 + 512)
                    V.tensor_tensor(H[:, t, c], H[:, t, c], bank[2 * t + half][:, :], ALU.add).then_inc(s.h_ready, 1)
            dve.wait_ge(s.h_sq, TT)
            V.tensor_scalar(SS, SS, 1.0 / D, EPS, ALU.mult, ALU.add).then_inc(s.h_var, 1)
            dve.wait_ge(s.h_root, 1)
            link(V.reciprocal(RS, RS))
            for t in range(TT):
                V.tensor_scalar(HS[:, t, :], H[:, t, :], RS[:, t:t + 1], None, ALU.mult).then_inc(s.h_scaled, 1)
            for b in range(4):
                dve.wait_ge(s.hst_ps, b + 1)
                for k in (2 * b, 2 * b + 1):
                    V.tensor_scalar(M[:, k * T:(k + 1) * T], bank[b][:, (k % 2) * T:(k % 2 + 1) * T], G2[:, k:k + 1], None,
                                    ALU.mult).then_inc(s.hst_sb, 1)
            for t in range(TT):
                dve.wait_ge(s.hs_hi, t + 1)
                V.tensor_tensor(XL[:, t * D:(t + 1) * D], HS[:, t, :], f32(XH[:, t * D:(t + 1) * D]), ALU.subtract)\
                    .then_inc(s.hs_split, 1)

            rc = [0]

            def rlink(ins):
                rc[0] += 1
                ins.then_inc(s.router_chain, 1)
                dve.wait_ge(s.router_chain, rc[0])

            rb = carver(RB, 800)
            GD = rb(8).rearrange("p (t g) -> p t g", t=TT)
            GE = rb(8).rearrange("p (t g) -> p t g", t=TT)
            DM = rb(2)
            EX2 = rb(2)
            one = lambda: rb(2)
            grp = lambda: rb(8).rearrange("p (t g) -> p t g", t=TT)
            exl = lambda: rb(16).rearrange("p (t e) -> p t e", t=TT)
            all_ = lambda: rb(64).rearrange("p (t g e) -> p t g e", t=TT, g=NG)
            GMAX, PG, IDX, M1, M2, W1, W2 = (one() for _ in range(7))
            GC, OG = grp(), grp()
            EIN, ED, OE1, OE2, O8, W8, E2 = (exl() for _ in range(7))
            EALL, O32 = all_(), all_()

            def spread(v, n):
                return v.unsqueeze(2).to_broadcast([P, TT, n])

            def iota(n):
                return tab("iota")[:, 0:n].unsqueeze(1).to_broadcast([P, TT, n])

            def first_of_max(onehot, dist, work, n):
                rlink(V.tensor_scalar(work, dist, 0.0, 100.0, ALU.is_lt, ALU.mult))
                rlink(V.tensor_tensor(work, work, iota(n), ALU.add))
                rlink(V.tensor_reduce(IDX, work, AXX, ALU.min))
                rlink(V.tensor_tensor(onehot, iota(n), spread(IDX, n), ALU.is_equal))

            dve.wait_ge(s.logits_ps, 1)
            rlink(V.tensor_tensor(LG, MISC[:, 0:72].rearrange("p (t n) -> p t n", t=TT),
                                  BR.unsqueeze(1).to_broadcast([P, TT, 36]), ALU.add))
            rlink(V.reduce_max(GMAX, LG[:, :, 0:NG], AXX))
            V.tensor_tensor(GD, LG[:, :, 0:NG], spread(GMAX, NG), ALU.subtract).then_inc(s.router_exp, 1)
            dve.wait_ge(s.router_exp, 1)
            first_of_max(OG, GD, GC, NG)
            rlink(V.tensor_tensor(EALL, LG[:, :, NG:36].rearrange("p t (g e) -> p t g e", g=NG),
                                  OG.unsqueeze(3).to_broadcast([P, TT, NG, EG]), ALU.mult))
            rlink(V.reduce_sum(EIN, EALL.rearrange("p t g e -> p t e g"), AXX))
            rlink(V.reduce_max(M1, EIN, AXX))
            rlink(V.tensor_tensor(ED, EIN, spread(M1, EG), ALU.subtract))
            first_of_max(OE1, ED, E2, EG)
            rlink(V.scalar_tensor_tensor(EIN, OE1, -3e38, EIN, ALU.mult, ALU.add))
            rlink(V.reduce_max(M2, EIN, AXX))
            dve.wait_ge(s.router_exp, 2)
            V.tensor_tensor(DM, M2, M1, ALU.subtract).then_inc(s.router_exp, 1)
            rlink(V.tensor_tensor(ED, EIN, spread(M2, EG), ALU.subtract))
            first_of_max(OE2, ED, E2, EG)
            rlink(V.reduce_sum(PG, GE, AXX))
            rlink(V.reciprocal(PG, PG))
            dve.wait_ge(s.router_exp, 4)
            rlink(V.tensor_scalar(W1, EX2, 1.0, None, ALU.add))
            rlink(V.reciprocal(W1, W1))
            rlink(V.tensor_tensor(W1, W1, PG, ALU.mult))
            rlink(V.tensor_tensor(W2, W1, EX2, ALU.mult))
            rlink(V.tensor_tensor(O8, OE1, OE2, ALU.add))
            rlink(V.tensor_tensor(OE1, OE1, spread(W1, EG), ALU.mult))
            rlink(V.tensor_tensor(OE2, OE2, spread(W2, EG), ALU.mult))
            rlink(V.tensor_tensor(W8, OE1, OE2, ALU.add))

            def outer(dst, a8):
                V_in = a8.unsqueeze(2).to_broadcast([P, TT, NG, EG])
                return V.tensor_tensor(dst, OG.unsqueeze(3).to_broadcast([P, TT, NG, EG]), V_in, ALU.mult)

            rlink(outer(WT.rearrange("p t (g e) -> p t g e", g=NG), W8))
            outer(O32, O8).then_inc(s.sel_ready, 1)
            dve.wait_ge(s.rank_ps, 1)
            o32 = O32.rearrange("p t g e -> p t (g e)")
            rlink(V.tensor_tensor(RANK[:, :, 0:NE], S0[:, 0:2 * NE].rearrange("p (t e) -> p t e", t=TT), o32, ALU.mult))
            for r in range(ROUNDS, -1, -1):
                rlink(V.tensor_scalar(RANK[:, :, r * NE:(r + 1) * NE], RANK[:, :, 0:NE], -1.0 - CAP * r, None, ALU.add))

            oc = [0]

            def olink(ins):
                oc[0] += 1
                ins.then_inc(s.over_chain, 1)
                dve.wait_ge(s.over_chain, oc[0])

            NC = ROUNDS * NQ
            ov = carver(OV, 700)
            CMAX, FLAG, POS = ov(NQ), ov(NC), ov(NC)
            EQ = ov(8 * NC).rearrange("p (j c) -> p j c", j=8)
            EQC = ov(8 * NC).rearrange("p (j c) -> p j c", j=8)
            LF = ov(17)
            olink(V.reduce_max(CMAX, S0[:, 2 * NE:3 * NE].rearrange("p (q e) -> p q e", q=NQ), AXX))
            for r in range(ROUNDS):
                olink(V.tensor_scalar(FLAG[:, r * NQ:(r + 1) * NQ], CMAX, float(CAP * (r + 1)), None, ALU.is_gt))
            olink(V.tensor_tensor_scan(POS, ones_mat[:, 0:NC], FLAG, 0.0, ALU.mult, ALU.add))
            olink(V.reduce_max(LF[:, 0:1], POS, AXX))
            olink(V.tensor_tensor(POS, POS, FLAG, ALU.mult))
            jota = tab("iota")[:, 1:9].unsqueeze(2).to_broadcast([P, 8, NC])
            olink(V.tensor_tensor(EQ, POS.unsqueeze(1).to_broadcast([P, 8, NC]), jota, ALU.is_equal))
            for i in range(2):
                code = tab("code")[:, i * NC:(i + 1) * NC].unsqueeze(1).to_broadcast([P, 8, NC])
                olink(V.tensor_tensor(EQC, EQ, code, ALU.mult))
                olink(V.reduce_sum(LF[:, 1 + 8 * i:9 + 8 * i], EQC, AXX))
            V.tensor_copy(LIST[0:1, 0:17], LF[0:1, :]).then_inc(s.over_ready, 1)
            dve.drain().then_inc(s.o_free, 2)

            def select(n, col):
                after(dve, s.wselt_ps, n * 2)
                after(dve, s.gather_ps, n * 4)
                slot = tab("iota").unsqueeze(1).to_broadcast([P, QUAD, CAP])
                for t in range(TT):
                    V.tensor_tensor(SEL[:, t, :, :], RANK[:, t, bass.ds(col, QUAD)].unsqueeze(2).to_broadcast([P, QUAD, CAP]),
                                    slot, ALU.is_equal).then_inc(s.sel_chain, 1)
                after(dve, s.sel_chain, n * 2 + 2)

            def weigh(n, expert):
                for t in range(TT):
                    V.tensor_tensor(WSEL[:, t, :, :], f32(SEL[:, t, :, :]),
                                    WT[:, t, bass.ds(expert, QUAD)].unsqueeze(2).to_broadcast([P, QUAD, CAP]), ALU.mult)\
                        .then_inc(s.wsel_ready, 1)

            def take_gathered(n, b):
                after(dve, s.gather_ps, n * 4 + b + 1)
                for k in (2 * b, 2 * b + 1):
                    V.tensor_scalar(M[:, k * T:(k + 1) * T], bank[6][:, (k % 2) * T:(k % 2 + 1) * T], G2[:, k:k + 1], None,
                                    ALU.mult).then_inc(s.xe_ready, 1)

            def y_low(n, pair, half):
                after(dve, s.y_hi, n * 4 + 2 * pair + half + 1)
                V.scalar_tensor_tensor(y_part(WL, pair, half), bank[2 + half][:, :],
                                       WS[:, pair:pair + 1], f32(y_part(WH, pair, half)),
                                       ALU.mult, ALU.subtract).then_inc(s.y_split, 1)

            def hidden(n, pair):
                hb = bank[pair]
                after(dve, s.hid_t, n * 2 + pair + 1)
                V.scalar_tensor_tensor(TH[:, pair, :], TH[:, pair, :], 1.0, hb[:, 0:FF], ALU.add, ALU.mult)\
                    .then_inc(s.step_chain, 1)
                after(dve, s.step_chain, n * 2 + pair + 1)
                V.scalar_tensor_tensor(HT_[:, pair, :], TH[:, pair, :], 0.5, hb[:, FF:2 * FF], ALU.mult, ALU.mult)\
                    .then_inc(s.hid_ready, 1)

            def hidden_t(n, pair):
                after(dve, s.hidt_ps, n * 2 + pair + 1)
                V.tensor_copy(HTT[:, pair, :, :], bank[7][:, T:2 * T].rearrange("p (j c) -> p j c", j=2)).then_inc(s.hidt_sb, 1)

            def slot_weights(n, pair):
                after(dve, s.wselt_ps, n * 2 + pair + 1)
                V.reduce_max(WS[:, pair:pair + 1], bank[7][:, 0:T], AXX).then_inc(s.slot_weight, 1)
                after(dve, s.slot_weight, n * 2 + pair + 1)
                V.tensor_scalar(SELT[:, pair, :], bank[7][:, 0:T], 0.0, None, ALU.is_gt).then_inc(s.selt_sb, 1)

            def add_outputs(n):
                for t in range(TT):
                    for half in range(2):
                        c = slice(half * 512, half * 512 + 512)
                        after(dve, s.o_ps, n * 4 + 2 * t + half + 1)
                        V.tensor_tensor(H[:, t, c], H[:, t, c], bank[4 + half][:, :], ALU.add).then_inc(s.o_free, 1)

            def step(n, select_next=None, add_previous=True):
                if add_previous:
                    add_outputs(n - 1)
                slot_weights(n, 0)
                hidden(n, 0)
                slot_weights(n, 1)
                if select_next is not None:
                    select_next()
                hidden_t(n, 0)
                hidden(n, 1)
                if select_next is not None:
                    take_gathered(n + 1, 0)
                hidden_t(n, 1)
                if select_next is not None:
                    take_gathered(n + 1, 1)
                y_low(n, 0, 0)
                if select_next is not None:
                    take_gathered(n + 1, 2)
                y_low(n, 0, 1)
                if select_next is not None:
                    take_gathered(n + 1, 3)
                y_low(n, 1, 0)
                y_low(n, 1, 1)

            def select_quad(n, col, expert):
                select(n, col)
                weigh(n, expert)

            select_quad(0, 0, 0)
            for b in range(4):
                take_gathered(0, b)
            step(0, lambda: select_quad(1, QUAD, QUAD), add_previous=False)
            with dve.Fori(1, NQ - 1) as i:
                step(i, lambda: select_quad(i + 1, i * QUAD + QUAD, i * QUAD + QUAD))
            step(NQ - 1)
            add_outputs(NQ - 1)
            count = dve.value_load(LIST[0:1, 0:1], min_val=0, max_val=MAXOVER)
            with dve.If(count > 0):
                with dve.Fori(0, count) as j:
                    col = dve.value_load(LIST[0:1, bass.ds(j + 1, 1)], min_val=0, max_val=(ROUNDS + 1) * NE - QUAD)
                    q = dve.value_load(LIST[0:1, bass.ds(j + 9, 1)], min_val=0, max_val=NQ - 1)
                    select_quad(j + NQ, col, q * QUAD)
                    for b in range(4):
                        take_gathered(j + NQ, b)
                    step(j + NQ, add_previous=False)
                    add_outputs(j + NQ)
            dve.end_ifs()
            dve.drain().then_inc(s.final_sq, 1)
            dve.wait_ge(s.final_sq, 1 + TT)
            V.tensor_scalar(SS, SS, 1.0 / D, EPS, ALU.mult, ALU.add).then_inc(s.final_var, 1)
            dve.wait_ge(s.final_root, 1)
            link(V.reciprocal(RS, RS))
            dve.wait_ge(s.final_in, 16)
            for t in range(TT):
                V.scalar_tensor_tensor(YOUT[:, t, :], H[:, t, :], RS[:, t:t + 1], FG, ALU.mult, ALU.mult)\
                    .then_inc(s.out_ready, 1)

        @block.tensor
        def _(pe):
            mm = nc.tensor.matmul

            def transpose(dst, src):
                k = src.shape[0]
                return nc.tensor.transpose(dst, src, ident[0:k, 0:k])

            pe.wait_ge(s.ident_in, 16)
            pe.wait_ge(s.xscaled, TT)
            xs = M[:, :].rearrange("p (t q k) -> p t q k", t=TT, k=KD)
            for k in range(KD):
                for t in range(TT):
                    ins = transpose(bank[k // 2][:, (k % 2) * T + t * P:(k % 2) * T + (t + 1) * P], xs[:, t, :, k])
                if k % 2:
                    ins.then_inc(s.xt_ps, 1)

            def three(dst, wh, wl, xh, xl, first, last):
                mm(dst, wh, xh, start=first, stop=False)
                mm(dst, wl, xh, start=False, stop=False)
                return mm(dst, wh, xl, start=False, stop=last)

            def act_tile(k, c=slice(0, T)):
                a = slice(k * T + c.start, k * T + c.stop)
                return XH[:, a], XL[:, a]

            def project(q, dst, wait_x=False):
                pe.wait_ge(s.w_lo, q + 1)
                for k in range(KD):
                    if wait_x:
                        pe.wait_ge(s.x_split, k + 1)
                    c = slice(k * 128, (k + 1) * 128)
                    ins = three(dst, part(WH, q, c), part(WL, q, c), *act_tile(k), k == 0, k == KD - 1)
                ins.then_inc(s.part_done, 1)
                return ins

            def project_tokens(n, dsts, ncol):
                for h in range(2):
                    q = 2 * n + h
                    pe.wait_ge(s.w_lo, q + 1)
                    for t in range(TT):
                        for k in range(4 * h, 4 * h + 4):
                            xh, xl = act_tile(k, slice(t * P, (t + 1) * P))
                            c = slice((k % 4) * ncol, (k % 4 + 1) * ncol)
                            wh, wl = part(WH, q, c), part(WL, q, c)
                            mm(dsts[t], xh, wh, start=(k == 0), stop=False)
                            mm(dsts[t], xl, wh, start=False, stop=False)
                            ins = mm(dsts[t], xh, wl, start=False, stop=(k == KD - 1))
                    ins.then_inc(s.part_done, 1)

            def channel_sum(dst, tiles, done):
                for j, tile in enumerate(tiles):
                    ins = mm(dst, ones_mat, tile, start=(j == 0), stop=(j == len(tiles) - 1))
                ins.then_inc(done, 1)

            def halves(ap):
                return [ap[:, 0:T], ap[:, T:2 * T]]

            def scores(p):
                b, hp = PAIRS[p]
                if p:
                    pe.wait_ge(s.logit_ready, 4 * p)
                else:
                    pe.wait_ge(s.kpe_ready, 1)
                    pe.wait_ge(s.mla_evac, 4)
                if b != 3:
                    pe.wait_ge(s.proj_evac, 2 if b == 1 else 4)
                if b == 1:
                    pe.wait_ge(s.cum_ready, 2)
                for qt in range(2):
                    n = P if qt == 0 else T
                    dst = (S0, S1)[qt][:, 0:2 * n]
                    q = slice(qt * P, (qt + 1) * P)
                    ins = mm(dst, Q[b][:, hp, q], KB[b][:, 2 * hp:2 * hp + 2, 0:n], start=True, stop=(b == 0))
                    if b == 3:
                        ins = mm(dst, QPE[:, q], KPE[:, 2 * hp:2 * hp + 2, 0:n], start=False, stop=True)
                    if b == 1:
                        ins = mm(dst, ones_mat[0:HEADS, :], CB[:, 2 * hp:2 * hp + 2, 0:n], start=False, stop=True)
                ins.then_inc(s.score_ps, 1)

            def transpose_probs(p):
                for h in range(2):
                    pe.wait_ge(s.prob_ready, 2 * p + h + 1)
                    if p:
                        pe.wait_ge(s.pt_sb, 2 * p - 1 + h)
                    for i in range(3):
                        ins = transpose((PT, MISC)[h][:, i * P:(i + 1) * P], PR[:, h, i * P:(i + 1) * P])
                    ins.then_inc(s.pt_ps, 1)

            def attend(p):
                b, hp = PAIRS[p]
                v = VMAP[b]
                for h in range(2):
                    if h == 0 and p:
                        pe.wait_ge(s.attn_ready, p)
                    if b == 0:
                        pe.wait_ge(s.proj_evac, 5)
                    pe.wait_ge(s.pt_sb, 2 * p + h + 1)
                    pts = (PTS, PTS2)[h]
                    r = slice(64 * h, 64 * h + 64)
                    vc = slice((2 * hp + h) * HD, (2 * hp + h + 1) * HD)
                    mm(PV[r, 0:P], v[:, 0, vc], pts[:, 0:P], start=True, stop=True)
                    mm(PV[r, P:T], v[:, 0, vc], pts[:, P:T], start=True, stop=False)
                    mm(PV[r, P:T], v[:, 1, vc], pts[:, T:384], start=False, stop=True).then_inc(s.pv_ps, 1)

            tri0 = tri[:, 0:P]
            for n in range(NIN + NGATE):
                pg = (PA, PB)[n % 2]
                if n == 1:
                    pe.wait_ge(s.params_in, 16 * 7)
                    transpose(MISC[:, 0:NROWS], ROWP[0:NROWS, :]).then_inc(s.params_ps, 1)
                if n == 3:
                    pe.wait_ge(s.tables_in, 16)
                    pe.wait_ge(s.params_sb, 1)
                    pe.wait_ge(s.cq_sq, 1)
                    channel_sum(MISC[:, 0:T], halves(TMPA), s.cq_sum)
                    pe.wait_ge(s.ckv_sq, 1)
                    channel_sum(MISC[:, T:2 * T], [TMPB[:, 0:T]], s.ckv_sum)
                if n == 4:
                    pe.wait_ge(s.cq_ready, 2)
                    pe.wait_ge(s.wmla_in, 96)
                    pe.wait_ge(s.wrot_ready, 4)
                    for m in range(2):
                        for j in range(2):
                            ins = mm(S1[:, m * T:(m + 1) * T], WUQ[:, j, m * P:(m + 1) * P], CQ[:, j, :],
                                     start=(j == 0), stop=(j == 1))
                    ins.then_inc(s.mla_ps, 1)
                    for j in range(2):
                        mm(PT[:, 0:T], WUQ[:, j, 256:384], CQ[:, j, :], start=(j == 0), stop=(j == 1))
                    for j in range(2):
                        ins = mm(PT[:, T:2 * T], WROT[:, j, :, :].rearrange("p h c -> p (h c)"), CQ[:, j, :],
                                 start=(j == 0), stop=(j == 1))
                    ins.then_inc(s.mla_ps, 1)
                    pe.wait_ge(s.ckv_ready, 1)
                    for m in range(2):
                        ins = mm(PV[:, m * T:(m + 1) * T], WUKV[:, m * P:(m + 1) * P], CKV, start=True, stop=True)
                    ins.then_inc(s.mla_ps, 1)
                    for t in range(TT):
                        ins = mm(BRB[:, t * T:(t + 1) * T], CKV[:, t * P:(t + 1) * P], WUKV[:, 256:512], start=True, stop=True)
                    ins.then_inc(s.mla_ps, 1)
                if n == 5:
                    pe.wait_ge(s.krope_sb, 1)
                    pe.wait_ge(s.mla_evac, 1)
                    mm(S1[:, 0:T], TABS[64:128, TAB["rep"][0]:TAB["rep"][1]], TMPB[64:128, T:2 * T], start=True, stop=True)\
                        .then_inc(s.kpe_ps, 1)
                    pe.wait_ge(s.fox_ready, 1)
                    pe.wait_ge(s.ckv_ve, 1)
                    mm(MISC[:, 0:4], tri0, FLOG[:, 0, :], start=True, stop=True)
                    mm(MISC[:, 4:8], ones_mat, FLOG[:, 0, :], start=True, stop=False)
                    mm(MISC[:, 4:8], tri0, FLOG[:, 1, :], start=False, stop=True)
                    mm(MISC[0:HEADS, T:T + P], FLOG[:, 0, :], tri0, start=True, stop=True)
                    mm(MISC[0:HEADS, T + P:2 * T], FLOG[:, 0, :], ones_mat, start=True, stop=False)
                    mm(MISC[0:HEADS, T + P:2 * T], FLOG[:, 1, :], tri0, start=False, stop=True).then_inc(s.fox_ps, 1)
                p = (n - FIRST_SCORES) // 2
                if (n - FIRST_SCORES) % 2 == 0 and 0 <= p <= len(PAIRS):
                    if p:
                        if n >= NIN:
                            pe.wait_ge(s.proj_evac, 5)
                        transpose_probs(p - 1)
                    if p < len(PAIRS):
                        scores(p)
                    if p:
                        attend(p - 1)
                if n == LN_AT + 1:
                    pe.wait_ge(s.conv_out, 2)
                    channel_sum(MISC[:, 0:T], [CACC[:, j, :] for j in range(2)], s.ln_sum)
                if n == LN_AT + 2:
                    pe.wait_ge(s.ln_sq, 1)
                    channel_sum(MISC[:, 0:T], halves(LNT), s.ln_var)
                if n == 2:
                    pe.wait_ge(s.cq_sq, 1)
                    project_tokens(n, [PA[:, 0:260], S0[:, 0:260]], 260)
                elif n == 9:
                    pe.wait_ge(s.proj_evac, 3)
                    pe.wait_ge(s.pt_sb, 2)
                    project_tokens(n, [PB[:, 0:T], MISC[:, 0:T]], 256)
                else:
                    if n == 0:
                        pass
                    elif n == 3:
                        pe.wait_ge(s.ckv_sq, 1)
                        pe.wait_ge(s.krope_sb, 1)
                    elif n == 4:
                        pe.wait_ge(s.fox_f, 1)
                    elif n == 5:
                        pe.wait_ge(s.proj_evac, 1)
                    elif n == 6:
                        pe.wait_ge(s.proj_evac, 2)
                    elif n == 7:
                        pe.wait_ge(s.conv_a_sb, 1)
                    elif n == 8:
                        pe.wait_ge(s.conv_t, 1)
                    elif n == NIN:
                        pe.wait_ge(s.proj_evac, 4)
                    elif n == NIN + 1:
                        pe.wait_ge(s.proj_evac, 5)
                    elif n > NIN + 1:
                        pe.wait_ge(s.gate_t, 2 * (n - NIN - 1))
                    for m in range(2):
                        ins = project(2 * n + m, pg[:, m * T:(m + 1) * T], n == 0 and m == 0)
                if n < NIN:
                    continue
                g = n - NIN
                b = BRANCHES[g // 4]
                if g % 4 == 0:
                    if b == 2:
                        pe.wait_ge(s.yc_ready, 1)
                    else:
                        pe.wait_ge(s.attn_ready, {3: 2, 1: 4, 0: 6}[b])
                if g:
                    pe.wait_ge(s.tmp_mul, g)
                wb = RAW[n % NRAW][:, 2048:2560].rearrange("p (j n) -> p j n", j=2)
                for m in range(2):
                    for j in range(2):
                        ins = mm(BRB[:, m * T:(m + 1) * T], wb[:, j, m * 128:(m + 1) * 128], YT[b][:, j, :],
                                 start=(j == 0), stop=(j == 1))
                ins.then_inc(s.branch_ps, 1)
            pe.wait_ge(s.gate_t, 2 * NGATE)
            pe.wait_ge(s.tmp_mul, NGATE)
            for m in range(KD):
                q = 2 * (NIN + NGATE) + m
                pe.wait_ge(s.w_lo, q + 1)
                pe.wait_ge(s.merge_split, m + 1)
                for t in range(TT):
                    xh, xl = act_tile(m, slice(t * P, (t + 1) * P))
                    for half in range(2):
                        c = slice(half * 512, half * 512 + 512)
                        dst = bank[2 * t + half][:, :]
                        mm(dst, xh, part(WH, q, c), start=(m == 0), stop=False)
                        mm(dst, xl, part(WH, q, c), start=False, stop=False)
                        ins = mm(dst, xh, part(WL, q, c), start=False, stop=(m == KD - 1))
                ins.then_inc(s.part_done, 1)
            pe.wait_ge(s.h_scaled, TT)
            pe.wait_ge(s.h_ready, 2 * TT)
            hs = HS.rearrange("p t (q k) -> p t q k", k=KD)
            for k in range(KD):
                for t in range(TT):
                    ins = transpose(bank[k // 2][:, (k % 2) * T + t * P:(k % 2) * T + (t + 1) * P], hs[:, t, :, k])
                if k % 2:
                    ins.then_inc(s.hst_ps, 1)
            pe.wait_ge(s.router_in, 32)
            for t in range(TT):
                for k in range(KD):
                    if t == 0:
                        pe.wait_ge(s.hst_sb, k + 1)
                    ins = mm(MISC[:, t * 36:(t + 1) * 36], M[:, k * T + t * P:k * T + (t + 1) * P], WR[:, k, :],
                             start=(k == 0), stop=(k == KD - 1))
            ins.then_inc(s.logits_ps, 1)
            pe.wait_ge(s.sel_ready, 1)
            o32 = RB_view(RB)
            mm(S0[:, 0:NE], tri0, o32[:, 0, :], start=True, stop=True)
            mm(S0[:, NE:2 * NE], ones_mat, o32[:, 0, :], start=True, stop=False)
            mm(S0[:, NE:2 * NE], tri0, o32[:, 1, :], start=False, stop=True)
            mm(S0[:, 2 * NE:3 * NE], ones_mat, o32[:, 0, :], start=True, stop=False)
            mm(S0[:, 2 * NE:3 * NE], ones_mat, o32[:, 1, :], start=False, stop=True).then_inc(s.rank_ps, 1)

            xe = M[:, :].rearrange("p (k c) -> p k c", k=KD)
            xh4 = XH[:, :].rearrange("p (t q k) -> p t q k", t=TT, k=KD)
            xl4 = XL[:, :].rearrange("p (t q k) -> p t q k", t=TT, k=KD)

            def gather_part(n, b):
                if b == 0:
                    after(pe, s.sel_chain, n * 2 + 2)
                after(pe, s.xe_ready, n * 8 + 2 * b)
                for k in (2 * b, 2 * b + 1):
                    dst = bank[6][:, (k % 2) * T:(k % 2 + 1) * T]
                    for t in range(TT):
                        sel = SEL[:, t, :, :]
                        mm(dst, xh4[:, t, :, k], sel, start=(t == 0), stop=False)
                        ins = mm(dst, xl4[:, t, :, k], sel, start=False, stop=(t == TT - 1))
                ins.then_inc(s.gather_ps, 1)

            def select_t(n, pair):
                if pair == 0:
                    after(pe, s.wsel_ready, n * 2 + 2)
                    after(pe, s.hidt_sb, n * 2)
                else:
                    after(pe, s.selt_sb, n * 2 + 1)
                for t in range(TT):
                    ins = transpose(bank[7][:, t * P:(t + 1) * P],
                                    WSEL[:, t, 2 * pair:2 * pair + 2, :].rearrange("p e c -> p (e c)"))
                ins.then_inc(s.wselt_ps, 1)

            def wait_slots(n, pair, kind):
                for e in range(2):
                    pe.wait_ge(exp_in[slot_plan.index((pair, kind, e))], n * 16 + 16)

            def hidden(n, pair, kind):
                if kind == 0:
                    after(pe, s.xe_ready, n * 8 + 8)
                    after(pe, s.hid_ready, n * 2 - 1 + pair)
                wait_slots(n, pair, kind)
                for k in range(KD):
                    for e in range(2):
                        w = expert_slot(pair, kind, e)[:, k * FF:(k + 1) * FF]
                        x = xe[:, k, (2 * pair + e) * CAP:(2 * pair + e + 1) * CAP]
                        ins = mm(bank[pair][64 * e:64 * e + 64, kind * FF:(kind + 1) * FF], x, w,
                                 start=(k == 0), stop=(k == KD - 1), skip_group_check=True)
                ins.then_inc((s.gates_ps, s.hid_ps)[kind], 1)

            def hidden_t(n, pair):
                after(pe, s.hid_ready, n * 2 + pair + 1)
                if pair == 0:
                    after(pe, s.selt_sb, n * 2 + 2)
                else:
                    after(pe, s.hidt_sb, n * 2 + 1)
                h2 = HT_[:, pair, :].rearrange("p (f j) -> p f j", j=2)
                for j in range(2):
                    ins = transpose(bank[7][:, T + j * P:T + (j + 1) * P], h2[:, :, j])
                ins.then_inc(s.hidt_ps, 1)

            def down(n, pair, half):
                if half == 0:
                    after(pe, s.hidt_sb, n * 2 + pair + 1)
                    wait_slots(n, pair, 2)
                after(pe, s.y_split, n * 4 + (half + 1 if pair else half - 1))
                for j in range(2):
                    for e in range(2):
                        w = expert_slot(pair, 2, e)[:, j * D + half * 512:j * D + half * 512 + 512]
                        ins = mm(bank[2 + half][64 * e:64 * e + 64, :], HTT[:, pair, j, 64 * e:64 * e + 64], w,
                                 start=(j == 0), stop=(j == 1), skip_group_check=True)
                ins.then_inc(s.y_ps, 1)

            def scatter(n):
                for t in range(TT):
                    for half in range(2):
                        i = 2 * t + half
                        after(pe, s.o_free, n * 4 + i + 1)
                        for pair in range(2):
                            after(pe, s.y_split, n * 4 + 2 * pair + half + 1)
                            lhs = SELT[:, pair, t * P:(t + 1) * P]
                            mm(bank[4 + half][:, :], lhs, y_part(WH, pair, half), start=(pair == 0), stop=False)
                            ins = mm(bank[4 + half][:, :], lhs, y_part(WL, pair, half), start=False, stop=(pair == 1))
                        ins.then_inc(s.o_ps, 1)

            def step(n, scatter_previous=True, gather_next=True):
                hidden(n, 0, 0)
                if scatter_previous:
                    scatter(n - 1)
                select_t(n, 0)
                hidden(n, 0, 1)
                select_t(n, 1)
                hidden(n, 1, 0)
                hidden_t(n, 0)
                hidden(n, 1, 1)
                if gather_next:
                    gather_part(n + 1, 0)
                down(n, 0, 0)
                hidden_t(n, 1)
                if gather_next:
                    gather_part(n + 1, 1)
                down(n, 0, 1)
                if gather_next:
                    gather_part(n + 1, 2)
                down(n, 1, 0)
                if gather_next:
                    gather_part(n + 1, 3)
                down(n, 1, 1)

            pe.wait_ge(s.hs_split, TT)
            pe.wait_ge(s.over_ready, 1)
            for b in range(4):
                gather_part(0, b)
            step(0, scatter_previous=False)
            with pe.Fori(1, NQ - 1) as i:
                step(i)
            step(NQ - 1, gather_next=False)
            scatter(NQ - 1)
            count = pe.value_load(LIST[0:1, 0:1], min_val=0, max_val=MAXOVER)
            with pe.If(count > 0):
                with pe.Fori(0, count) as j:
                    for b in range(4):
                        gather_part(j + NQ, b)
                    step(j + NQ, scatter_previous=False, gather_next=False)
                    scatter(j + NQ)
            pe.end_ifs()


def RB_view(RB):
    at = 20 + 7 * 2 + 2 * 8 + 7 * 16 + 64
    return RB[:, at:at + 64].rearrange("p (t e) -> p t e", t=TT)


_INS = ["x", "norm1_g", "w_in", "b_forget", "conv_w", "conv_b", "conv_ln_g", "conv_ln_b", "mla_gq", "mla_wuq", "mla_gkv",
        "mla_wukv", "w_gate", "b_gate", "w_branch", "w_out", "norm2_g", "w_router_group", "b_router_group",
        "w_router_expert", "b_router_expert", "w_exp_gate", "w_exp_up", "w_exp_down", "final_g"]


def kernel(**inputs):
    import concourse.bacc as bacc
    from concourse.bass_utils import run_bass_kernel_spmd

    nc = bacc.Bacc("TRN2", target_bir_lowering=False, num_devices=1)
    arrays, aps = {}, {}
    for name in _INS:
        a = np.ascontiguousarray(inputs[name])
        arrays[f"in_{name}"] = a
        aps[name] = nc.dram_tensor(f"in_{name}", a.shape, mybir.dt.from_np(a.dtype), kind="ExternalInput").ap()
    arrays["in_tables"] = shape_tables()
    aps["tables"] = nc.dram_tensor("in_tables", (P, NTAB), F32, kind="ExternalInput").ap()
    out = nc.dram_tensor("out_y", (1, T, D), F32, kind="ExternalOutput").ap()
    trunk_kernel(nc, aps, out)
    r = run_bass_kernel_spmd(nc, [arrays], core_ids=[0])
    return r.results[0]["out_y"]
```

```python
from contextlib import ExitStack

import numpy as np

import concourse.bass as bass
from concourse import mybir

F32 = mybir.dt.float32
F32R = mybir.dt.float32r
I32 = mybir.dt.int32
ALU = mybir.AluOpType
ACT = mybir.ActivationFunctionType
AXX = mybir.AxisListType.X

P = 128
D = 1024
T = 256
TT = T // P
KD = D // P
HD = 64
HEADS = 4
NE = 32
EG = 8
NG = 4
FF = 256
CONV_K = 31
EPS = 1e-6
NEG = -1e30
CAP = 64
QUAD = 4
NQ = NE // QUAD
ROUNDS = T // CAP - 1
MAXOVER = 2 * T // (CAP + 1)
SLOT = 2 * D
RAWW = 10 * 256
NRAW = 3
PARTW = 4 * 260
NPART = 4

W_IN_UNITS = [("cq", 2052, 2308), ("ckv", 2308, 2468), ("fox_v", 1280, 1540), ("fox_q", 768, 1024),
              ("fox_k", 1024, 1280), ("conv_a", 1540, 1796), ("conv_g", 1796, 2052), ("moba_q", 0, 256),
              ("moba_k", 256, 512), ("moba_v", 512, 768)]
BRANCHES = [3, 1, 0, 2]
NIN = len(W_IN_UNITS)
NGATE = 4 * len(BRANCHES)
NOUT = 4
UNITS = NIN + NGATE + NOUT
PREFETCH_AT = NIN + 2
FIRST_SCORES = 6
CONV_FROM, CONV_TAPS = 8, 6
LN_AT = CONV_FROM + -(-2 * CONV_K // CONV_TAPS)

ROWS = {}
_r = 0
for _n, _c in (("conv_w", 2 * CONV_K), ("conv_b", 2), ("ln_g", 2), ("ln_b", 2), ("gq", 2), ("gkv", 1), ("b_gate", 32)):
    ROWS[_n] = _r
    _r += _c
NROWS = _r

TAB = {}
_r = 0
for _n, _c in (("ident", P), ("tri", 256), ("iota", CAP + 1), ("down", EG), ("code", 2 * ROUNDS * NQ),
               ("dist", 384), ("mask", 384), ("cos", T), ("sin", T), ("kcs", T), ("rep", P)):
    TAB[_n] = (_r, _r + _c)
    _r += _c
NTAB = _r
NKEEP = TAB["dist"][0]


def shape_tables():
    t = np.zeros((P, NTAB), np.float32)

    def put(name, a):
        t[:, TAB[name][0]:TAB[name][1]] = a

    p = np.arange(P)[:, None]
    put("ident", np.eye(P))
    q = np.concatenate([np.broadcast_to(p, (P, P)), np.broadcast_to(p + P, (P, T))], 1)
    s = np.concatenate([np.arange(P), np.arange(T)])[None, :]
    put("dist", np.where(q >= s, -(q - s), NEG))
    put("mask", np.where(q >= s, 0.0, NEG))
    put("tri", np.arange(T)[None, :] >= p)
    inv = (np.float32(10000.0) ** (-np.arange(0, 32, 2, dtype=np.float32) / np.float32(32))).astype(np.float32)
    ang = (np.arange(T, dtype=np.float32)[:, None] * inv[None, :]).astype(np.float32)
    cos, sin = np.cos(ang).T, np.sin(ang).T
    cos32, sin32 = np.concatenate([cos, cos]), np.concatenate([-sin, sin])
    put("cos", np.tile(cos32, (4, 1)))
    put("sin", np.tile(sin32, (4, 1)))
    put("kcs", np.concatenate([cos32, sin32, cos32, sin32]))
    put("rep", (p % 32) == (np.arange(P) % 32)[None, :])
    put("iota", np.arange(CAP + 1))
    put("down", np.arange(EG) - 100)
    r, qd = np.divmod(np.arange(ROUNDS * NQ), NQ)
    put("code", np.concatenate([(r + 1) * NE + qd * QUAD, qd]))
    return t


def after(engine, semaphore, value):
    if not isinstance(value, int) or value > 0:
        engine.wait_ge(semaphore, value)


def trunk_kernel(nc, A, out):
    ctx = ExitStack()
    with ctx:
        placed = {}

        def sb(name, shape, dt=F32):
            tensor = ctx.enter_context(nc.sbuf_tensor(name, shape, dt))
            placed[name] = nc.sbuf_base - 4 * int(np.prod(shape[1:]))
            return tensor

        def alias(name, of, at, n, dt):
            return nc.alloc_sbuf_tensor_at(name, [P, n], dt, offset=placed[of] + 4 * at)[:, :]

        names = """params_in ident_in tables_in norm_in norm2_in wmla_in bias_in router_in final_in
            sumsq xvar xroot xscaled params_ps params_sb half_params xt_ps x_hi x_split
            w_hi w_lo part_done proj_evac branch_ps
            conv_t conv_u conv_acc conv_out ln_sum ln_cent ln_sq ln_var ln_ve ln_root ln_rec ln_z ln_t yc_ready
            cq_sb cq_sq cq_sum cq_ve cq_root cq_rec cq_ready
            ckv_sb ckv_sq ckv_sum ckv_ve ckv_root ckv_rec ckv_ready krope_sb kpe_ps kpe_ready
            wrot_ready zeros_ready mla_ps mla_evac rope_mul
            fox_f fox_exp fox_ln fox_ready fox_ps cum_ready
            score_ps conv_a_sb logit_ready row_max neg_max prob_exp row_sum prob_ready pt_ps pt_sb pv_ps attn_ready
            gate_t merged tmp_mul merge_hi merge_split
            tile_done h_ready wr_ready h_sq h_var h_root h_rstd hs_hi hs_split hst_ps hst_sb_act hst_sb_dve logits_ps router_exp
            rank_ps total_ps sel_ready gather_ps xe_ready over_ready over_ps
            wselt_ps selt_sb gates_ps hid_ps hid_t hid_ready hidt_ps hidt_sb y_ps y_hi y_split o_ps o_free
            final_sq final_var final_root out_ready stored router_chain sel_chain step_chain x_chain over_chain
            slot_weight wsel_ready warm""".split()
        s = type("Semaphores", (), {n: ctx.enter_context(nc.semaphore(n)) for n in names})
        raw_in = [ctx.enter_context(nc.semaphore(f"raw_in{i}")) for i in range(NRAW)]
        x_tile_in = [ctx.enter_context(nc.semaphore(f"x_tile_in{i}")) for i in range(TT)]
        apart_in = [ctx.enter_context(nc.semaphore(f"apart_in{i}")) for i in range(5)]
        exp_in = [ctx.enter_context(nc.semaphore(f"exp_in{i}")) for i in range(12)]

        EX = sb("expert_slots", [P, 12 * SLOT])
        mixer_area = 6 * SLOT

        def ex(slot):
            return EX[:, slot * SLOT:(slot + 1) * SLOT]

        def area(at, n):
            return EX[:, mixer_area + at:mixer_area + at + n]

        RAW = [area(i * RAWW, RAWW) for i in range(NRAW)]
        kb_at = NRAW * RAWW
        KB = {b: area(kb_at + i * 1024, 1024).rearrange("p (h t) -> p h t", h=HEADS) for i, b in enumerate((3, 1, 0))}
        KPE = area(kb_at + 3072, 1024).rearrange("p (h t) -> p h t", h=HEADS)
        VMLA = area(kb_at + 4096, 512).rearrange("p (t c) -> p t c", t=TT)
        MH = alias("merged_hi", "expert_slots", mixer_area + kb_at, KD * T, F32R)
        ML = alias("merged_lo", "expert_slots", mixer_area + kb_at + KD * T, KD * T, F32R)

        XH = sb("act_hi", [P, KD * T], F32R)
        XL = sb("act_lo", [P, KD * T], F32R)
        WH = sb("w_high", [P, NPART * PARTW], F32R)
        WL = sb("w_low", [P, NPART * PARTW], F32R)
        H = sb("residual", [P, TT, D])
        M = sb("merged_t", [P, KD * T])
        SEL = sb("select", [P, TT, QUAD, CAP], F32R)
        SELT = sb("select_t", [P, 2, T], F32R)
        TABS = sb("shape_tables", [P, NKEEP])
        VEC = sb("vectors", [P, 272])
        SCR_N = 8516 + NTAB - NKEEP
        SCR = sb("scratch", [P, SCR_N])


        def carver(area_ap, size):
            used = [0]

            def carve(n, start=None):
                if start is not None:
                    used[0] = start
                a = area_ap[:, used[0]:used[0] + n]
                used[0] += n
                assert used[0] <= size, used[0]
                return a
            carve.used = lambda: used[0]
            return carve

        mx = carver(SCR[:, :], SCR_N)
        MTABS = mx(NTAB - NKEEP)

        def tab(name, rows=slice(0, P)):
            a, b = TAB[name]
            return TABS[rows, a:b] if b <= NKEEP else MTABS[rows, a - NKEEP:b - NKEEP]

        ident = tab("ident")
        tri = tab("tri")
        ones_mat = tri[:, P:2 * P]
        LNV = tab("cos")
        Q = {b: mx(512).rearrange("p (j t) -> p j t", j=2) for b in (3, 1, 0)}
        QPE = mx(T)
        VF = mx(2 * 260).rearrange("p (t c) -> p t c", t=TT)
        UPAD = mx(2 * 286).rearrange("p (j t) -> p j t", j=2)
        CACC = mx(512).rearrange("p (j t) -> p j t", j=2)
        YT = {b: mx(512).rearrange("p (j t) -> p j t", j=2) for b in (1, 3)}
        YT[2] = CACC
        YT[0] = Q[3]
        CQV = mx(512)
        CQ = CQV.rearrange("p (j t) -> p j t", j=2)
        VM = CQV.rearrange("p (t c) -> p t c", t=TT)
        PTS = mx(384)
        TMPA = mx(512)
        TMPB = mx(512)
        CBW = mx(1024)
        WUKV = CBW[:, 0:512]
        WROT = CBW[:, 512:768].rearrange("p (j h c) -> p j h c", j=2, h=HEADS)
        CKV = CBW[:, 768:1024]
        CB = CBW[0:HEADS, :].rearrange("p (h t) -> p h t", h=HEADS)
        PTS2 = mx(384)
        ROWP = PTS[:, 0:P]
        PRB = mx(768)
        PR = PRB.rearrange("p (h c) -> p h c", h=2)
        LNT = PRB[:, 0:512]
        WUQ = PRB.rearrange("p (j n) -> p j n", j=2)
        VMAP = {3: VMLA, 1: VF, 0: VM}

        mo = carver(SCR[:, :], SCR_N)
        WSEL = mo(512).rearrange("p (t e c) -> p t e c", t=TT, e=QUAD)
        HT_ = mo(512).rearrange("p (a f) -> p a f", a=2)
        TH = mo(512).rearrange("p (a f) -> p a f", a=2)
        HTT = mo(512).rearrange("p (a j c) -> p a j c", a=2, j=2)
        WR = mo(KD * 36).rearrange("p (k n) -> p k n", k=KD)
        LG = mo(72).rearrange("p (t n) -> p t n", t=TT)
        RB = mo(320)
        RB_O32 = 20 + 9 * 2 + 2 * 8 + 8 * 16 + 64
        RANK = mo(TT * (ROUNDS + 1) * NE).rearrange("p (t r) -> p t r", t=TT)
        WT = mo(TT * NE).rearrange("p (t e) -> p t e", t=TT)
        OV = mo(460)
        YOUTV = mo(2 * D)
        FGV = mo(SLOT)
        FG = FGV[:, 0:D]
        YOUT = YOUTV.rearrange("p (t d) -> p t d", t=TT)
        APART = [alias("apart_0", "w_high", NPART * PARTW - SLOT, SLOT, F32),
                 alias("apart_1", "w_low", NPART * PARTW - SLOT, SLOT, F32), YOUTV, FGV, mo(SLOT)]
        DOUBLE = len(APART)

        vv = carver(VEC[:, :], 272)
        PAR = vv(NROWS)
        HPAR = vv(4)
        G1 = vv(KD)
        G2 = vv(KD)
        BF = vv(HEADS)
        BR = vv(36)
        SS = vv(2)
        RS = vv(2)
        FW = vv(4 * 8)
        FLOG = vv(8).rearrange("p (t h) -> p t h", t=TT)
        CTOK = vv(8).rearrange("p (t h) -> p t h", t=TT)
        MAXV = vv(4)
        NMAX = vv(4)
        SUMV = vv(4)
        RECV = vv(4)
        WS = vv(2)
        WARM = vv(2)
        HGB = vv(32)
        LIST = sb("overflow_list", [1, 24], I32)

        def par(name, i=0):
            c = ROWS[name] + i
            return PAR[:, c:c + 1]

        bank = [ctx.enter_context(nc.psum_tensor(f"bank{i}", [P, 512], F32)) for i in range(8)]
        PA, PB, BRB, S0, S1, PT, PV, MISC = bank
        OUT = (S0, S1, PT, PV)
        HT = (PA, PB, BRB, MISC)

        x_v = A["x"][0].rearrange("(t p) d -> p t d", p=P)
        out_v = out[0].rearrange("(t p) d -> p t d", p=P)
        w_in_v = A["w_in"][0].rearrange("(p k) n -> p k n", k=KD)
        w_out_v = A["w_out"][0].rearrange("(m p) n -> p m n", p=P)
        e_gate = A["w_exp_gate"][0].rearrange("e (p k) f -> e p (k f)", k=KD)
        e_up = A["w_exp_up"][0].rearrange("e (p k) f -> e p (k f)", k=KD)
        e_down = A["w_exp_down"][0].rearrange("e (p j) d -> e p (j d)", j=2)

        def unit_dmas(n):
            raw = RAW[n % NRAW]
            if n < NIN:
                _, a, b = W_IN_UNITS[n]
                return [(raw[:, 0:8 * (b - a)].rearrange("p (k n) -> p k n", k=8), w_in_v[:, :, a:b])]
            if n < NIN + NGATE:
                g = n - NIN
                i, u = BRANCHES[g // 4], g % 4
                cols = slice(u * 256, u * 256 + 256)
                return [(raw[:, 0:2048].rearrange("p (k n) -> p k n", k=8),
                         A["w_gate"][0, i].rearrange("(p k) n -> p k n", k=8)[:, :, cols]),
                        (raw[:, 2048:2560].rearrange("p (j n) -> p j n", j=2),
                         A["w_branch"][0, i].rearrange("(j p) n -> p j n", p=P)[:, :, cols])]
            u = n - NIN - NGATE
            return [(raw[:, 0:2048].rearrange("p (m n) -> p m n", m=2), w_out_v[:, 2 * u:2 * u + 2, :])]

        def raw_count(n):
            return sum(16 * (2 if NIN <= m < NIN + NGATE else 1) for m in range(n % NRAW, n + 1, NRAW))

        def part(w, q, cols=slice(0, 1024)):
            at = (q % NPART) * PARTW
            return w[:, at + cols.start:at + cols.stop]

        def part_copies(q):
            n, h = divmod(q, 2)
            raw = RAW[n % NRAW]
            if n >= NIN + NGATE:
                return [((0, 1024, None), raw[:, h * 1024:(h + 1) * 1024])]
            if n < NIN and W_IN_UNITS[n][0].endswith("_v"):
                w = 4 * (W_IN_UNITS[n][2] - W_IN_UNITS[n][1])
                return [((0, w, None), raw[:, h * w:(h + 1) * w])]
            if n < NIN and W_IN_UNITS[n][0] == "ckv":
                r = raw[:, 0:8 * 160].rearrange("p (k n) -> p k n", k=8)
                if h == 0:
                    return [((0, 128, 8), r[:, :, 0:128])]
                return [((0, 64, 8), r[:, :, 0:64]), ((64, 96, 8), r[:, :, 128:160]), ((96, 112, 8), r[:, :, 144:160]),
                        ((112, 128, 8), r[:, :, 128:144])]
            r = raw[:, 0:2048].rearrange("p (k n) -> p k n", k=8)
            return [((0, 128, 8), r[:, :, h * 128:(h + 1) * 128])]

        def part_slice(w, q, where):
            a, b, k = where
            if k is None:
                return part(w, q, slice(a, b))
            return part(w, q).rearrange("p (k n) -> p k n", k=k)[:, :, a:b]

        slot_plan = [(pair, kind, e) for pair, kind in ((0, 0), (0, 1), (1, 0), (1, 1), (0, 2), (1, 2)) for e in range(2)]

        def expert_slot(parity, slot):
            return APART[slot] if parity == 0 and slot < DOUBLE else ex(slot)

        def slot_signal(parity, slot):
            return apart_in[slot] if parity == 0 and slot < DOUBLE else exp_in[slot]

        def y_part(w, pair, half):
            at = pair * D + half * 512
            return w[:, at:at + 512]

        PAIRS = [(3, 0), (3, 1), (1, 0), (1, 1), (0, 0), (0, 1)]

        block = ctx.enter_context(nc.Block())

        def f32(ap):
            return ap.bitcast(F32)

        @block.sync
        def _(sp):
            for t in range(TT):
                sp.dma_start(H[:, t, :], x_v[:, t, :]).then_inc(x_tile_in[t], 16)

            def load_unit(n):
                if n >= NRAW:
                    m = n - NRAW
                    sp.wait_ge(s.w_lo, 2 * m + 2)
                    if NIN <= m < NIN + NGATE:
                        sp.wait_ge(s.branch_ps, m - NIN + 1)
                for dst, src in unit_dmas(n):
                    sp.dma_start(dst, src).then_inc(raw_in[n % NRAW], 16)

            def load_expert(q, slot, parity):
                pair, kind, e = slot_plan[slot]
                src = (e_gate, e_up, e_down)[kind]
                sp.dma_start(expert_slot(parity, slot), src[q * QUAD + 2 * pair + e]).then_inc(slot_signal(parity, slot), 16)

            def rows(name):
                return ROWP[ROWS[name]:ROWS[name] + {"conv_w": 62, "b_gate": 32, "gkv": 1}.get(name, 2), :]

            for n in range(UNITS):
                load_unit(n)
                if n == NRAW - 1:
                    sp.dma_start(rows("conv_w"), A["conv_w"][0].rearrange("k (j p) -> (k j) p", p=P)).then_inc(s.params_in, 16)
                    for name, key in (("conv_b", "conv_b"), ("ln_g", "conv_ln_g"), ("ln_b", "conv_ln_b"), ("gq", "mla_gq"),
                                      ("gkv", "mla_gkv")):
                        sp.dma_start(rows(name), A[key][0].rearrange("(j p) -> j p", p=P)).then_inc(s.params_in, 16)
                    sp.dma_start(rows("b_gate"), A["b_gate"][0].rearrange("i (m p) -> (i m) p", p=P)).then_inc(s.params_in, 16)
                    sp.dma_start(TABS[:, P:NKEEP], A["tables"][:, P:NKEEP]).then_inc(s.tables_in, 16)
                    sp.dma_start(MTABS, A["tables"][:, NKEEP:NTAB]).then_inc(s.tables_in, 16)
                    sp.dma_start(G2, A["norm2_g"][0].rearrange("(p k) -> p k", k=KD)).then_inc(s.norm2_in, 16)
                    for j in range(2):
                        wuq = A["mla_wuq"][0, j * P:(j + 1) * P, :].rearrange("p (h c) -> p h c", h=HEADS)
                        sp.dma_start(WUQ[:, j, 0:256].rearrange("p (h c) -> p h c", h=HEADS), wuq[:, :, 0:64]).then_inc(s.wmla_in, 16)
                        sp.dma_start(WUQ[:, j, 256:384].rearrange("p (h c) -> p h c", h=HEADS), wuq[:, :, 64:96]).then_inc(s.wmla_in, 16)
                    wukv = A["mla_wukv"][0].rearrange("p (h a c) -> p h a c", h=HEADS, a=2)
                    for a in range(2):
                        sp.dma_start(WUKV[:, a * 256:(a + 1) * 256].rearrange("p (h c) -> p h c", h=HEADS), wukv[:, :, a, :])\
                            .then_inc(s.wmla_in, 16)
                    sp.dma_start(BF, A["b_forget"][0].partition_broadcast(P)).then_inc(s.bias_in, 16)
                    sp.dma_start(BR[:, 0:4], A["b_router_group"][0].partition_broadcast(P)).then_inc(s.bias_in, 16)
                    sp.dma_start(BR[:, 4:36], A["b_router_expert"][0].partition_broadcast(P)).then_inc(s.bias_in, 16)
                if n == PREFETCH_AT:
                    for slot in range(6):
                        if slot < DOUBLE:
                            load_expert(1, slot, 1)
                        else:
                            load_expert(0, slot, 0)
            sp.wait_ge(s.branch_ps, NGATE)
            sp.wait_ge(s.merged, NGATE - 4)
            sp.dma_start(WR[:, :, 0:NG], A["w_router_group"][0].rearrange("(p k) n -> p k n", k=KD)).then_inc(s.router_in, 16)
            sp.dma_start(WR[:, :, NG:36], A["w_router_expert"][0].rearrange("(p k) n -> p k n", k=KD)).then_inc(s.router_in, 16)
            for slot in range(2, DOUBLE):
                load_expert(0, slot, 0)
            sp.wait_ge(s.w_lo, 2 * UNITS)
            for slot in range(6, 9):
                load_expert(0, slot, 0)
            sp.wait_ge(s.tile_done, TT)
            for slot in (0, 1, 9, 10, 11):
                load_expert(0, slot, 0)

            def used(n, slot):
                pair, kind, _ = slot_plan[slot]
                if kind < 2:
                    sp.wait_ge((s.gates_ps, s.hid_ps)[kind], n * 2 + 1 + pair)
                else:
                    sp.wait_ge(s.y_ps, n * 4 + 2 + 2 * pair)

            def refill(n, parity, doubled=True):
                if doubled:
                    for slot in range(DOUBLE):
                        used(n, slot)
                        load_expert(n + 2, slot, parity)
                for slot in range(DOUBLE, 12):
                    used(n, slot)
                    load_expert(n + 1, slot, parity)

            with sp.Fori(0, (NQ - 2) // 2) as i:
                refill(i * 2, 0)
                refill(i * 2 + 1, 1)
            refill(NQ - 2, 0, doubled=False)
            sp.wait_ge(s.over_ready, 1)
            count = sp.value_load(LIST[0:1, 0:1], min_val=0, max_val=MAXOVER)
            with sp.If(count > 0):
                with sp.Fori(0, count) as j:
                    q = sp.value_load(LIST[0:1, bass.ds(j + 9, 1)], min_val=0, max_val=NQ - 1)
                    for slot in range(12):
                        used(j + NQ - 1, slot)
                        load_expert(q, slot, 1)
            sp.end_ifs()
            sp.dma_start(FG, A["final_g"].partition_broadcast(P)).then_inc(s.final_in, 16)
            for t in range(TT):
                sp.wait_ge(s.out_ready, t + 1)
                sp.dma_start(out_v[:, t, :], YOUT[:, t, :]).then_inc(s.stored, 16)
            sp.wait_ge(s.stored, 16 * TT)

        @block.gpsimd
        def _(pool):
            nc.gpsimd.memset(WARM, 0.0).then_inc(s.zeros_ready, 1)
            for b in (3, 1, 0):
                nc.gpsimd.memset(KB[b], 0.0).then_inc(s.zeros_ready, 1)
            nc.gpsimd.memset(KPE, 0.0).then_inc(s.zeros_ready, 1)
            nc.gpsimd.memset(UPAD[:, :, 0:30], 0.0).then_inc(s.zeros_ready, 1)
            pool.wait_ge(s.wmla_in, 96)
            wq = WUQ[:, :, 256:384].rearrange("p j (h c) -> p j h c", h=HEADS)
            for j in range(2):
                nc.gpsimd.tensor_copy(WROT[:, j, :, 0:16], wq[:, j, :, 16:32]).then_inc(s.wrot_ready, 1)
                nc.gpsimd.tensor_copy(WROT[:, j, :, 16:32], wq[:, j, :, 0:16]).then_inc(s.wrot_ready, 1)

        @block.scalar
        def _(act):
            act.dma_start(ident, A["tables"][:, 0:P]).then_inc(s.ident_in, 16)
            act.dma_start(G1, A["norm1_g"][0].rearrange("(p k) -> p k", k=KD)).then_inc(s.norm_in, 16)
            def warm_roots():
                nc.scalar.activation(WARM[:, 1:2], WARM[:, 0:1], ACT.Sqrt).then_inc(s.warm, 1)

            act.wait_ge(s.zeros_ready, 1)
            warm_roots()
            for t in range(TT):
                act.wait_ge(x_tile_in[t], 16)
                nc.scalar.activation(M[:, t * D:(t + 1) * D], H[:, t, :], ACT.Square, accum_out=SS[:, t:t + 1]).then_inc(s.sumsq, 1)
            for t in range(TT):
                act.wait_ge(s.xvar, t + 1)
                nc.scalar.activation(RS[:, t:t + 1], SS[:, t:t + 1], ACT.Sqrt).then_inc(s.xroot, 1)
            def split_hi(q):
                n = q // 2
                act.wait_ge(raw_in[n % NRAW], raw_count(n))
                if q >= NPART:
                    act.wait_ge(s.part_done, q - NPART + 1)
                    act.wait_ge(s.w_lo, q - NPART + 1)
                for where, raw in part_copies(q):
                    ins = nc.scalar.activation(part_slice(WH, q, where), raw, ACT.Copy)
                ins.then_inc(s.w_hi, 1)

            split_hi(0)
            act.wait_ge(s.norm_in, 16)
            for b in range(4):
                act.wait_ge(s.xt_ps, b + 1)
                for k in (2 * b, 2 * b + 1):
                    nc.scalar.activation(XH[:, k * T:(k + 1) * T], bank[4 + b][:, (k % 2) * T:(k % 2 + 1) * T], ACT.Copy,
                                         scale=G1[:, k:k + 1]).then_inc(s.x_hi, 1)

            def flat(ap):
                return ap.rearrange("p j t -> p (j t)")

            def exp_pair(p):
                b = PAIRS[p][0]
                scale = (96.0 if b == 3 else 64.0) ** -0.5
                act.wait_ge(s.neg_max, p + 1)
                for h in range(2):
                    for qt in range(2):
                        c = slice(0, P) if qt == 0 else slice(P, 384)
                        i = 2 * h + qt
                        nc.scalar.activation(PR[:, h, c], PR[:, h, c], ACT.Exp, bias=NMAX[:, i:i + 1], scale=scale,
                                             accum_out=SUMV[:, i:i + 1]).then_inc(s.prob_exp, 1)

            def attend(p):
                b, hp = PAIRS[p]
                for h in range(2):
                    act.wait_ge(s.pt_ps, 2 * p + h + 1)
                    if p:
                        act.wait_ge(s.pv_ps, 2 * p - 1 + h)
                    nc.scalar.activation((PTS, PTS2)[h], (PT, MISC)[h][:, 0:384], ACT.Copy).then_inc(s.pt_sb, 1)
                act.wait_ge(s.pv_ps, 2 * p + 2)
                nc.scalar.activation(YT[b][:, hp, :], PV[:, 0:T], ACT.Copy).then_inc(s.attn_ready, 1)

            def projection(n):
                kind = W_IN_UNITS[n][0]
                pb = (PA, PB)[n % 2]
                b = 1 if kind.startswith("fox") else 0
                act.wait_ge(s.part_done, 2 * n + 2)
                if kind.endswith("q"):
                    nc.scalar.activation(flat(Q[b]), pb[:, :], ACT.Copy).then_inc(s.proj_evac, 1)
                else:
                    act.wait_ge(s.zeros_ready, 6)
                    for h in range(HEADS):
                        r = slice(64 * (h % 2), 64 * (h % 2) + 64)
                        ins = nc.scalar.activation(KB[b][r, h, :], pb[r, (h // 2) * T:(h // 2 + 1) * T], ACT.Copy)
                    ins.then_inc(s.proj_evac, 1)

            def merged_hi(m):
                act.wait_ge(s.merged, NGATE - 8 + m // 2 + 1)
                for i in (m, m + 1):
                    nc.scalar.activation(MH[:, i * T:(i + 1) * T], M[:, i * T:(i + 1) * T], ACT.Copy, scale=0.5)\
                        .then_inc(s.merge_hi, 1)

            split_hi(1)
            for n in range(NIN + NGATE + 1):
                split_hi(2 * n + 2)
                g = n - 1 - NIN
                if g >= 0:
                    act.wait_ge(s.part_done, 2 * (NIN + g) + 2)
                    if g >= 1:
                        act.wait_ge(s.tmp_mul, g)
                    i, u = BRANCHES[g // 4], g % 4
                    for m in range(2):
                        c = i * 8 + u * 2 + m
                        nc.scalar.activation(TMPB[:, m * T:(m + 1) * T], (PA, PB)[g % 2][:, m * T:(m + 1) * T], ACT.Tanh,
                                             bias=HGB[:, c:c + 1], scale=0.5).then_inc(s.gate_t, 1)
                if n == 1:
                    act.wait_ge(s.part_done, 2)
                    nc.scalar.activation(flat(CQ), PA[:, :], ACT.Copy).then_inc(s.cq_sb, 1)
                    nc.scalar.activation(TMPA, PA[:, :], ACT.Square).then_inc(s.cq_sq, 1)
                if n == 2:
                    act.wait_ge(s.part_done, 4)
                    nc.scalar.activation(CKV, PB[:, 0:T], ACT.Copy).then_inc(s.ckv_sb, 1)
                    nc.scalar.activation(TMPB[:, 0:T], PB[:, 0:T], ACT.Square).then_inc(s.ckv_sq, 1)
                if n == 3:
                    act.wait_ge(s.cq_ve, 1)
                    nc.scalar.activation(TMPA[:, 0:T], TMPA[:, 0:T], ACT.Sqrt).then_inc(s.cq_root, 1)
                    act.wait_ge(s.ckv_ve, 1)
                    nc.scalar.activation(TMPB[:, 0:T], TMPB[:, 0:T], ACT.Sqrt).then_inc(s.ckv_root, 1)
                    act.wait_ge(s.fox_f, 1)
                    nc.scalar.activation(FW[:, 16:24], FW[:, 8:16], ACT.Exp, scale=-1.0).then_inc(s.fox_exp, 1)
                    act.wait_ge(s.fox_exp, 1)
                    nc.scalar.activation(FW[:, 24:32], FW[:, 16:24], ACT.Ln, bias=1.0).then_inc(s.fox_ln, 1)
                if n in (4, 5, 8, 9):
                    projection(n - 1)
                if n == 6:
                    act.wait_ge(s.part_done, 12)
                    act.wait_ge(s.kpe_ps, 1)
                    nc.scalar.activation(TMPB, PB[:, :], ACT.Copy).then_inc(s.conv_a_sb, 1)
                if n == 7:
                    act.wait_ge(s.part_done, 14)
                    act.wait_ge(s.mla_evac, 2)
                    nc.scalar.activation(TMPA, PA[:, :], ACT.Tanh, scale=0.5).then_inc(s.conv_t, 1)
                if n == 10:
                    act.wait_ge(s.part_done, 20)
                    nc.scalar.activation(VM[:, 0, :], PB[:, 0:T], ACT.Copy)
                    nc.scalar.activation(VM[:, 1, :], MISC[:, 0:T], ACT.Copy).then_inc(s.proj_evac, 1)
                p = (n - FIRST_SCORES) // 2
                if (n - FIRST_SCORES) % 2 == 0 and 1 <= p <= len(PAIRS):
                    attend(p - 1)
                split_hi(2 * n + 3)
                if (n - FIRST_SCORES) % 2 == 0 and 0 <= p < len(PAIRS):
                    exp_pair(p)
                if g - 1 >= NGATE - 4:
                    merged_hi(2 * ((g - 1) % 4))
                if n == LN_AT + 1:
                    act.wait_ge(s.ln_cent, 1)
                    nc.scalar.activation(LNT, flat(CACC), ACT.Square).then_inc(s.ln_sq, 1)
                if n == LN_AT + 2:
                    act.wait_ge(s.ln_ve, 1)
                    nc.scalar.activation(LNV, LNV, ACT.Sqrt).then_inc(s.ln_root, 1)
                    act.wait_ge(s.ln_z, 1)
                    nc.scalar.activation(LNT, flat(CACC), ACT.Tanh).then_inc(s.ln_t, 1)
            merged_hi(KD - 2)
            for q in range(2 * (NIN + NGATE) + 4, 2 * UNITS):
                split_hi(q)
            act.wait_ge(s.warm, 1)
            warm_roots()
            for t in range(TT):
                act.wait_ge(s.h_ready, 2 * t + 2)
                nc.scalar.activation(XL[:, t * D:(t + 1) * D], H[:, t, :], ACT.Square, accum_out=SS[:, t:t + 1])\
                    .then_inc(s.h_sq, 1)
                act.wait_ge(s.hst_ps, 2 * t + 1)
                nc.scalar.activation(M[:, 2 * t * 512:(2 * t + 1) * 512], HT[2 * t][:, :], ACT.Copy).then_inc(s.hst_sb_act, 1)
                act.wait_ge(s.h_var, t + 1)
                nc.scalar.activation(RS[:, t:t + 1], SS[:, t:t + 1], ACT.Sqrt).then_inc(s.h_root, 1)
            for t in range(TT):
                act.wait_ge(s.h_rstd, t + 1)
                nc.scalar.activation(XH[:, t * D:(t + 1) * D], H[:, t, :], ACT.Copy, scale=RS[:, t:t + 1]).then_inc(s.hs_hi, 1)
            act.wait_ge(s.router_exp, 1)
            nc.scalar.activation(RB[:, 8:16], RB[:, 0:8], ACT.Exp).then_inc(s.router_exp, 1)
            act.wait_ge(s.router_exp, 3)
            nc.scalar.activation(RB[:, 18:20], RB[:, 16:18], ACT.Exp).then_inc(s.router_exp, 1)

            def step(n):
                for pair in range(2):
                    after(act, s.hid_ps, n * 2 + pair + 1)
                    after(act, s.hid_ready, n * 2 + pair)
                    nc.scalar.activation(TH[:, pair, :], bank[0 + pair][:, 0:FF], ACT.Tanh, scale=0.5)\
                        .then_inc(s.hid_t, 1)
                for pair in range(2):
                    for half in range(2):
                        after(act, s.y_ps, n * 4 + 2 * pair + half + 1)
                        after(act, s.o_ps, n * 4)
                        after(act, s.selt_sb, n * 2 + pair + 1)
                        nc.scalar.activation(y_part(WH, pair, half), bank[2 + half][:, :], ACT.Copy,
                                             scale=WS[:, pair:pair + 1]).then_inc(s.y_hi, 1)

            step(0)
            with act.Fori(1, NQ) as i:
                step(i)
            act.wait_ge(s.over_ready, 1)
            count = act.value_load(LIST[0:1, 0:1], min_val=0, max_val=MAXOVER)
            with act.If(count > 0):
                with act.Fori(0, count) as j:
                    step(j + NQ)
            act.end_ifs()
            act.wait_ge(s.warm, 2)
            warm_roots()
            for t in range(TT):
                act.wait_ge(s.o_free, count * 4 + (4 * NQ + 2 * t))
                nc.scalar.activation(YOUT[:, t, :], H[:, t, :], ACT.Square, accum_out=SS[:, t:t + 1])\
                    .then_inc(s.final_sq, 1)
            for t in range(TT):
                act.wait_ge(s.final_var, t + 1)
                nc.scalar.activation(RS[:, t:t + 1], SS[:, t:t + 1], ACT.Sqrt).then_inc(s.final_root, 1)

        @block.vector
        def _(dve):
            V = nc.vector
            chain = [0]

            def link(ins):
                chain[0] += 1
                ins.then_inc(s.x_chain, 1)
                dve.wait_ge(s.x_chain, chain[0])

            for t in range(TT):
                dve.wait_ge(s.sumsq, t + 1)
                V.tensor_scalar(SS[:, t:t + 1], SS[:, t:t + 1], 1.0 / D, EPS, ALU.mult, ALU.add).then_inc(s.xvar, 1)
            for t in range(TT):
                dve.wait_ge(s.xroot, t + 1)
                link(V.reciprocal(RS[:, t:t + 1], RS[:, t:t + 1]))
                V.tensor_scalar(M[:, t * D:(t + 1) * D], H[:, t, :], RS[:, t:t + 1], None, ALU.mult).then_inc(s.xscaled, 1)

            def split_lo(q):
                dve.wait_ge(s.w_hi, q + 1)
                for where, raw in part_copies(q):
                    ins = V.tensor_tensor(part_slice(WL, q, where), raw, f32(part_slice(WH, q, where)), ALU.subtract)
                ins.then_inc(s.w_lo, 1)

            split_lo(0)
            for k in range(KD):
                dve.wait_ge(s.x_hi, 2 * (k // 2) + 2)
                V.scalar_tensor_tensor(XL[:, k * T:(k + 1) * T], bank[4 + k // 2][:, (k % 2) * T:(k % 2 + 1) * T],
                                       G1[:, k:k + 1], f32(XH[:, k * T:(k + 1) * T]), ALU.mult, ALU.subtract)\
                    .then_inc(s.x_split, 1)

            steps = [0]

            def conv_steps(count):
                for _ in range(count):
                    k, j = divmod(steps[0], 2)
                    if k >= CONV_K:
                        return
                    if steps[0] >= 2:
                        dve.wait_ge(s.conv_acc, steps[0] - 1)
                    w = PAR[:, ROWS["conv_w"] + 2 * k + j:ROWS["conv_w"] + 2 * k + j + 1]
                    src = UPAD[:, j, k:k + T]
                    if k == 0:
                        ins = V.tensor_scalar(CACC[:, j, :], src, w, None, ALU.mult)
                    else:
                        ins = V.scalar_tensor_tensor(CACC[:, j, :], src, w, CACC[:, j, :], ALU.mult, ALU.add)
                    ins.then_inc(s.conv_acc, 1)
                    steps[0] += 1

            def logits(p):
                b, hp = PAIRS[p]
                scale = (96.0 if b == 3 else 64.0) ** -0.5
                dve.wait_ge(s.score_ps, p + 1)
                if p:
                    dve.wait_ge(s.pt_ps, 2 * p)
                else:
                    dve.wait_ge(s.mla_ps, 4)
                for qt in range(2):
                    for h in range(2):
                        c = slice(0, P) if qt == 0 else slice(P, 384)
                        n = P if qt == 0 else T
                        sc = (S0, S1)[qt][:, h * n:(h + 1) * n]
                        head = 2 * hp + h
                        if b == 0:
                            slope = 2.0 ** (-8.0 * (head + 1) / HEADS)
                            V.scalar_tensor_tensor(PR[:, h, c], tab("dist")[:, c], slope / scale, sc, ALU.mult, ALU.add)\
                                .then_inc(s.logit_ready, 1)
                        elif b == 1:
                            V.scalar_tensor_tensor(PR[:, h, c], sc, CTOK[:, qt, head:head + 1], tab("mask")[:, c],
                                                   ALU.add, ALU.add).then_inc(s.logit_ready, 1)
                        else:
                            V.tensor_tensor(PR[:, h, c], sc, tab("mask")[:, c], ALU.add).then_inc(s.logit_ready, 1)
                mv = MAXV.rearrange("p (h q) -> p h q", h=2)
                for qt in range(2):
                    dve.wait_ge(s.logit_ready, 4 * p + 2 * qt + 2)
                    c = slice(0, P) if qt == 0 else slice(P, 384)
                    V.reduce_max(mv[:, :, qt:qt + 1], PR[:, :, c], AXX).then_inc(s.row_max, 1)
                dve.wait_ge(s.row_max, 2 * p + 2)
                V.tensor_scalar(NMAX, MAXV, -scale, None, ALU.mult).then_inc(s.neg_max, 1)

            def normalise(p):
                dve.wait_ge(s.prob_exp, 4 * p + 4)
                link(V.reciprocal(RECV, SUMV))
                for h in range(2):
                    for qt in range(2):
                        c = slice(0, P) if qt == 0 else slice(P, 384)
                        i = 2 * h + qt
                        ins = V.tensor_scalar(PR[:, h, c], PR[:, h, c], RECV[:, i:i + 1], None, ALU.mult)
                    ins.then_inc(s.prob_ready, 1)

            def merge(g):
                dve.wait_ge(s.gate_t, 2 * g + 2)
                dve.wait_ge(s.branch_ps, g + 1)
                mc = M[:, (g % 4) * 512:(g % 4 + 1) * 512]
                if g < 4:
                    V.scalar_tensor_tensor(mc, TMPB, 1.0, BRB[:, :], ALU.add, ALU.mult).then_inc(s.tmp_mul, 1)
                else:
                    if g > 4:
                        dve.wait_ge(s.merged, g - 4)
                    if g + NIN > LN_AT + 1:
                        dve.wait_ge(s.yc_ready, 1)
                    V.scalar_tensor_tensor(TMPA, TMPB, 1.0, BRB[:, :], ALU.add, ALU.mult).then_inc(s.tmp_mul, 1)
                    dve.wait_ge(s.tmp_mul, g + 1)
                    V.tensor_tensor(mc, mc, TMPA, ALU.add).then_inc(s.merged, 1)

            def merged_lo(m):
                for i in (m, m + 1):
                    dve.wait_ge(s.merge_hi, i + 1)
                    V.scalar_tensor_tensor(ML[:, i * T:(i + 1) * T], M[:, i * T:(i + 1) * T], 0.5,
                                           f32(MH[:, i * T:(i + 1) * T]), ALU.mult, ALU.subtract).then_inc(s.merge_split, 1)

            split_lo(1)
            for n in range(NIN + NGATE + 1):
                split_lo(2 * n + 2)
                if n - 1 - NIN >= 0:
                    merge(n - 1 - NIN)
                if n == 2:
                    dve.wait_ge(s.params_ps, 1)
                    V.tensor_copy(PAR, MISC[:, 0:NROWS]).then_inc(s.params_sb, 1)
                    dve.wait_ge(s.params_sb, 1)
                    V.tensor_scalar(HPAR, PAR[:, ROWS["ln_g"]:ROWS["ln_g"] + 4], 0.5, None, ALU.mult).then_inc(s.half_params, 1)
                    V.tensor_scalar(HGB, PAR[:, ROWS["b_gate"]:ROWS["b_gate"] + 32], 0.5, None, ALU.mult).then_inc(s.half_params, 1)
                if n == 3:
                    dve.wait_ge(s.cq_sum, 1)
                    dve.wait_ge(s.ckv_sum, 1)
                    V.tensor_scalar(TMPA[:, 0:T], MISC[:, 0:T], 1.0 / 256, EPS, ALU.mult, ALU.add).then_inc(s.cq_ve, 1)
                    V.tensor_scalar(TMPB[:, 0:T], MISC[:, T:2 * T], 1.0 / 128, EPS, ALU.mult, ALU.add).then_inc(s.ckv_ve, 1)
                    dve.wait_ge(s.part_done, 6)
                    for t in range(TT):
                        link(V.tensor_copy(VF[:, t, :], (PA, S0)[t][:, 0:260]))
                    dve.wait_ge(s.bias_in, 48)
                    fw = FW[:, 0:8].rearrange("p (t h) -> p t h", t=TT)
                    link(V.tensor_tensor(fw, VF[:, :, 256:260], BF.unsqueeze(1).to_broadcast([P, TT, HEADS]), ALU.add))
                    V.scalar_tensor_tensor(FW[:, 8:16], FW[:, 0:8], -1.0, FW[:, 0:8], ALU.mult, ALU.max).then_inc(s.fox_f, 1)
                    dve.wait_ge(s.cq_root, 1)
                    link(V.reciprocal(TMPA[:, 0:T], TMPA[:, 0:T]))
                    for j in range(2):
                        V.scalar_tensor_tensor(CQ[:, j, :], CQ[:, j, :], par("gq", j), TMPA[:, 0:T], ALU.mult, ALU.mult)\
                            .then_inc(s.cq_ready, 1)
                    dve.wait_ge(s.ckv_root, 1)
                    link(V.reciprocal(TMPB[:, 0:T], TMPB[:, 0:T]))
                    V.scalar_tensor_tensor(CKV, CKV, par("gkv"), TMPB[:, 0:T], ALU.mult, ALU.mult).then_inc(s.ckv_ready, 1)
                if n == 2:
                    dve.wait_ge(s.part_done, 4)
                    dve.wait_ge(s.ckv_sq, 1)
                    dve.wait_ge(s.tables_in, 32)
                    V.tensor_tensor(TMPB[64:128, T:2 * T], PB[64:128, T:2 * T],
                                    tab("kcs", slice(64, 128)), ALU.mult).then_inc(s.krope_sb, 1)
                if n == 4:
                    dve.wait_ge(s.fox_ln, 1)
                    V.scalar_tensor_tensor(FLOG.rearrange("p t h -> p (t h)"), FW[:, 0:8], 0.0, FW[:, 24:32], ALU.min,
                                           ALU.subtract).then_inc(s.fox_ready, 1)
                    dve.wait_ge(s.mla_ps, 1)
                    V.tensor_copy(Q[3].rearrange("p j t -> p (j t)"), S1[:, :]).then_inc(s.mla_evac, 1)
                    dve.wait_ge(s.mla_ps, 2)
                    dve.wait_ge(s.cq_ready, 2)
                    V.tensor_tensor(TMPA[:, 0:T], PT[:, 0:T], tab("cos"), ALU.mult).then_inc(s.rope_mul, 1)
                    V.tensor_tensor(TMPA[:, T:2 * T], PT[:, T:2 * T], tab("sin"), ALU.mult).then_inc(s.rope_mul, 1)
                    dve.wait_ge(s.rope_mul, 2)
                    V.tensor_tensor(QPE, TMPA[:, 0:T], TMPA[:, T:2 * T], ALU.add).then_inc(s.mla_evac, 1)
                    dve.wait_ge(s.mla_ps, 3)
                    dve.wait_ge(s.zeros_ready, 6)
                    for h in range(HEADS):
                        r = slice(64 * (h % 2), 64 * (h % 2) + 64)
                        ins = V.tensor_copy(KB[3][r, h, :], PV[r, (h // 2) * T:(h // 2 + 1) * T])
                    ins.then_inc(s.mla_evac, 1)
                    dve.wait_ge(s.mla_ps, 4)
                    V.tensor_copy(VMLA.rearrange("p t c -> p (t c)"), BRB[:, :]).then_inc(s.mla_evac, 1)
                if n == 5:
                    dve.wait_ge(s.kpe_ps, 1)
                    for h in range(HEADS):
                        r = slice(32 * h, 32 * h + 32)
                        ins = V.tensor_copy(KPE[r, h, :], S1[r, 0:T])
                    ins.then_inc(s.kpe_ready, 1)
                    dve.wait_ge(s.fox_ps, 1)
                    V.tensor_scalar(CTOK.rearrange("p t h -> p (t h)"), MISC[:, 0:8], 8.0, None, ALU.mult)\
                        .then_inc(s.cum_ready, 1)
                    for h in range(HEADS):
                        ins = V.tensor_scalar(CB[:, h, :], MISC[0:HEADS, T:2 * T], TABS[0:HEADS, h:h + 1], -8.0, ALU.mult, ALU.mult)
                    ins.then_inc(s.cum_ready, 1)
                if n == 7:
                    dve.wait_ge(s.conv_t, 1)
                    dve.wait_ge(s.conv_a_sb, 1)
                    V.scalar_tensor_tensor(UPAD[:, :, 30:286], TMPA.rearrange("p (j t) -> p j t", j=2), 1.0,
                                           TMPB.rearrange("p (j t) -> p j t", j=2), ALU.add, ALU.mult).then_inc(s.conv_u, 1)
                    dve.wait_ge(s.conv_u, 1)
                p = (n - FIRST_SCORES) // 2
                scoring = (n - FIRST_SCORES) % 2 == 0 and 0 <= p < len(PAIRS)
                if scoring:
                    logits(p)
                split_lo(2 * n + 3)
                if scoring:
                    normalise(p)
                if CONV_FROM <= n < LN_AT:
                    conv_steps(CONV_TAPS)
                if n == LN_AT:
                    dve.wait_ge(s.conv_acc, 2 * CONV_K)
                    for j in range(2):
                        V.tensor_scalar(CACC[:, j, :], CACC[:, j, :], 0.5, par("conv_b", j), ALU.mult, ALU.add)\
                            .then_inc(s.conv_out, 1)
                if n == LN_AT + 1:
                    dve.wait_ge(s.ln_sum, 1)
                    V.scalar_tensor_tensor(CACC, MISC[:, 0:T].unsqueeze(1).to_broadcast([P, 2, T]), -1.0 / 256, CACC,
                                           ALU.mult, ALU.add).then_inc(s.ln_cent, 1)
                if n - 2 - NIN >= NGATE - 4:
                    merged_lo(2 * ((n - 2 - NIN) % 4))
                if n == LN_AT + 2:
                    dve.wait_ge(s.ln_var, 1)
                    V.tensor_scalar(LNV, MISC[:, 0:T], 1.0 / 256, EPS, ALU.mult, ALU.add).then_inc(s.ln_ve, 1)
                    dve.wait_ge(s.ln_root, 1)
                    link(V.reciprocal(LNV, LNV))
                    link(V.tensor_tensor(CACC, CACC, LNV.unsqueeze(1).to_broadcast([P, 2, T]), ALU.mult))
                    for j in range(2):
                        ins = V.tensor_scalar(CACC[:, j, :], CACC[:, j, :], HPAR[:, j:j + 1], HPAR[:, 2 + j:3 + j], ALU.mult, ALU.add)
                    ins.then_inc(s.ln_z, 1)
                    dve.wait_ge(s.ln_t, 1)
                    V.scalar_tensor_tensor(YT[2].rearrange("p j t -> p (j t)"), LNT, 1.0, CACC.rearrange("p j t -> p (j t)"),
                                           ALU.add, ALU.mult).then_inc(s.yc_ready, 1)
            merged_lo(KD - 2)
            for q in range(2 * (NIN + NGATE) + 4, 2 * UNITS):
                split_lo(q)
            for t in range(TT):
                dve.wait_ge(s.tile_done, t + 1)
                for half in range(2):
                    c = slice(half * 512, half * 512 + 512)
                    V.tensor_tensor(H[:, t, c], H[:, t, c], OUT[2 * t + half][:, :], ALU.add).then_inc(s.h_ready, 1)
            dve.wait_ge(s.router_in, 32)
            dve.wait_ge(s.norm2_in, 16)
            V.tensor_tensor(WR, WR, G2.unsqueeze(2).to_broadcast([P, KD, 36]), ALU.mult).then_inc(s.wr_ready, 1)
            for t in range(TT):
                dve.wait_ge(s.h_sq, t + 1)
                V.tensor_scalar(SS[:, t:t + 1], SS[:, t:t + 1], 1.0 / D, EPS, ALU.mult, ALU.add).then_inc(s.h_var, 1)
                dve.wait_ge(s.hst_ps, 2 * t + 2)
                V.tensor_copy(M[:, (2 * t + 1) * 512:(2 * t + 2) * 512], HT[2 * t + 1][:, :]).then_inc(s.hst_sb_dve, 1)
                dve.wait_ge(s.h_root, t + 1)
                V.reciprocal(RS[:, t:t + 1], RS[:, t:t + 1]).then_inc(s.h_rstd, 1)

            def residual_lo(t):
                dve.wait_ge(s.hs_hi, t + 1)
                V.scalar_tensor_tensor(XL[:, t * D:(t + 1) * D], H[:, t, :], RS[:, t:t + 1], f32(XH[:, t * D:(t + 1) * D]),
                                       ALU.mult, ALU.subtract).then_inc(s.hs_split, 1)

            residual_lo(0)
            rc = [0]

            def rlink(ins):
                rc[0] += 1
                ins.then_inc(s.router_chain, 1)
                dve.wait_ge(s.router_chain, rc[0])

            rb = carver(RB, 320)
            GD = rb(8).rearrange("p (t g) -> p t g", t=TT)
            GE = rb(8).rearrange("p (t g) -> p t g", t=TT)
            DM = rb(2)
            EX2 = rb(2)
            one = lambda: rb(2)
            grp = lambda: rb(8).rearrange("p (t g) -> p t g", t=TT)
            exl = lambda: rb(16).rearrange("p (t e) -> p t e", t=TT)
            all_ = lambda: rb(64).rearrange("p (t g e) -> p t g e", t=TT, g=NG)
            GMAX, PG, GI, I1, I2, M1, M2, W1, W2 = (one() for _ in range(9))
            GC, OG = grp(), grp()
            EIN, EIN2, E1, E2, OE1, OE2, O8, W8 = (exl() for _ in range(8))
            EALL = all_()
            assert rb.used() == RB_O32
            O32 = all_()

            def spread(v, n):
                return v.unsqueeze(2).to_broadcast([P, TT, n])

            def below(n):
                return tab("down")[:, 0:n]

            def first_of_max(index, values, top, work, n):
                for t in range(TT):
                    V.scalar_tensor_tensor(work[:, t], values[:, t], top[:, t:t + 1], below(n), ALU.is_ge, ALU.mult)\
                        .then_inc(s.router_chain, 1)
                rc[0] += TT
                dve.wait_ge(s.router_chain, rc[0])
                rlink(V.tensor_reduce(index, work, AXX, ALU.min))

            def one_hot(dst, index, n):
                return V.tensor_tensor(dst, below(n).unsqueeze(1).to_broadcast([P, TT, n]), spread(index, n), ALU.is_equal)

            def outer(dst, a8):
                return V.tensor_tensor(dst, OG.unsqueeze(3).to_broadcast([P, TT, NG, EG]),
                                       a8.unsqueeze(2).to_broadcast([P, TT, NG, EG]), ALU.mult)

            dve.wait_ge(s.logits_ps, 1)
            dve.wait_ge(s.h_rstd, TT)
            for t in range(TT):
                V.scalar_tensor_tensor(LG[:, t, :], S0[:, t * 36:(t + 1) * 36], RS[:, t:t + 1], BR, ALU.mult, ALU.add)\
                    .then_inc(s.router_chain, 1)
            rc[0] += TT
            dve.wait_ge(s.router_chain, rc[0])
            rlink(V.reduce_max(GMAX, LG[:, :, 0:NG], AXX))
            V.tensor_tensor(GD, LG[:, :, 0:NG], spread(GMAX, NG), ALU.subtract).then_inc(s.router_exp, 1)
            first_of_max(GI, LG[:, :, 0:NG], GMAX, GC, NG)
            rlink(one_hot(OG, GI, NG))
            rlink(V.tensor_tensor(EALL, LG[:, :, NG:36].rearrange("p t (g e) -> p t g e", g=NG),
                                  OG.unsqueeze(3).to_broadcast([P, TT, NG, EG]), ALU.mult))
            rlink(V.reduce_sum(EIN, EALL.rearrange("p t g e -> p t e g"), AXX))
            rlink(V.reduce_max(M1, EIN, AXX))
            first_of_max(I1, EIN, M1, E1, EG)
            rlink(one_hot(OE1, I1, EG))
            rlink(V.scalar_tensor_tensor(EIN2, OE1, -3e38, EIN, ALU.mult, ALU.add))
            rlink(V.reduce_max(M2, EIN2, AXX))
            dve.wait_ge(s.router_exp, 2)
            V.tensor_tensor(DM, M2, M1, ALU.subtract).then_inc(s.router_exp, 1)
            first_of_max(I2, EIN2, M2, E2, EG)
            for t in range(TT):
                V.scalar_tensor_tensor(O8[:, t], below(EG), I2[:, t:t + 1], OE1[:, t], ALU.is_equal, ALU.add)\
                    .then_inc(s.router_chain, 1)
            rc[0] += TT
            dve.wait_ge(s.router_chain, rc[0])
            outer(O32, O8).then_inc(s.sel_ready, 1)
            residual_lo(1)
            dve.wait_ge(s.sel_ready, 1)
            dve.wait_ge(s.rank_ps, 1)
            o32 = O32.rearrange("p t g e -> p t (g e)")
            rlink(V.tensor_tensor(RANK[:, :, 0:NE], PB[:, 0:2 * NE].rearrange("p (t e) -> p t e", t=TT), o32, ALU.mult))

            def router_weights():
                rlink(V.tensor_tensor(OE2, O8, OE1, ALU.subtract))
                rlink(V.reduce_sum(PG, GE, AXX))
                rlink(V.reciprocal(PG, PG))
                dve.wait_ge(s.router_exp, 4)
                rlink(V.tensor_scalar(W1, EX2, 1.0, None, ALU.add))
                rlink(V.reciprocal(W1, W1))
                rlink(V.tensor_tensor(W1, W1, PG, ALU.mult))
                rlink(V.tensor_tensor(W2, W1, EX2, ALU.mult))
                rlink(V.tensor_tensor(OE1, OE1, spread(W1, EG), ALU.mult))
                rlink(V.tensor_tensor(OE2, OE2, spread(W2, EG), ALU.mult))
                rlink(V.tensor_tensor(W8, OE1, OE2, ALU.add))
                rlink(outer(WT.rearrange("p t (g e) -> p t g e", g=NG), W8))

            oc = [0]

            def olink(ins):
                oc[0] += 1
                ins.then_inc(s.over_chain, 1)
                dve.wait_ge(s.over_chain, oc[0])

            NC = ROUNDS * NQ
            ov = carver(OV, 460)
            CMAX, FLAG, POS = ov(NQ), ov(NC), ov(NC)
            EQ = ov(8 * NC).rearrange("p (j c) -> p j c", j=8)
            EQC = ov(8 * NC).rearrange("p (j c) -> p j c", j=8)
            LF = ov(17)

            def totals():
                dve.wait_ge(s.total_ps, 1)
                olink(V.reduce_max(CMAX, S0[:, 0:NE].rearrange("p (q e) -> p q e", q=NQ), AXX))

            def overflow_list():
                for r in range(1, ROUNDS + 1):
                    olink(V.tensor_scalar(RANK[:, :, r * NE:(r + 1) * NE], RANK[:, :, 0:NE], -1.0 * CAP * r, None, ALU.add))
                for r in range(ROUNDS):
                    olink(V.tensor_scalar(FLAG[:, r * NQ:(r + 1) * NQ], CMAX, float(CAP * (r + 1)), None, ALU.is_gt))
                olink(V.tensor_tensor_scan(POS, ones_mat[:, 0:NC], FLAG, 0.0, ALU.mult, ALU.add))
                olink(V.reduce_max(LF[:, 0:1], POS, AXX))
                olink(V.tensor_tensor(POS, POS, FLAG, ALU.mult))
                jota = tab("iota")[:, 1:9].unsqueeze(2).to_broadcast([P, 8, NC])
                olink(V.tensor_tensor(EQ, POS.unsqueeze(1).to_broadcast([P, 8, NC]), jota, ALU.is_equal))
                for i in range(2):
                    code = tab("code")[:, i * NC:(i + 1) * NC].unsqueeze(1).to_broadcast([P, 8, NC])
                    olink(V.tensor_tensor(EQC, EQ, code, ALU.mult))
                    olink(V.reduce_sum(LF[:, 1 + 8 * i:9 + 8 * i], EQC, AXX))
                V.tensor_copy(LIST[0:1, 0:17], LF[0:1, :]).then_inc(s.over_ready, 1)
                dve.drain().then_inc(s.o_free, 2)

            def select(n, col):
                after(dve, s.wselt_ps, n * 2)
                after(dve, s.gather_ps, n * 4)
                slot = tab("iota")[:, 1:CAP + 1].unsqueeze(1).to_broadcast([P, QUAD, CAP])
                for t in range(TT):
                    V.tensor_tensor(SEL[:, t, :, :], RANK[:, t, bass.ds(col, QUAD)].unsqueeze(2).to_broadcast([P, QUAD, CAP]),
                                    slot, ALU.is_equal).then_inc(s.sel_chain, 1)
                after(dve, s.sel_chain, n * 2 + 2)

            def weigh(n, expert):
                for t in range(TT):
                    V.tensor_tensor(WSEL[:, t, :, :], f32(SEL[:, t, :, :]),
                                    WT[:, t, bass.ds(expert, QUAD)].unsqueeze(2).to_broadcast([P, QUAD, CAP]), ALU.mult)\
                        .then_inc(s.wsel_ready, 1)

            def take_gathered(n, b, src=bank[6]):
                after(dve, s.gather_ps, n * 4 + b + 1)
                for k in (2 * b, 2 * b + 1):
                    V.tensor_scalar(M[:, k * T:(k + 1) * T], src[:, (k % 2) * T:(k % 2 + 1) * T], G2[:, k:k + 1], None,
                                    ALU.mult).then_inc(s.xe_ready, 1)

            def y_low(n, pair, half):
                after(dve, s.y_hi, n * 4 + 2 * pair + half + 1)
                V.scalar_tensor_tensor(y_part(WL, pair, half), bank[2 + half][:, :],
                                       WS[:, pair:pair + 1], f32(y_part(WH, pair, half)),
                                       ALU.mult, ALU.subtract).then_inc(s.y_split, 1)

            def hidden(n, pair):
                hb = bank[pair]
                after(dve, s.hid_t, n * 2 + pair + 1)
                V.scalar_tensor_tensor(TH[:, pair, :], TH[:, pair, :], 1.0, hb[:, 0:FF], ALU.add, ALU.mult)\
                    .then_inc(s.step_chain, 1)
                after(dve, s.step_chain, n * 2 + pair + 1)
                V.scalar_tensor_tensor(HT_[:, pair, :], TH[:, pair, :], 0.5, hb[:, FF:2 * FF], ALU.mult, ALU.mult)\
                    .then_inc(s.hid_ready, 1)

            def hidden_t(n, pair):
                after(dve, s.hidt_ps, n * 2 + pair + 1)
                V.tensor_copy(HTT[:, pair, :, :], bank[7][:, T:2 * T].rearrange("p (j c) -> p j c", j=2)).then_inc(s.hidt_sb, 1)

            def slot_weights(n, pair):
                after(dve, s.wselt_ps, n * 2 + pair + 1)
                V.reduce_max(WS[:, pair:pair + 1], bank[7][:, 0:T], AXX).then_inc(s.slot_weight, 1)
                after(dve, s.slot_weight, n * 2 + pair + 1)
                V.tensor_scalar(SELT[:, pair, :], bank[7][:, 0:T], 0.0, None, ALU.is_gt).then_inc(s.selt_sb, 1)

            def add_outputs(n):
                for t in range(TT):
                    for half in range(2):
                        c = slice(half * 512, half * 512 + 512)
                        after(dve, s.o_ps, n * 4 + 2 * t + half + 1)
                        V.tensor_tensor(H[:, t, c], H[:, t, c], bank[4 + half][:, :], ALU.add).then_inc(s.o_free, 1)

            def step(n, select_next=None, add_previous=True):
                if add_previous:
                    add_outputs(n - 1)
                slot_weights(n, 0)
                hidden(n, 0)
                slot_weights(n, 1)
                if select_next is not None:
                    select_next()
                hidden_t(n, 0)
                hidden(n, 1)
                if select_next is not None:
                    take_gathered(n + 1, 0)
                hidden_t(n, 1)
                if select_next is not None:
                    take_gathered(n + 1, 1)
                y_low(n, 0, 0)
                if select_next is not None:
                    take_gathered(n + 1, 2)
                y_low(n, 0, 1)
                if select_next is not None:
                    take_gathered(n + 1, 3)
                y_low(n, 1, 0)
                y_low(n, 1, 1)

            def select_quad(n, col, expert):
                select(n, col)
                weigh(n, expert)

            select(0, 0)
            totals()
            router_weights()
            weigh(0, 0)
            for b in range(4):
                take_gathered(0, b, bank[4 + b])
            overflow_list()
            step(0, lambda: select_quad(1, QUAD, QUAD), add_previous=False)
            with dve.Fori(1, NQ - 1) as i:
                step(i, lambda: select_quad(i + 1, i * QUAD + QUAD, i * QUAD + QUAD))
            step(NQ - 1)
            add_outputs(NQ - 1)
            count = dve.value_load(LIST[0:1, 0:1], min_val=0, max_val=MAXOVER)
            with dve.If(count > 0):
                with dve.Fori(0, count) as j:
                    col = dve.value_load(LIST[0:1, bass.ds(j + 1, 1)], min_val=0, max_val=(ROUNDS + 1) * NE - QUAD)
                    q = dve.value_load(LIST[0:1, bass.ds(j + 9, 1)], min_val=0, max_val=NQ - 1)
                    select_quad(j + NQ, col, q * QUAD)
                    for b in range(4):
                        take_gathered(j + NQ, b)
                    step(j + NQ, add_previous=False)
                    add_outputs(j + NQ)
            dve.end_ifs()
            dve.wait_ge(s.o_free, count * 4 + (4 * NQ + 2))
            for t in range(TT):
                dve.wait_ge(s.final_sq, t + 1)
                V.tensor_scalar(SS[:, t:t + 1], SS[:, t:t + 1], 1.0 / D, EPS, ALU.mult, ALU.add).then_inc(s.final_var, 1)
            dve.wait_ge(s.final_in, 16)
            for t in range(TT):
                dve.wait_ge(s.final_root, t + 1)
                link(V.reciprocal(RS[:, t:t + 1], RS[:, t:t + 1]))
                V.scalar_tensor_tensor(YOUT[:, t, :], H[:, t, :], RS[:, t:t + 1], FG, ALU.mult, ALU.mult)\
                    .then_inc(s.out_ready, 1)

        @block.tensor
        def _(pe):
            mm = nc.tensor.matmul

            def transpose(dst, src):
                k = src.shape[0]
                return nc.tensor.transpose(dst, src, ident[0:k, 0:k])

            pe.wait_ge(s.ident_in, 16)
            xs = M[:, :].rearrange("p (t q k) -> p t q k", t=TT, k=KD)
            for t in range(TT):
                pe.wait_ge(s.xscaled, t + 1)
                for k in range(KD):
                    ins = transpose(bank[4 + k // 2][:, (k % 2) * T + t * P:(k % 2) * T + (t + 1) * P], xs[:, t, :, k])
                    if t == TT - 1 and k % 2:
                        ins.then_inc(s.xt_ps, 1)

            def three(dst, wh, wl, xh, xl, first, last):
                mm(dst, wh, xh, start=first, stop=False)
                mm(dst, wl, xh, start=False, stop=False)
                return mm(dst, wh, xl, start=False, stop=last)

            def act_tile(k, c=slice(0, T)):
                a = slice(k * T + c.start, k * T + c.stop)
                return XH[:, a], XL[:, a]

            def project(q, dst, wait_x=False):
                pe.wait_ge(s.w_lo, q + 1)
                for k in range(KD):
                    if wait_x:
                        pe.wait_ge(s.x_split, k + 1)
                    c = slice(k * 128, (k + 1) * 128)
                    ins = three(dst, part(WH, q, c), part(WL, q, c), *act_tile(k), k == 0, k == KD - 1)
                ins.then_inc(s.part_done, 1)
                return ins

            def project_tokens(n, dsts, ncol):
                for h in range(2):
                    q = 2 * n + h
                    pe.wait_ge(s.w_lo, q + 1)
                    for t in range(TT):
                        for k in range(4 * h, 4 * h + 4):
                            xh, xl = act_tile(k, slice(t * P, (t + 1) * P))
                            c = slice((k % 4) * ncol, (k % 4 + 1) * ncol)
                            wh, wl = part(WH, q, c), part(WL, q, c)
                            mm(dsts[t], xh, wh, start=(k == 0), stop=False)
                            mm(dsts[t], xl, wh, start=False, stop=False)
                            ins = mm(dsts[t], xh, wl, start=False, stop=(k == KD - 1))
                    ins.then_inc(s.part_done, 1)

            def channel_sum(dst, tiles, done):
                for j, tile in enumerate(tiles):
                    ins = mm(dst, ones_mat, tile, start=(j == 0), stop=(j == len(tiles) - 1))
                ins.then_inc(done, 1)

            def halves(ap):
                return [ap[:, 0:T], ap[:, T:2 * T]]

            def scores(p):
                b, hp = PAIRS[p]
                if p:
                    pe.wait_ge(s.logit_ready, 4 * p)
                else:
                    pe.wait_ge(s.kpe_ready, 1)
                    pe.wait_ge(s.mla_evac, 4)
                if b != 3:
                    pe.wait_ge(s.proj_evac, 2 if b == 1 else 4)
                if b == 1:
                    pe.wait_ge(s.cum_ready, 2)
                for qt in range(2):
                    n = P if qt == 0 else T
                    dst = (S0, S1)[qt][:, 0:2 * n]
                    q = slice(qt * P, (qt + 1) * P)
                    ins = mm(dst, Q[b][:, hp, q], KB[b][:, 2 * hp:2 * hp + 2, 0:n], start=True, stop=(b == 0))
                    if b == 3:
                        ins = mm(dst, QPE[:, q], KPE[:, 2 * hp:2 * hp + 2, 0:n], start=False, stop=True)
                    if b == 1:
                        ins = mm(dst, ones_mat[0:HEADS, :], CB[:, 2 * hp:2 * hp + 2, 0:n], start=False, stop=True)
                ins.then_inc(s.score_ps, 1)

            def transpose_probs(p):
                for h in range(2):
                    pe.wait_ge(s.prob_ready, 2 * p + h + 1)
                    if p:
                        pe.wait_ge(s.pt_sb, 2 * p - 1 + h)
                    if h and FIRST_SCORES + 2 * (p + 1) >= NIN:
                        pe.wait_ge(s.proj_evac, 5)
                    for i in range(3):
                        ins = transpose((PT, MISC)[h][:, i * P:(i + 1) * P], PR[:, h, i * P:(i + 1) * P])
                    ins.then_inc(s.pt_ps, 1)

            def attend(p):
                b, hp = PAIRS[p]
                v = VMAP[b]
                for h in range(2):
                    if h == 0 and p:
                        pe.wait_ge(s.attn_ready, p)
                    if b == 0:
                        pe.wait_ge(s.proj_evac, 5)
                    pe.wait_ge(s.pt_sb, 2 * p + h + 1)
                    pts = (PTS, PTS2)[h]
                    r = slice(64 * h, 64 * h + 64)
                    vc = slice((2 * hp + h) * HD, (2 * hp + h + 1) * HD)
                    mm(PV[r, 0:P], v[:, 0, vc], pts[:, 0:P], start=True, stop=True)
                    mm(PV[r, P:T], v[:, 0, vc], pts[:, P:T], start=True, stop=False)
                    mm(PV[r, P:T], v[:, 1, vc], pts[:, T:384], start=False, stop=True).then_inc(s.pv_ps, 1)

            tri0 = tri[:, 0:P]
            for n in range(NIN + NGATE):
                pg = (PA, PB)[n % 2]
                if n == 1:
                    pe.wait_ge(s.params_in, 16 * 7)
                    transpose(MISC[:, 0:NROWS], ROWP[0:NROWS, :]).then_inc(s.params_ps, 1)
                if n == 3:
                    pe.wait_ge(s.tables_in, 32)
                    pe.wait_ge(s.params_sb, 1)
                    pe.wait_ge(s.cq_sq, 1)
                    channel_sum(MISC[:, 0:T], halves(TMPA), s.cq_sum)
                    pe.wait_ge(s.ckv_sq, 1)
                    channel_sum(MISC[:, T:2 * T], [TMPB[:, 0:T]], s.ckv_sum)
                if n == 4:
                    pe.wait_ge(s.cq_ready, 2)
                    pe.wait_ge(s.wmla_in, 96)
                    pe.wait_ge(s.wrot_ready, 4)
                    for m in range(2):
                        for j in range(2):
                            ins = mm(S1[:, m * T:(m + 1) * T], WUQ[:, j, m * P:(m + 1) * P], CQ[:, j, :],
                                     start=(j == 0), stop=(j == 1))
                    ins.then_inc(s.mla_ps, 1)
                    for j in range(2):
                        mm(PT[:, 0:T], WUQ[:, j, 256:384], CQ[:, j, :], start=(j == 0), stop=(j == 1))
                    for j in range(2):
                        ins = mm(PT[:, T:2 * T], WROT[:, j, :, :].rearrange("p h c -> p (h c)"), CQ[:, j, :],
                                 start=(j == 0), stop=(j == 1))
                    ins.then_inc(s.mla_ps, 1)
                    pe.wait_ge(s.ckv_ready, 1)
                    for m in range(2):
                        ins = mm(PV[:, m * T:(m + 1) * T], WUKV[:, m * P:(m + 1) * P], CKV, start=True, stop=True)
                    ins.then_inc(s.mla_ps, 1)
                    for t in range(TT):
                        ins = mm(BRB[:, t * T:(t + 1) * T], CKV[:, t * P:(t + 1) * P], WUKV[:, 256:512], start=True, stop=True)
                    ins.then_inc(s.mla_ps, 1)
                if n == 5:
                    pe.wait_ge(s.krope_sb, 1)
                    pe.wait_ge(s.mla_evac, 1)
                    mm(S1[:, 0:T], tab("rep", slice(64, 128)), TMPB[64:128, T:2 * T], start=True, stop=True)\
                        .then_inc(s.kpe_ps, 1)
                    pe.wait_ge(s.fox_ready, 1)
                    pe.wait_ge(s.ckv_ve, 1)
                    mm(MISC[:, 0:4], tri0, FLOG[:, 0, :], start=True, stop=True)
                    mm(MISC[:, 4:8], ones_mat, FLOG[:, 0, :], start=True, stop=False)
                    mm(MISC[:, 4:8], tri0, FLOG[:, 1, :], start=False, stop=True)
                    mm(MISC[0:HEADS, T:T + P], FLOG[:, 0, :], tri0, start=True, stop=True)
                    mm(MISC[0:HEADS, T + P:2 * T], FLOG[:, 0, :], ones_mat, start=True, stop=False)
                    mm(MISC[0:HEADS, T + P:2 * T], FLOG[:, 1, :], tri0, start=False, stop=True).then_inc(s.fox_ps, 1)
                p = (n - FIRST_SCORES) // 2
                if (n - FIRST_SCORES) % 2 == 0 and 0 <= p <= len(PAIRS):
                    if p:
                        transpose_probs(p - 1)
                    if p < len(PAIRS):
                        scores(p)
                    if p:
                        attend(p - 1)
                if n == LN_AT + 1:
                    pe.wait_ge(s.conv_out, 2)
                    channel_sum(MISC[:, 0:T], [CACC[:, j, :] for j in range(2)], s.ln_sum)
                if n == LN_AT + 2:
                    pe.wait_ge(s.ln_sq, 1)
                    channel_sum(MISC[:, 0:T], halves(LNT), s.ln_var)
                if n == 2:
                    pe.wait_ge(s.cq_sq, 1)
                    project_tokens(n, [PA[:, 0:260], S0[:, 0:260]], 260)
                elif n == 9:
                    pe.wait_ge(s.proj_evac, 3)
                    pe.wait_ge(s.pt_sb, 2)
                    project_tokens(n, [PB[:, 0:T], MISC[:, 0:T]], 256)
                else:
                    if n == 0:
                        pass
                    elif n == 3:
                        pe.wait_ge(s.ckv_sq, 1)
                        pe.wait_ge(s.krope_sb, 1)
                    elif n == 4:
                        pe.wait_ge(s.fox_f, 1)
                    elif n == 5:
                        pe.wait_ge(s.proj_evac, 1)
                    elif n == 6:
                        pe.wait_ge(s.proj_evac, 2)
                    elif n == 7:
                        pe.wait_ge(s.conv_a_sb, 1)
                    elif n == 8:
                        pe.wait_ge(s.conv_t, 1)
                    elif n == NIN:
                        pe.wait_ge(s.proj_evac, 4)
                    elif n == NIN + 1:
                        pe.wait_ge(s.proj_evac, 5)
                    elif n > NIN + 1:
                        pe.wait_ge(s.gate_t, 2 * (n - NIN - 1))
                    for m in range(2):
                        ins = project(2 * n + m, pg[:, m * T:(m + 1) * T], n == 0 and m == 0)
                if n < NIN:
                    continue
                g = n - NIN
                b = BRANCHES[g // 4]
                if g % 4 == 0:
                    if b == 2:
                        pe.wait_ge(s.yc_ready, 1)
                    else:
                        pe.wait_ge(s.attn_ready, {3: 2, 1: 4, 0: 6}[b])
                if g:
                    pe.wait_ge(s.tmp_mul, g)
                wb = RAW[n % NRAW][:, 2048:2560].rearrange("p (j n) -> p j n", j=2)
                for m in range(2):
                    for j in range(2):
                        ins = mm(BRB[:, m * T:(m + 1) * T], wb[:, j, m * 128:(m + 1) * 128], YT[b][:, j, :],
                                 start=(j == 0), stop=(j == 1))
                ins.then_inc(s.branch_ps, 1)
            pe.wait_ge(s.logit_ready, 4 * len(PAIRS))
            pe.wait_ge(s.attn_ready, len(PAIRS))
            for m in range(KD):
                q = 2 * (NIN + NGATE) + m
                pe.wait_ge(s.w_lo, q + 1)
                pe.wait_ge(s.merge_split, m + 1)
                for t in range(TT):
                    a = slice(m * T + t * P, m * T + (t + 1) * P)
                    xh, xl = MH[:, a], ML[:, a]
                    for half in range(2):
                        c = slice(half * 512, half * 512 + 512)
                        dst = OUT[2 * t + half][:, :]
                        mm(dst, xh, part(WH, q, c), start=(m == 0), stop=False)
                        mm(dst, xl, part(WH, q, c), start=False, stop=False)
                        ins = mm(dst, xh, part(WL, q, c), start=False, stop=(m == KD - 1))
                    if m == KD - 1:
                        ins.then_inc(s.tile_done, 1)
                    elif t == TT - 1:
                        ins.then_inc(s.part_done, 1)
            for t in range(TT):
                pe.wait_ge(s.h_ready, 2 * t + 2)
                h_t = H[:, t, :].rearrange("p (q k) -> p q k", k=KD)
                for k in range(KD):
                    ins = transpose(HT[2 * t + k // 4][:, (k % 4) * P:(k % 4 + 1) * P], h_t[:, :, k])
                    if k % 4 == 3:
                        ins.then_inc(s.hst_ps, 1)
            pe.wait_ge(s.wr_ready, 1)
            for t in range(TT):
                for k in range(KD):
                    if k % 4 == 0:
                        pe.wait_ge((s.hst_sb_act, s.hst_sb_dve)[k // 4], t + 1)
                    ins = mm(S0[:, t * 36:(t + 1) * 36], M[:, (t * KD + k) * P:(t * KD + k + 1) * P], WR[:, k, :],
                             start=(k == 0), stop=(k == KD - 1))
            ins.then_inc(s.logits_ps, 1)
            pe.wait_ge(s.sel_ready, 1)
            o32 = RB[:, RB_O32:RB_O32 + TT * NE].rearrange("p (t e) -> p t e", t=TT)
            mm(PB[:, 0:NE], tri0, o32[:, 0, :], start=True, stop=True)
            mm(PB[:, NE:2 * NE], ones_mat, o32[:, 0, :], start=True, stop=False)
            mm(PB[:, NE:2 * NE], tri0, o32[:, 1, :], start=False, stop=True).then_inc(s.rank_ps, 1)
            mm(S0[:, 0:NE], ones_mat, o32[:, 0, :], start=True, stop=False)
            mm(S0[:, 0:NE], ones_mat, o32[:, 1, :], start=False, stop=True).then_inc(s.total_ps, 1)

            xe = M[:, :].rearrange("p (k c) -> p k c", k=KD)
            xh4 = XH[:, :].rearrange("p (t q k) -> p t q k", t=TT, k=KD)
            xl4 = XL[:, :].rearrange("p (t q k) -> p t q k", t=TT, k=KD)

            def gather_part(n, b, into=bank[6]):
                if b == 0:
                    after(pe, s.sel_chain, n * 2 + 2)
                if into is bank[6]:
                    after(pe, s.xe_ready, n * 8 + 2 * b)
                for k in (2 * b, 2 * b + 1):
                    dst = into[:, (k % 2) * T:(k % 2 + 1) * T]
                    for t in range(TT):
                        sel = SEL[:, t, :, :]
                        mm(dst, xh4[:, t, :, k], sel, start=(t == 0), stop=False)
                        ins = mm(dst, xl4[:, t, :, k], sel, start=False, stop=(t == TT - 1))
                ins.then_inc(s.gather_ps, 1)

            def select_t(n, pair):
                if pair == 0:
                    after(pe, s.wsel_ready, n * 2 + 2)
                    after(pe, s.hidt_sb, n * 2)
                else:
                    after(pe, s.selt_sb, n * 2 + 1)
                for t in range(TT):
                    ins = transpose(bank[7][:, t * P:(t + 1) * P],
                                    WSEL[:, t, 2 * pair:2 * pair + 2, :].rearrange("p e c -> p (e c)"))
                ins.then_inc(s.wselt_ps, 1)

            def wait_slots(n, parity, pair, kind):
                for e in range(2):
                    slot = slot_plan.index((pair, kind, e))
                    if slot >= DOUBLE:
                        pe.wait_ge(exp_in[slot], n * 16 + 16)
                    elif parity is None:
                        pe.wait_ge(exp_in[slot], (n - NQ) * 16 + NQ // 2 * 16 + 16)
                    else:
                        pe.wait_ge(slot_signal(parity, slot), (n - parity) * 8 + 16)

            def hidden(n, parity, pair, kind):
                if kind == 0:
                    after(pe, s.hid_ready, n * 2 - 1 + pair)
                wait_slots(n, parity, pair, kind)
                for k in range(KD):
                    if kind == 0 and pair == 0 and k % 2 == 0:
                        pe.wait_ge(s.xe_ready, n * 8 + k + 2)
                    for e in range(2):
                        w = expert_slot(parity, slot_plan.index((pair, kind, e)))[:, k * FF:(k + 1) * FF]
                        x = xe[:, k, (2 * pair + e) * CAP:(2 * pair + e + 1) * CAP]
                        ins = mm(bank[pair][64 * e:64 * e + 64, kind * FF:(kind + 1) * FF], x, w,
                                 start=(k == 0), stop=(k == KD - 1), skip_group_check=True)
                ins.then_inc((s.gates_ps, s.hid_ps)[kind], 1)

            def hidden_t(n, pair):
                after(pe, s.hid_ready, n * 2 + pair + 1)
                if pair == 0:
                    after(pe, s.selt_sb, n * 2 + 2)
                else:
                    after(pe, s.hidt_sb, n * 2 + 1)
                h2 = HT_[:, pair, :].rearrange("p (f j) -> p f j", j=2)
                for j in range(2):
                    ins = transpose(bank[7][:, T + j * P:T + (j + 1) * P], h2[:, :, j])
                ins.then_inc(s.hidt_ps, 1)

            def down(n, parity, pair, half):
                if half == 0:
                    after(pe, s.hidt_sb, n * 2 + pair + 1)
                    wait_slots(n, parity, pair, 2)
                after(pe, s.y_split, n * 4 + (half + 1 if pair else half - 1))
                for j in range(2):
                    for e in range(2):
                        w = expert_slot(parity, slot_plan.index((pair, 2, e)))[:, j * D + half * 512:j * D + half * 512 + 512]
                        ins = mm(bank[2 + half][64 * e:64 * e + 64, :], HTT[:, pair, j, 64 * e:64 * e + 64], w,
                                 start=(j == 0), stop=(j == 1), skip_group_check=True)
                ins.then_inc(s.y_ps, 1)

            def scatter(n):
                for t in range(TT):
                    for half in range(2):
                        i = 2 * t + half
                        after(pe, s.o_free, n * 4 + i + 1)
                        for pair in range(2):
                            after(pe, s.y_split, n * 4 + 2 * pair + half + 1)
                            lhs = SELT[:, pair, t * P:(t + 1) * P]
                            mm(bank[4 + half][:, :], lhs, y_part(WH, pair, half), start=(pair == 0), stop=False)
                            ins = mm(bank[4 + half][:, :], lhs, y_part(WL, pair, half), start=False, stop=(pair == 1))
                        ins.then_inc(s.o_ps, 1)

            def step(n, parity, scatter_previous=True, gather_next=True):
                hidden(n, parity, 0, 0)
                if scatter_previous:
                    scatter(n - 1)
                select_t(n, 0)
                hidden(n, parity, 0, 1)
                select_t(n, 1)
                hidden(n, parity, 1, 0)
                hidden_t(n, 0)
                hidden(n, parity, 1, 1)
                if gather_next:
                    gather_part(n + 1, 0)
                down(n, parity, 0, 0)
                hidden_t(n, 1)
                if gather_next:
                    gather_part(n + 1, 1)
                down(n, parity, 0, 1)
                if gather_next:
                    gather_part(n + 1, 2)
                down(n, parity, 1, 0)
                if gather_next:
                    gather_part(n + 1, 3)
                down(n, parity, 1, 1)

            pe.wait_ge(s.hs_split, TT)
            for b in range(4):
                gather_part(0, b, bank[4 + b])
            pe.wait_ge(s.over_chain, 1)
            step(0, 0, scatter_previous=False)
            with pe.Fori(0, (NQ - 2) // 2) as i:
                step(i * 2 + 1, 1)
                step(i * 2 + 2, 0)
            step(NQ - 1, 1, gather_next=False)
            scatter(NQ - 1)
            count = pe.value_load(LIST[0:1, 0:1], min_val=0, max_val=MAXOVER)
            with pe.If(count > 0):
                with pe.Fori(0, count) as j:
                    for b in range(4):
                        gather_part(j + NQ, b)
                    step(j + NQ, None, scatter_previous=False, gather_next=False)
                    scatter(j + NQ)
            pe.end_ifs()


_INS = ["x", "norm1_g", "w_in", "b_forget", "conv_w", "conv_b", "conv_ln_g", "conv_ln_b", "mla_gq", "mla_wuq", "mla_gkv",
        "mla_wukv", "w_gate", "b_gate", "w_branch", "w_out", "norm2_g", "w_router_group", "b_router_group",
        "w_router_expert", "b_router_expert", "w_exp_gate", "w_exp_up", "w_exp_down", "final_g"]


def kernel(**inputs):
    import concourse.bacc as bacc
    from concourse.bass_utils import run_bass_kernel_spmd

    nc = bacc.Bacc("TRN2", target_bir_lowering=False, num_devices=1)
    arrays, aps = {}, {}
    for name in _INS:
        a = np.ascontiguousarray(inputs[name])
        arrays[f"in_{name}"] = a
        aps[name] = nc.dram_tensor(f"in_{name}", a.shape, mybir.dt.from_np(a.dtype), kind="ExternalInput").ap()
    arrays["in_tables"] = shape_tables()
    aps["tables"] = nc.dram_tensor("in_tables", (P, NTAB), F32, kind="ExternalInput").ap()
    out = nc.dram_tensor("out_y", (1, T, D), F32, kind="ExternalOutput").ap()
    trunk_kernel(nc, aps, out)
    r = run_bass_kernel_spmd(nc, [arrays], core_ids=[0])
    return r.results[0]["out_y"]
```
